# Optimizing a Trainium2 kernel written in Bass

```python
import math
import jax, jax.numpy as jnp
from jax import lax
import numpy as np

D_MODEL = 1024
BATCH = 1
SEQ = 512
DEPTH = 1

SSM_WIDTH = D_MODEL // 2
SSM_GROUP = 16
SSM_GROUPS = SSM_WIDTH // SSM_GROUP
SSM_STATE = 64
NSA_HEADS = 8
NSA_KV_GROUPS = 2
NSA_HEAD_DIM = (D_MODEL // 2) // NSA_HEADS
NSA_WIDTH = NSA_HEADS * NSA_HEAD_DIM
KV_WIDTH = NSA_KV_GROUPS * NSA_HEAD_DIM
CMP_BLOCK = 32
CMP_STRIDE = 16
CMP_HIDDEN = 2 * NSA_HEAD_DIM
SEL_BLOCK = 64
SEL_TOPK = 16
WINDOW = 512
Q_BLOCK = 128
FORCE_BONUS = 1.0e4
PEER_HEADS = 8
PEER_NKEYS = 128
PEER_EXPERTS = PEER_NKEYS * PEER_NKEYS
PEER_KEY_DIM = 128
PEER_TOPK = 16
PEER_CHUNK = 128
IN_COLS = SSM_WIDTH + NSA_WIDTH + 6 * KV_WIDTH + 3 * NSA_HEADS + 2 * D_MODEL
DN_ALPHA = (2.0 * DEPTH) ** 0.25
DN_BETA = (8.0 * DEPTH) ** -0.25
LN_EPS = 1e-5
NEG = -1e30

kernel_name = "hybrid_s5_nsa_peer_deepnorm"

def layer_norm(x, g, b):
    xf = x.astype(jnp.float32)
    mu = xf.mean(-1, keepdims=True)
    var = jnp.square(xf - mu).mean(-1, keepdims=True)
    return ((xf - mu) * lax.rsqrt(var + LN_EPS) * g.astype(jnp.float32) + b.astype(jnp.float32)).astype(x.dtype)

def masked_softmax(s, mask):
    s = jnp.where(mask, s.astype(jnp.float32), NEG)
    m = jnp.max(s, axis=-1, keepdims=True)
    p = jnp.exp(s - m) * mask
    return p / jnp.maximum(p.sum(-1, keepdims=True), 1e-30)

def alibi_slopes():
    return jnp.exp2(-8.0 * jnp.arange(1, NSA_HEADS + 1, dtype=jnp.float32) / NSA_HEADS)

def s5_mixer(u, a_re, a_im, log_dt, b_re, b_im, c_re, c_im, d_skip, w_glu):
    Bsz, S, _ = u.shape
    f32 = jnp.float32
    uf = u.astype(f32).reshape(Bsz, S, SSM_GROUPS, SSM_GROUP)
    lam = lax.complex(a_re.astype(f32), a_im.astype(f32))
    dt = jnp.exp(log_dt.astype(f32))[:, None]
    lam_bar = jnp.exp(lam * dt)
    b = lax.complex(b_re.astype(f32), b_im.astype(f32))
    b_bar = ((lam_bar - 1.0) / lam)[:, :, None] * b
    bu = lax.complex(jnp.einsum('bsgh,gph->sbgp', uf, jnp.real(b_bar)),
                     jnp.einsum('bsgh,gph->sbgp', uf, jnp.imag(b_bar)))
    a = jnp.broadcast_to(lam_bar[None, None], (S, 1) + lam_bar.shape)

    def combine(left, right):
        a_l, b_l = left
        a_r, b_r = right
        return a_r * a_l, a_r * b_l + b_r

    _, xs = lax.associative_scan(combine, (a, bu), axis=0)
    y = (jnp.einsum('sbgp,ghp->bsgh', jnp.real(xs), c_re.astype(f32))
         - jnp.einsum('sbgp,ghp->bsgh', jnp.imag(xs), c_im.astype(f32)))
    y = y.reshape(Bsz, S, SSM_WIDTH) + d_skip.astype(f32) * uf.reshape(Bsz, S, SSM_WIDTH)
    y = jax.nn.gelu(y)
    ga, gb = jnp.split(y @ w_glu.astype(f32), 2, axis=-1)
    return (ga * jax.nn.sigmoid(gb)).astype(u.dtype)

def compress(kv, pe, w1, w2):
    S = kv.shape[2]
    n_cmp = (S - CMP_BLOCK) // CMP_STRIDE + 1
    pos = jnp.arange(n_cmp)[:, None] * CMP_STRIDE + jnp.arange(CMP_BLOCK)[None, :]
    blocks = kv[:, :, pos] + pe
    flat = blocks.reshape(blocks.shape[:3] + (CMP_BLOCK * NSA_HEAD_DIM,))
    return jax.nn.gelu(flat @ w1) @ w2

def nsa_mixer(q, k_cmp, v_cmp, k_slc, v_slc, k_win, v_win, gates,
              pe_k, w1_k, w2_k, pe_v, w1_v, w2_v):
    Bsz, S, _ = q.shape
    G, R, dk = NSA_KV_GROUPS, NSA_HEADS // NSA_KV_GROUPS, NSA_HEAD_DIM
    f32 = jnp.float32
    qh = q.reshape(Bsz, S, G, R, dk).transpose(0, 2, 3, 1, 4) * (dk ** -0.5)

    def kvh(t):
        return t.reshape(Bsz, S, G, dk).transpose(0, 2, 1, 3)

    gate = jax.nn.sigmoid(gates.astype(f32)).reshape(Bsz, S, G, R, 3).transpose(0, 2, 3, 1, 4)
    slopes = alibi_slopes().reshape(G, R)[None, :, :, None, None]

    kc = compress(kvh(k_cmp), pe_k, w1_k, w2_k)
    vc = compress(kvh(v_cmp), pe_v, w1_v, w2_v)
    n_cmp = kc.shape[2]
    c_start = jnp.arange(n_cmp) * CMP_STRIDE
    c_end = c_start + CMP_BLOCK - 1
    n_slc = S // SEL_BLOCK
    s_start = jnp.arange(n_slc) * SEL_BLOCK
    overlap = ((c_start[:, None] < s_start[None, :] + SEL_BLOCK)
               & (c_start[:, None] + CMP_BLOCK > s_start[None, :])).astype(f32)
    n_pick = min(SEL_TOPK, n_slc)
    ks_blk = kvh(k_slc).reshape(Bsz, G, n_slc, SEL_BLOCK, dk)
    vs_blk = kvh(v_slc).reshape(Bsz, G, n_slc, SEL_BLOCK, dk)
    pad = ((0, 0), (0, 0), (WINDOW, 0), (0, 0))
    kw_pad = jnp.pad(kvh(k_win), pad)
    vw_pad = jnp.pad(kvh(v_win), pad)
    gather = jax.vmap(jax.vmap(lambda blk, ix: blk[ix]))
    j_idx = jnp.arange(n_slc)

    def query_block(i):
        qs = i * Q_BLOCK
        t = qs + jnp.arange(Q_BLOCK)
        qb = lax.dynamic_slice_in_dim(qh, qs, Q_BLOCK, axis=3)
        gb = lax.dynamic_slice_in_dim(gate, qs, Q_BLOCK, axis=3)
        s_c = jnp.einsum('bgrqd,bgcd->bgrqc', qb, kc)
        dist_c = (t[:, None] - c_end[None, :]).astype(f32)
        p_c = masked_softmax(s_c - slopes * dist_c, dist_c >= 0)
        o_c = jnp.einsum('bgrqc,bgcd->bgrqd', p_c.astype(vc.dtype), vc)
        imp = jnp.einsum('bgrqc,cj->bgqj', p_c, overlap)
        cur = t // SEL_BLOCK
        forced = (j_idx[None, :] == 0) | (j_idx[None, :] == cur[:, None]) | (j_idx[None, :] == cur[:, None] - 1)
        valid = s_start[None, :] <= t[:, None]
        score = jnp.where(valid, imp + forced * FORCE_BONUS, NEG)
        _, idx = lax.top_k(score, n_pick)
        ks = gather(ks_blk, idx).reshape(Bsz, G, Q_BLOCK, n_pick * SEL_BLOCK, dk)
        vs = gather(vs_blk, idx).reshape(Bsz, G, Q_BLOCK, n_pick * SEL_BLOCK, dk)
        kpos = (idx[..., None] * SEL_BLOCK + jnp.arange(SEL_BLOCK)).reshape(Bsz, G, Q_BLOCK, n_pick * SEL_BLOCK)
        dist_s = (t[None, None, :, None] - kpos).astype(f32)[:, :, None]
        s_s = jnp.einsum('bgrqd,bgqkd->bgrqk', qb, ks)
        p_s = masked_softmax(s_s - slopes * dist_s, dist_s >= 0)
        o_s = jnp.einsum('bgrqk,bgqkd->bgrqd', p_s.astype(vs.dtype), vs)
        kw = lax.dynamic_slice_in_dim(kw_pad, qs, Q_BLOCK + WINDOW, axis=2)
        vw = lax.dynamic_slice_in_dim(vw_pad, qs, Q_BLOCK + WINDOW, axis=2)
        wpos = qs - WINDOW + jnp.arange(Q_BLOCK + WINDOW)
        dist_w = t[:, None] - wpos[None, :]
        mask_w = (dist_w >= 0) & (dist_w < WINDOW) & (wpos[None, :] >= 0)
        s_w = jnp.einsum('bgrqd,bgkd->bgrqk', qb, kw)
        p_w = masked_softmax(s_w - slopes * dist_w.astype(f32), mask_w)
        o_w = jnp.einsum('bgrqk,bgkd->bgrqd', p_w.astype(vw.dtype), vw)
        return gb[..., 0:1] * o_c + gb[..., 1:2] * o_s + gb[..., 2:3] * o_w

    o = lax.map(query_block, jnp.arange(S // Q_BLOCK))
    return o.transpose(1, 0, 4, 2, 3, 5).reshape(Bsz, S, NSA_WIDTH).astype(q.dtype)

def peer_ffn(x, w_q, subkeys, u_tab, v_tab):
    Bsz, S, D = x.shape
    xt = x.reshape((Bsz * S) // PEER_CHUNK, PEER_CHUNK, D)
    half = PEER_KEY_DIM // 2

    def chunk(xc):
        q = (xc @ w_q).reshape(PEER_CHUNK, PEER_HEADS, 2, half)
        s = jnp.einsum('thcd,hckd->thck', q, subkeys).astype(jnp.float32)
        sv, si = lax.top_k(s, PEER_TOPK)
        cand = sv[..., 0, :, None] + sv[..., 1, None, :]
        cidx = si[..., 0, :, None] * PEER_NKEYS + si[..., 1, None, :]
        best, pos = lax.top_k(cand.reshape(PEER_CHUNK, PEER_HEADS, -1), PEER_TOPK)
        experts = jnp.take_along_axis(cidx.reshape(PEER_CHUNK, PEER_HEADS, -1), pos, axis=-1)
        g = jax.nn.softmax(best, axis=-1)
        u = u_tab[experts]
        v = v_tab[experts]
        h = jax.nn.gelu(jnp.einsum('thkd,td->thk', u, xc).astype(jnp.float32))
        return jnp.einsum('thk,thkd->td', (g * h).astype(v.dtype), v)

    return lax.map(chunk, xt).reshape(Bsz, S, D).astype(x.dtype)

def hybrid_layer(x, w_in, b_in, ssm_a_re, ssm_a_im, ssm_log_dt, ssm_b_re, ssm_b_im,
                 ssm_c_re, ssm_c_im, ssm_d, w_glu, w_up_ssm,
                 nsa_pe_k, nsa_w1_k, nsa_w2_k, nsa_pe_v, nsa_w1_v, nsa_w2_v, w_up_nsa,
                 w_out, ln1_g, ln1_b, peer_w_q, peer_subkeys, peer_u, peer_v, ln2_g, ln2_b):
    sizes = [SSM_WIDTH, NSA_WIDTH] + [KV_WIDTH] * 6 + [3 * NSA_HEADS, 2 * D_MODEL]
    offsets = np.cumsum(sizes)[:-1].tolist()
    proj = x @ w_in + b_in
    u_ssm, q, k_cmp, v_cmp, k_slc, v_slc, k_win, v_win, nsa_gates, merge_logits = jnp.split(proj, offsets, axis=-1)
    y_a = s5_mixer(u_ssm, ssm_a_re, ssm_a_im, ssm_log_dt, ssm_b_re, ssm_b_im,
                   ssm_c_re, ssm_c_im, ssm_d, w_glu) @ w_up_ssm
    y_b = nsa_mixer(q, k_cmp, v_cmp, k_slc, v_slc, k_win, v_win, nsa_gates,
                    nsa_pe_k, nsa_w1_k, nsa_w2_k, nsa_pe_v, nsa_w1_v, nsa_w2_v) @ w_up_nsa
    g_a, g_b = jnp.split(jax.nn.sigmoid(merge_logits), 2, axis=-1)
    mix = (g_a * y_a + g_b * y_b) @ w_out
    x = layer_norm(DN_ALPHA * x + mix, ln1_g, ln1_b)
    y = peer_ffn(x, peer_w_q, peer_subkeys, peer_u, peer_v)
    return layer_norm(DN_ALPHA * x + y, ln2_g, ln2_b)

def setup_inputs(seed: int = 0) -> dict:
    key = jax.random.key(seed)
    ks = jax.random.split(key, 32)
    f32 = jnp.float32

    def nrm(k, shape, scale):
        return jax.random.normal(k, shape, f32) * scale

    L = DEPTH
    P, G, H = SSM_STATE, SSM_GROUPS, SSM_GROUP
    ldk = CMP_BLOCK * NSA_HEAD_DIM
    return {
        "x": nrm(ks[0], (BATCH, SEQ, D_MODEL), 1.0),
        "w_in": nrm(ks[1], (L, D_MODEL, IN_COLS), D_MODEL ** -0.5),
        "b_in": nrm(ks[2], (L, IN_COLS), 0.02),
        "ssm_a_re": -0.5 + nrm(ks[3], (L, G, P), 0.01),
        "ssm_a_im": jnp.pi * jnp.arange(P, dtype=f32)[None, None, :] + nrm(ks[4], (L, G, P), 0.01),
        "ssm_log_dt": jax.random.uniform(ks[5], (L, G), f32, math.log(1e-3), math.log(1e-1)),
        "ssm_b_re": nrm(ks[6], (L, G, P, H), (2.0 * H) ** -0.5),
        "ssm_b_im": nrm(ks[7], (L, G, P, H), (2.0 * H) ** -0.5),
        "ssm_c_re": nrm(ks[8], (L, G, H, P), P ** -0.5),
        "ssm_c_im": nrm(ks[9], (L, G, H, P), P ** -0.5),
        "ssm_d": nrm(ks[10], (L, SSM_WIDTH), 1.0),
        "w_glu": nrm(ks[11], (L, SSM_WIDTH, 2 * SSM_WIDTH), SSM_WIDTH ** -0.5),
        "w_up_ssm": nrm(ks[12], (L, SSM_WIDTH, D_MODEL), SSM_WIDTH ** -0.5),
        "nsa_pe_k": nrm(ks[13], (L, CMP_BLOCK, NSA_HEAD_DIM), 0.1),
        "nsa_w1_k": nrm(ks[14], (L, ldk, CMP_HIDDEN), ldk ** -0.5),
        "nsa_w2_k": nrm(ks[15], (L, CMP_HIDDEN, NSA_HEAD_DIM), CMP_HIDDEN ** -0.5),
        "nsa_pe_v": nrm(ks[16], (L, CMP_BLOCK, NSA_HEAD_DIM), 0.1),
        "nsa_w1_v": nrm(ks[17], (L, ldk, CMP_HIDDEN), ldk ** -0.5),
        "nsa_w2_v": nrm(ks[18], (L, CMP_HIDDEN, NSA_HEAD_DIM), CMP_HIDDEN ** -0.5),
        "w_up_nsa": nrm(ks[19], (L, NSA_WIDTH, D_MODEL), NSA_WIDTH ** -0.5),
        "w_out": nrm(ks[20], (L, D_MODEL, D_MODEL), DN_BETA * D_MODEL ** -0.5),
        "ln1_g": 1.0 + nrm(ks[21], (L, D_MODEL), 0.05),
        "ln1_b": nrm(ks[22], (L, D_MODEL), 0.02),
        "peer_w_q": nrm(ks[23], (L, D_MODEL, PEER_HEADS * PEER_KEY_DIM), D_MODEL ** -0.5),
        "peer_subkeys": nrm(ks[24], (L, PEER_HEADS, 2, PEER_NKEYS, PEER_KEY_DIM // 2), (PEER_KEY_DIM // 2) ** -0.5),
        "peer_u": nrm(ks[25], (L, PEER_EXPERTS, D_MODEL), D_MODEL ** -0.5),
        "peer_v": nrm(ks[26], (L, PEER_EXPERTS, D_MODEL), DN_BETA),
        "ln2_g": 1.0 + nrm(ks[27], (L, D_MODEL), 0.05),
        "ln2_b": nrm(ks[28], (L, D_MODEL), 0.02),
    }

def reference(x, w_in, b_in, ssm_a_re, ssm_a_im, ssm_log_dt, ssm_b_re, ssm_b_im,
              ssm_c_re, ssm_c_im, ssm_d, w_glu, w_up_ssm,
              nsa_pe_k, nsa_w1_k, nsa_w2_k, nsa_pe_v, nsa_w1_v, nsa_w2_v, w_up_nsa,
              w_out, ln1_g, ln1_b, peer_w_q, peer_subkeys, peer_u, peer_v, ln2_g, ln2_b):
    for l in range(DEPTH):
        x = hybrid_layer(x, w_in[l], b_in[l], ssm_a_re[l], ssm_a_im[l], ssm_log_dt[l],
                         ssm_b_re[l], ssm_b_im[l], ssm_c_re[l], ssm_c_im[l], ssm_d[l],
                         w_glu[l], w_up_ssm[l],
                         nsa_pe_k[l], nsa_w1_k[l], nsa_w2_k[l], nsa_pe_v[l], nsa_w1_v[l], nsa_w2_v[l],
                         w_up_nsa[l], w_out[l], ln1_g[l], ln1_b[l],
                         peer_w_q[l], peer_subkeys[l], peer_u[l], peer_v[l], ln2_g[l], ln2_b[l])
    return x


_drawn_inputs = setup_inputs


def setup_inputs(seed=0):
    import zlib

    import numpy as np

    out = dict(_drawn_inputs(seed))
    spreads = {}
    factors = {'b_in': 2.779,
     'ssm_a_re': 64.0,
     'ssm_b_re': 2.672,
     'nsa_pe_k': 7.362,
     'ln2_b': 2.741,
     'ssm_b_im': 4.172,
     'ssm_c_re': 2.752,
     'ssm_c_im': 2.856}
    for name, (base, spread) in spreads.items():
        noise = np.random.default_rng([zlib.crc32(name.encode()), seed]).standard_normal(out[name].shape)
        drawn = base * np.exp(spread * noise) if base else spread * noise
        out[name] = __import__('jax').numpy.asarray(drawn.astype(out[name].dtype))
    for name, factor in factors.items():
        out[name] = (out[name] * factor).astype(out[name].dtype)
    return out
```

```python
from contextlib import ExitStack
import math

import numpy as np

import concourse.bass as bass
from concourse import mybir

F32 = mybir.dt.float32
U32 = mybir.dt.uint32
ALU = mybir.AluOpType
ACT = mybir.ActivationFunctionType
AX = mybir.AxisListType

P = 128
D = 1024
S = 512
KD = D // P
TT = S // P
SSM = D // 2
SG, SH, SP = 32, 16, 64
NPAIR = SG // 2
CH = SSM // P
HEADS, KVG, HD = 8, 2, 64
HPG = HEADS // KVG
CB, CS = 32, 16
NCMP = (S - CB) // CS + 1
NC32 = 32
GATES = 3 * HEADS
PH, PK, PE_TOP = 8, 128, 16
NEG = -1e30
DN_ALPHA = 2.0 ** 0.25
LN_EPS = 1e-5

C_U, C_Q = 0, SSM
C_KC = C_Q + SSM
C_VC, C_KS, C_VS, C_KW, C_VW, C_G = (C_KC + P * n for n in range(1, 7))
C_M = C_G + GATES
C_END = C_M + 2 * D
W_GROUPS = [(0, 512), (512, 1024), (1024, 1536), (1536, C_M)] + [(C_M + 512 * n, C_M + 512 * (n + 1)) for n in range(4)]
W_RING = 3
G_Q = 1
R_U, R_Q, R_KC, R_VC, R_KS, R_KW, R_M, R_D = 0, 4, 8, 9, 10, 11, 12, 28
PI2_A = 6.28125
PI2_B = float(np.round((2 * math.pi - PI2_A) * 2 ** 20) / 2 ** 20)
PI2_C = 2 * math.pi - PI2_A - PI2_B
ROUND = 1.5 * 2.0 ** 23

UNITS = (
    [("u", 0, P * c, c) for c in range(4)]
    + [("q", 1, P * c, c) for c in range(4)]
    + [("kc", 2, 0, 0), ("vc", 2, P, 0), ("ks", 2, 2 * P, 0), ("kw", 3, 0, 0)]
    + [("vg", 3, 0, t) for t in range(TT)]
    + [("m", 4 + c // 4, P * (c % 4), c) for c in range(16)]
)
BY_ACT = ("u", "m")
NX = 2 * TT


def build(nc: bass.Bass, a, out, dbg=None):
    l0 = lambda name: a[name][0]
    ctx = ExitStack()
    with ctx:
        def sb(name, shape, dt=F32, on=ctx):
            return on.enter_context(nc.sbuf_tensor(name, shape, dt))

        def sem(name):
            return ctx.enter_context(nc.semaphore(name))

        def spread(vec, n):
            return vec.rearrange("(a n) -> a n", a=1).broadcast_to([P, n])

        bank = [ctx.enter_context(nc.psum_tensor(f"bank{i}", [P, 512], F32)) for i in range(8)]

        def chained(eng, sem_):
            n = [0]

            def link(ins):
                n[0] += 1
                ins.then_inc(sem_, 1)
                eng.wait_ge(sem_, n[0])
            return link

        ident = sb("ident", [P, P])
        col = sb("col", [P, 32])
        x1 = sb("x1", [P, TT, D])
        x1T = sb("x1T", [P, KD, S])
        early = ExitStack()
        gmT = sb("gmT", [P, 16, S], on=early)
        uT = sb("uT", [P, CH, S], on=early)
        gluT = sb("gluT", [P, CH, S], on=early)
        qT = sb("qT", [P, 4, S], on=early)
        kT = sb("kT", [P, 4, S], on=early)
        nsaT = sb("nsaT", [P, CH, S], on=early)
        vN = sb("vN", [P, TT, 2 * P + GATES], on=early)

        p1 = ExitStack()
        xN = sb("xN", [P, TT, D], on=p1)
        xT = sb("xT", [P, KD, S], on=p1)
        wr = sb("wr", [P, W_RING, KD, 512], on=p1)
        rows = sb("rows", [32, P], on=p1)
        vbias = sb("vbias", [P, 2 * P + GATES], on=p1)
        iota_d = sb("iota_d", [P, P], on=p1)
        p1.close()

        s_x = sem("x_loaded")
        s_rows = sem("rows_loaded")
        s_w = [sem(f"w_in_loaded{n}") for n in range(W_RING)]
        s_iota = sem("iota_made")
        s_id = sem("identity_made")
        s_unit = sem("units_made")
        s_act = sem("units_taken_by_act")
        s_dve = sem("units_taken_by_dve")
        s_v1 = sem("dve_steps_1")

        w_in, b_in = l0("w_in"), l0("b_in")
        taken = [("dve", 0)] * (NX + 1) + [("act" if k in BY_ACT else "dve", 0) for k, *_ in UNITS]
        nth = []
        seen = {"act": 0, "dve": 0}
        for e, _ in taken:
            seen[e] += 1
            nth.append((e, seen[e]))
        w_landed = [16 * sum(KD * KVG if h == G_Q else 1 for h in range(g % W_RING, g + 1, W_RING)) for g in range(len(W_GROUPS))]
        last_unit = {}
        for n, (_, g, _, _) in enumerate(UNITS):
            last_unit[g] = NX + 1 + n + 1
        last_unit[2] = last_unit[3]

        with nc.Block() as block:
            @block.sync
            def _(sp):
                for t in range(TT):
                    sp.dma_start(xN[:, t, :], a["x"][0, t * P:(t + 1) * P, :]).then_inc(s_x, 16)
                sp.dma_start(rows[R_U:R_U + 4, :], b_in[C_U:C_U + SSM].rearrange("(r c) -> r c", c=P)).then_inc(s_rows, 16)
                for g in range(KVG):
                    sp.dma_start(rows[R_Q:R_Q + 4, g * HD:(g + 1) * HD],
                                 b_in[C_Q + 256 * g:C_Q + 256 * (g + 1)].rearrange("(r c) -> r c", c=HD)).then_inc(s_rows, 16)
                for r, c, n in ((R_KC, C_KC, 3), (R_KW, C_KW, 1), (R_M, C_M, 16)):
                    sp.dma_start(rows[r:r + n, :], b_in[c:c + n * P].rearrange("(r c) -> r c", c=P)).then_inc(s_rows, 16)
                sp.dma_start(rows[R_D:R_D + 4, :], l0("ssm_d").rearrange("(r c) -> r c", c=P)).then_inc(s_rows, 16)
                sp.dma_start(vbias[:, 0:P], spread(b_in[C_VS:C_VS + P], P)).then_inc(s_rows, 16)
                sp.dma_start(vbias[:, P:], spread(b_in[C_VW:C_M], P + GATES)).then_inc(s_rows, 16)
                for g, (c0, c1) in enumerate(W_GROUPS):
                    if g >= W_RING:
                        sp.wait_ge(s_unit, last_unit[g - W_RING])
                    if g == G_Q:
                        for k in range(KD):
                            for j in range(KVG):
                                sp.dma_start(wr[:, g % W_RING, k].rearrange("p (r j d) -> p j r d", j=KVG, d=HD)[:, j],
                                             w_in[k * P:(k + 1) * P, c0 + 256 * j:c0 + 256 * (j + 1)]
                                             .rearrange("p (r d) -> p r d", d=HD)).then_inc(s_w[g % W_RING], 16)
                        continue
                    sp.dma_start(wr[:, g % W_RING, :, 0:c1 - c0],
                                 w_in[:, c0:c1].rearrange("(k p) c -> p k c", p=P)).then_inc(s_w[g % W_RING], 16)

            @block.gpsimd
            def _(pool):
                pool.iota(iota_d[:], [[1, P]], base=0, channel_multiplier=-1,
                          allow_small_or_imprecise_dtypes=True).then_inc(s_iota, 1)

            @block.tensor
            def _(pe):
                pe.wait_ge(s_id, 1)

                def free(n):
                    if n >= 8:
                        e, m = nth[n - 8]
                        pe.wait_ge(s_act if e == "act" else s_dve, m)
                for t in range(TT):
                    pe.wait_ge(s_x, 16 * (TT))
                    for h in range(2):
                        n = 2 * t + h
                        for k in range(4):
                            last = pe.transpose(bank[n][:, k * P:(k + 1) * P],
                                                xN[:, t, (4 * h + k) * P:(4 * h + k + 1) * P], ident[:])
                        last.then_inc(s_unit, 1)
                pe.wait_ge(s_rows, 16 * 9)
                free(NX)
                pe.transpose(bank[NX % 8][:, 0:32], rows[:], ident[0:32, 0:32]).then_inc(s_unit, 1)
                pe.wait_ge(s_dve, NX)
                for m, (kind, g, c0, i) in enumerate(UNITS):
                    n = NX + 1 + m
                    b = bank[n % 8]
                    pe.wait_ge(s_w[g % W_RING], w_landed[g])
                    free(n)
                    w = wr[:, g % W_RING]
                    for k in range(KD):
                        first, end = k == 0, k == KD - 1
                        if kind == "vg":
                            xt = xT[:, k, i * P:(i + 1) * P]
                            w2 = wr[:, 2 % W_RING, k, 3 * P:4 * P]
                            pe.matmul(b[:, 0:P], xt, w2, start=first, stop=end)
                        else:
                            last = pe.matmul(b[:], w[:, k, c0:c0 + P], xT[:, k, :], start=first, stop=end)
                    if kind == "vg":
                        for k in range(KD):
                            xt = xT[:, k, i * P:(i + 1) * P]
                            last = pe.matmul(b[:, P:2 * P + GATES], xt, w[:, k, P:2 * P + GATES],
                                             start=k == 0, stop=k == KD - 1)
                    last.then_inc(s_unit, 1)

            @block.scalar
            def _(act):
                act.wait_ge(s_dve, NX + 1)
                for m, (kind, g, c0, i) in enumerate(UNITS):
                    n = NX + 1 + m
                    if kind == "u":
                        act.wait_ge(s_unit, n + 1)
                        act.activation(uT[:, i, :], bank[n % 8][:], ACT.Identity,
                                       bias=col[:, R_U + i:R_U + i + 1]).then_inc(s_act, 1)
                    elif kind == "m":
                        act.wait_ge(s_unit, n + 1)
                        act.activation(gmT[:, i, :], bank[n % 8][:], ACT.Sigmoid,
                                       bias=col[:, R_M + i:R_M + i + 1]).then_inc(s_act, 1)

            @block.vector
            def _(dve):
                dve.wait_ge(s_iota, 1)
                dve.tensor_scalar(ident[:], iota_d[:], 0.0, None, ALU.is_equal).then_inc(s_id, 1)
                for n in range(NX):
                    t, h = n // 2, n % 2
                    dve.wait_ge(s_unit, n + 1)
                    dve.tensor_copy(xT[:, 4 * h:4 * h + 4, t * P:(t + 1) * P],
                                    bank[n][:].rearrange("p (k t) -> p k t", k=4)).then_inc(s_dve, 1)
                dve.wait_ge(s_unit, NX + 1)
                dve.tensor_copy(col[:], bank[NX % 8][:, 0:32]).then_inc(s_dve, 1)
                dve.wait_ge(s_dve, NX + 1)
                for m, (kind, g, c0, i) in enumerate(UNITS):
                    n = NX + 1 + m
                    b = bank[n % 8]
                    if kind in BY_ACT:
                        continue
                    dve.wait_ge(s_unit, n + 1)
                    if kind == "q":
                        ins = dve.tensor_scalar(qT[:, i, :], b[:], col[:, R_Q + i:R_Q + i + 1], HD ** -0.5, ALU.add, ALU.mult)
                    elif kind == "vg":
                        ins = dve.tensor_tensor(vN[:, i, :], b[:, 0:2 * P + GATES], vbias[:], ALU.add)
                    else:
                        j = ("kc", "vc", "ks", "kw").index(kind)
                        ins = dve.tensor_scalar(kT[:, j, :], b[:], col[:, R_KC + j:R_KC + j + 1], None, ALU.add)
                    ins.then_inc(s_dve, 1)


        TA, TB = 16, 32
        p2 = ExitStack()
        sa = sb("sa", [NPAIR, 2, P], on=p2)
        sdt = sb("sdt", [NPAIR, 2], on=p2)
        sdtx = sb("sdtx", [NPAIR, 2, SP], on=p2)
        prm = sb("prm", [NPAIR, 5, P], on=p2)
        wk = sb("wk", [NPAIR, 8, P], on=p2)
        prT = sb("prT", [P, 5, NPAIR], on=p2)
        ea = sb("ea", [P, 2, NPAIR, TA], on=p2)
        eb = sb("eb", [P, 2, NPAIR, TB], on=p2)
        pw = sb("pw", [P, 2, NPAIR], on=p2)
        wp = sb("wp", [P, 4, NPAIR, TB], on=p2)
        braw = sb("braw", [P, 2, NPAIR, SH], on=p2)
        bbar = sb("bbar", [P, 2, NPAIR, 2, SH], on=p2)
        bT = sb("bT", [P, 2, CH, P], on=p2)
        craw = sb("craw", [P, 2, CH, SP], on=p2)
        cw = sb("cw", [P, 2, CH, 2, SP], on=p2)
        cT = sb("cT", [P, 2, CH, P], on=p2)
        half_i = sb("half_i", [P, 1], mybir.dt.int32, on=p2)
        half = sb("half", [P, 2], on=p2)
        et = sb("et", [P, 2, 2, S], on=p2)
        er = sb("er", [P, 4, S], on=p2)
        br = sb("br", [P, 4, S], on=p2)
        zin = sb("zin", [P, 2, S], on=p2)
        z = sb("z", [P, 2, 2, S], on=p2)
        xr = sb("xr", [P, 4, S], on=p2)
        xs = sb("xs", [P, 2, 2, S], on=p2)
        wg, sg = x1, x1T[:, 0:CH]
        p2.close()

        s_par = sem("s5_params_loaded")
        s_bc = sem("s5_b_c_loaded")
        s_wg = sem("w_glu_loaded")
        s_v2 = sem("dve_steps_2")
        s_a2 = sem("act_steps_2")
        s_p2 = sem("pool_steps_2")
        s_prm = sem("params_ready_to_turn")
        s_turn = sem("params_turned")
        s_bbar = sem("b_ready_to_turn")
        s_cw = sem("c_ready_to_turn")
        s_bct = sem("b_c_turned")
        s_bcs = sem("b_c_in_place")
        s_half = sem("halves_made")
        s_table = sem("tables_of_pairs")
        s_bu = sem("inputs_of_pairs")
        s_rot = sem("inputs_rotated")
        s_scan = sem("pairs_scanned")
        s_back = sem("pairs_rotated_back")
        s_yc = sem("pairs_projected")
        s_ys = sem("skip_added")
        s_gel = sem("gelu_done")
        s_glu = sem("glu_units")
        s_sig = sem("glu_gates")
        s_out2 = sem("glu_products")

        with nc.Block() as block:
            @block.sync
            def _(sp):
                sp.dma_start(sa[:, 0, :], l0("ssm_a_re").rearrange("(q g) s -> q (g s)", g=2)).then_inc(s_par, 16)
                sp.dma_start(sa[:, 1, :], l0("ssm_a_im").rearrange("(q g) s -> q (g s)", g=2)).then_inc(s_par, 16)
                sp.dma_start(sdt[:], l0("ssm_log_dt").rearrange("(q g) -> q g", g=2)).then_inc(s_par, 16)
                for n, name in enumerate(("ssm_b_re", "ssm_b_im")):
                    sp.dma_start(braw[:, n], l0(name).rearrange("(q g) s h -> (g s) q h", g=2)).then_inc(s_bc, 16)
                for n, name in enumerate(("ssm_c_re", "ssm_c_im")):
                    sp.dma_start(craw[:, n], l0(name).rearrange("(c g) h s -> (g h) c s", c=CH)).then_inc(s_bc, 16)
                sp.dma_start(wg[:], l0("w_glu").rearrange("(k p) n -> p k n", p=P)).then_inc(s_wg, 16)

            @block.gpsimd
            def _(pool):
                link = chained(pool, s_p2)
                pool.iota(half_i[:], [[0, 1]], base=0, channel_multiplier=1).then_inc(s_half, 1)
                pool.memset(bbar[:], 0.0).then_inc(s_half, 1)
                for q in range(NPAIR):
                    o = q % 2
                    pool.wait_ge(s_scan, q + 1)
                    if q >= 2:
                        pool.wait_ge(s_yc, q - 1)
                    zr, zi, c, s = z[:, o, 0], z[:, o, 1], et[:, o, 0], et[:, o, 1]
                    pool.tensor_tensor(xr[:, 0], zr, c, ALU.mult)
                    pool.tensor_tensor(xr[:, 1], zi, s, ALU.mult)
                    pool.tensor_tensor(xr[:, 2], zr, s, ALU.mult)
                    link(pool.tensor_tensor(xr[:, 3], zi, c, ALU.mult))
                    pool.tensor_tensor(xs[:, o, 0], xr[:, 0], xr[:, 1], ALU.subtract)
                    link(pool.tensor_tensor(xs[:, o, 1], xr[:, 2], xr[:, 3], ALU.add))
                    pool.sem_inc(s_back, 1)

            @block.scalar
            def _(act):
                link = chained(act, s_a2)
                act.wait_ge(s_par, 48)
                link(act.activation(sdt[:], sdt[:], ACT.Exp))
                act.wait_ge(s_v2, 2)
                link(act.activation(prm[:, 0, :], wk[:, 0, :], ACT.Exp))
                act.wait_ge(s_v2, 9)
                link(act.activation(wk[:, 3, :], wk[:, 2, :], ACT.Sin))
                link(act.activation(wk[:, 4, :], wk[:, 2, :], ACT.Sin, scale=0.5))
                for c in range(CH):
                    act.wait_ge(s_ys, c + 1)
                    act.activation(uT[:, c, :], uT[:, c, :], ACT.Gelu_apprx_tanh).then_inc(s_gel, 1)
                for c in range(CH):
                    act.wait_ge(s_glu, c + 1)
                    act.activation(sg[:, c, :], bank[c][:], ACT.Sigmoid).then_inc(s_sig, 1)

            @block.tensor
            def _(pe):
                pe.wait_ge(s_prm, 1)
                for n in range(5):
                    last = pe.transpose(bank[0][:, n * NPAIR:(n + 1) * NPAIR], prm[:, n, :], ident[0:NPAIR, 0:NPAIR])
                last.then_inc(s_turn, 1)
                pe.wait_ge(s_bbar, 1)
                for n in range(2):
                    for c in range(CH):
                        last = pe.transpose(bank[1 + n][:, c * P:(c + 1) * P],
                                            bbar[:, n, 4 * c:4 * c + 4].rearrange("p q g h -> p (q g h)"), ident[:])
                last.then_inc(s_bct, 1)
                pe.wait_ge(s_cw, 1)
                for n in range(2):
                    for c in range(CH):
                        last = pe.transpose(bank[3 + n][:, c * P:(c + 1) * P],
                                            cw[:, n, c].rearrange("p g s -> p (g s)"), ident[:])
                last.then_inc(s_bct, 1)
                pe.wait_ge(s_bcs, 4)

                def inputs(q):
                    if q >= 2:
                        pe.wait_ge(s_rot, q - 1)
                    c, r = q // 4, 32 * (q % 4)
                    for n in range(2):
                        last = pe.matmul(bank[2 * (q % 2) + n][:], bT[r:r + 32, n, c, :], uT[r:r + 32, c, :],
                                         start=True, stop=True)
                    last.then_inc(s_bu, 1)

                inputs(0)
                for q in range(NPAIR):
                    if q + 1 < NPAIR:
                        inputs(q + 1)
                    pe.wait_ge(s_back, q + 1)
                    c, r = q // 4, 32 * (q % 4)
                    for n in range(2):
                        last = pe.matmul(bank[4 + c][r:r + 32, :], cT[:, n, c, r:r + 32], xs[:, q % 2, n, :],
                                         start=n == 0, stop=n == 1)
                    last.then_inc(s_yc, 1)
                pe.wait_ge(s_wg, 16)
                for half_ in (1, 0):
                    for c in range(CH):
                        for k in range(CH):
                            pe.wait_ge(s_gel, k + 1)
                            last = pe.matmul(bank[4 * (1 - half_) + c][:], wg[:, k, half_ * SSM + c * P:half_ * SSM + (c + 1) * P],
                                             uT[:, k, :], start=k == 0, stop=k == CH - 1)
                        last.then_inc(s_glu, 1)

            @block.vector
            def _(dve):
                link = chained(dve, s_v2)
                dve.wait_ge(s_a2, 1)
                dtb = sdt[:].unsqueeze(2).broadcast_to([NPAIR, 2, SP])
                w = lambda n: wk[:, n, :]
                link(dve.tensor_copy(sdtx[:], dtb))
                dts = sdtx[:].rearrange("p g s -> p (g s)")
                link(dve.tensor_tensor(w(0), sa[:, 0, :], dts, ALU.mult))
                link(dve.tensor_tensor(w(1), sa[:, 1, :], dts, ALU.mult))
                link(dve.tensor_scalar(w(5), w(1), 1 / (2 * math.pi), ROUND, ALU.mult, ALU.add))
                link(dve.tensor_scalar(w(5), w(5), ROUND, None, ALU.subtract))
                link(dve.scalar_tensor_tensor(w(1), w(5), -PI2_A, w(1), ALU.mult, ALU.add))
                link(dve.scalar_tensor_tensor(w(6), w(5), -PI2_B, w(1), ALU.mult, ALU.add))
                link(dve.scalar_tensor_tensor(w(6), w(5), -PI2_C, w(6), ALU.mult, ALU.add))
                link(dve.tensor_scalar(w(2), w(6), 3.1415925, -3.1415925, ALU.min, ALU.max))
                dve.wait_ge(s_a2, 4)
                link(dve.tensor_tensor(w(5), w(4), w(4), ALU.mult))
                link(dve.tensor_scalar(w(5), w(5), -2.0, 1.0, ALU.mult, ALU.add))
                link(dve.tensor_tensor(w(6), w(5), w(5), ALU.mult))
                link(dve.tensor_tensor(w(7), w(3), w(3), ALU.mult))
                link(dve.tensor_tensor(w(6), w(6), w(7), ALU.add))
                link(dve.tensor_scalar(w(6), w(6), -0.5, 1.5, ALU.mult, ALU.add))
                link(dve.tensor_tensor(prm[:, 1, :], w(5), w(6), ALU.mult))
                link(dve.tensor_tensor(prm[:, 2, :], w(3), w(6), ALU.mult))
                link(dve.tensor_tensor(w(0), prm[:, 0, :], prm[:, 1, :], ALU.mult))
                link(dve.tensor_scalar(w(0), w(0), 1.0, None, ALU.subtract))
                link(dve.tensor_tensor(w(1), prm[:, 0, :], prm[:, 2, :], ALU.mult))
                link(dve.tensor_tensor(w(2), sa[:, 0, :], sa[:, 0, :], ALU.mult))
                link(dve.tensor_tensor(w(3), sa[:, 1, :], sa[:, 1, :], ALU.mult))
                link(dve.tensor_tensor(w(2), w(2), w(3), ALU.add))
                link(dve.reciprocal(w(2), w(2)))
                link(dve.tensor_tensor(w(4), w(0), sa[:, 0, :], ALU.mult))
                link(dve.tensor_tensor(w(5), w(1), sa[:, 1, :], ALU.mult))
                link(dve.tensor_tensor(w(4), w(4), w(5), ALU.add))
                link(dve.tensor_tensor(w(6), w(1), sa[:, 0, :], ALU.mult))
                link(dve.tensor_tensor(w(7), w(0), sa[:, 1, :], ALU.mult))
                link(dve.tensor_tensor(w(6), w(6), w(7), ALU.subtract))
                link(dve.tensor_tensor(prm[:, 3, :], w(4), w(2), ALU.mult))
                link(dve.tensor_tensor(prm[:, 4, :], w(6), w(2), ALU.mult))
                dve.sem_inc(s_prm, 1)
                dve.wait_ge(s_half, 2)
                link(dve.tensor_scalar(half_i[:], half_i[:], 4, 1, ALU.arith_shift_right, ALU.bitwise_and))
                link(dve.tensor_copy(half[:, 1:2], half_i[:]))
                link(dve.tensor_scalar(half[:, 0:1], half[:, 1:2], -1.0, 1.0, ALU.mult, ALU.add))
                dve.wait_ge(s_bc, 64)
                for n in range(2):
                    for g in range(2):
                        link(dve.tensor_scalar(cw[:, n, :, g, :], craw[:, n], half[:, g:g + 1],
                                               1.0 - 2.0 * n, ALU.mult, ALU.mult))
                dve.sem_inc(s_cw, 1)
                dve.wait_ge(s_turn, 1)
                link(dve.tensor_copy(prT[:], bank[0][:, 0:5 * NPAIR].rearrange("p (n q) -> p n q", n=5)))
                fr = prT[:, 3, :].unsqueeze(2).broadcast_to([P, NPAIR, SH])
                fi = prT[:, 4, :].unsqueeze(2).broadcast_to([P, NPAIR, SH])
                t = lambda n: wp[:, n, :, 0:SH]
                for n, (x, y, op) in enumerate(((fr, fi, ALU.subtract), (fi, fr, ALU.add))):
                    link(dve.tensor_tensor(t(0), x, braw[:, 0], ALU.mult))
                    link(dve.tensor_tensor(t(1), y, braw[:, 1], ALU.mult))
                    for g in range(2):
                        h = slice(g * SP, (g + 1) * SP)
                        link(dve.tensor_tensor(bbar[h, n, :, g, :], wp[h, 0, :, 0:SH], wp[h, 1, :, 0:SH], op))
                dve.sem_inc(s_bbar, 1)

                def cmul(oc, os, ac, as_, bc, bs, tmp):
                    link(dve.tensor_tensor(tmp(0), ac, bc, ALU.mult))
                    link(dve.tensor_tensor(tmp(1), as_, bs, ALU.mult))
                    link(dve.tensor_tensor(tmp(2), ac, bs, ALU.mult))
                    link(dve.tensor_tensor(tmp(3), as_, bc, ALU.mult))
                    link(dve.tensor_tensor(oc, tmp(0), tmp(1), ALU.subtract))
                    link(dve.tensor_tensor(os, tmp(2), tmp(3), ALU.add))

                def powers(tab, count):
                    link(dve.memset(tab[:, 0, :, 0:1], 1.0))
                    link(dve.memset(tab[:, 1, :, 0:1], 0.0))
                    n = 1
                    while n < count:
                        bc = pw[:, 0, :].unsqueeze(2).broadcast_to([P, NPAIR, n])
                        bs = pw[:, 1, :].unsqueeze(2).broadcast_to([P, NPAIR, n])
                        cmul(tab[:, 0, :, n:2 * n], tab[:, 1, :, n:2 * n], tab[:, 0, :, 0:n], tab[:, 1, :, 0:n],
                             bc, bs, lambda m: wp[:, m, :, 0:n])
                        cmul(pw[:, 0, :], pw[:, 1, :], pw[:, 0, :], pw[:, 1, :], pw[:, 0, :], pw[:, 1, :],
                             lambda m: wp[:, m, :, 0])
                        link(dve.tensor_tensor(wp[:, 0, :, 0], pw[:, 0, :], pw[:, 0, :], ALU.mult))
                        link(dve.tensor_tensor(wp[:, 1, :, 0], pw[:, 1, :], pw[:, 1, :], ALU.mult))
                        link(dve.tensor_tensor(wp[:, 0, :, 0], wp[:, 0, :, 0], wp[:, 1, :, 0], ALU.add))
                        link(dve.tensor_scalar(wp[:, 0, :, 0], wp[:, 0, :, 0], -0.5, 1.5, ALU.mult, ALU.add))
                        link(dve.tensor_tensor(pw[:, 0, :], pw[:, 0, :], wp[:, 0, :, 0], ALU.mult))
                        link(dve.tensor_tensor(pw[:, 1, :], pw[:, 1, :], wp[:, 0, :, 0], ALU.mult))
                        n *= 2

                link(dve.tensor_copy(pw[:], prT[:, 1:3, :]))
                powers(eb, TB)
                powers(ea, TA)
                for n, (dst, src) in enumerate(((bT, 1), (cT, 3))):
                    dve.wait_ge(s_bct, n + 1)
                    for m in range(2):
                        dve.tensor_copy(dst[:, m], bank[src + m][:].rearrange("p (c x) -> p c x", c=CH)).then_inc(s_bcs, 1)

                def table(q):
                    o = q % 2
                    if q >= 2:
                        dve.wait_ge(s_back, q - 1)
                    A = lambda n: ea[:, n, q, :].unsqueeze(2).broadcast_to([P, TA, TB])
                    B = lambda n: eb[:, n, q, :].unsqueeze(1).broadcast_to([P, TA, TB])
                    v = lambda x: x.rearrange("p (a b) -> p a b", b=TB)
                    dve.tensor_tensor(v(er[:, 0]), A(0), B(0), ALU.mult)
                    dve.tensor_tensor(v(er[:, 1]), A(1), B(1), ALU.mult)
                    dve.tensor_tensor(v(er[:, 2]), A(0), B(1), ALU.mult)
                    link(dve.tensor_tensor(v(er[:, 3]), A(1), B(0), ALU.mult))
                    dve.tensor_tensor(et[:, o, 0], er[:, 0], er[:, 1], ALU.subtract)
                    link(dve.tensor_tensor(et[:, o, 1], er[:, 2], er[:, 3], ALU.add))

                for q in range(NPAIR):
                    o = q % 2
                    table(q)
                    c, s = et[:, o, 0], et[:, o, 1]
                    dve.wait_ge(s_bu, q + 1)
                    bre, bim = bank[2 * o][:], bank[2 * o + 1][:]
                    dve.tensor_tensor(br[:, 0], bre, c, ALU.mult)
                    dve.tensor_tensor(br[:, 1], bim, s, ALU.mult)
                    dve.tensor_tensor(br[:, 2], bim, c, ALU.mult)
                    link(dve.tensor_tensor(br[:, 3], bre, s, ALU.mult))
                    dve.sem_inc(s_rot, 1)
                    dve.tensor_tensor(zin[:, 0], br[:, 0], br[:, 1], ALU.add)
                    link(dve.tensor_tensor(zin[:, 1], br[:, 2], br[:, 3], ALU.subtract))
                    rr = prT[:, 0, q:q + 1].broadcast_to([P, S])
                    dve.tensor_tensor_scan(z[:, o, 0], rr, zin[:, 0], 0.0, ALU.mult, ALU.add)
                    link(dve.tensor_tensor_scan(z[:, o, 1], rr, zin[:, 1], 0.0, ALU.mult, ALU.add))
                    dve.sem_inc(s_scan, 1)
                for c in range(CH):
                    dve.wait_ge(s_yc, 4 * (c + 1))
                    dve.scalar_tensor_tensor(uT[:, c, :], uT[:, c, :], col[:, R_D + c:R_D + c + 1], bank[4 + c][:],
                                             ALU.mult, ALU.add).then_inc(s_ys, 1)
                for c in range(CH):
                    dve.wait_ge(s_sig, c + 1)
                    dve.wait_ge(s_glu, CH + c + 1)
                    dve.tensor_tensor(gluT[:, c, :], bank[4 + c][:], sg[:, c, :], ALU.mult).then_inc(s_out2, 1)

        NB = 2
        p3 = ExitStack()
        w1 = sb("w1", [P, 2, CB, P], on=p3)
        w2k = sb("w2k", [P, 2, HD], on=p3)
        w2v = sb("w2v", [P, HD], on=p3)
        pe_r = sb("pe_r", [CB, 2, 2, HD], on=p3)
        peT = sb("peT", [P, 2, CB], on=p3)
        blk = sb("blk", [P, 2, CB, NC32], on=p3)
        hT = sb("hT", [P, 2, KVG, NC32], on=p3)
        h4 = sb("h4", [P, KVG, HPG, NC32], on=p3)
        kcmp = sb("kcmp", [P, NC32], on=p3)
        vbd = sb("vbd", [P, KVG, HPG, HD], on=p3)
        slopes = sb("slopes", [P, HEADS], on=p3)
        dist = sb("dist", [P, S], on=p3)
        distc = sb("distc", [P, TT, NC32], on=p3)
        maskc = sb("maskc", [P, TT, NC32], on=p3)
        gate = sb("gate", [P, TT, GATES], on=p3)
        sc_c = sb("sc_c", [P, HEADS, NC32], on=p3)
        p_c = sb("p_c", [P, HEADS, NC32], on=p3)
        mx_c = sb("mx_c", [P, HEADS], on=p3)
        pTc = sb("pTc", [P, 2, P], on=p3)
        den = sb("den", [P, 2, 3, HEADS], on=p3)
        coef = sb("coef", [P, 3, HEADS], on=p3)
        sc = sb("sc", [P, 3, S], on=p3)
        nmx = sb("nmx", [P, 3], on=p3)
        pr = sb("pr", [P, 3, S], on=p3)
        pT = sb("pT", [P, 2, S], on=p3)
        acc = sb("acc", [P, HEADS, HD], on=p3)
        tmp3 = sb("tmp3", [P, HEADS, HD], on=p3)
        p3.close()

        s_w1 = sem("compression_loaded")
        s_tab = sem("distances_made")
        s_v3 = sem("dve_steps_3")
        s_pe3 = sem("pe_positions_turned")
        s_blk = sem("blocks_made")
        s_hid = sem("hidden_made")
        s_hT = sem("hidden_gelu")
        s_cmp = sem("compressed_made")
        s_cin = sem("compressed_in_place")
        s_gt = sem("gates_made")
        s_sc = sem("scores_made")
        s_mx = sem("scores_shifted")
        s_ex = sem("exponentials")
        s_tp = sem("probs_turned")
        s_pt = sem("probs_in_place")
        s_pv = sem("heads_weighed")
        s_scc = sem("cmp_scores_made")
        s_mxc = sem("cmp_scores_shifted")
        s_exc = sem("cmp_exponentials")
        s_pc = sem("cmp_probs_masked")
        s_tpc = sem("cmp_probs_turned")
        s_ptc = sem("cmp_probs_in_place")
        s_oc = sem("cmp_output_made")
        s_comb = sem("tiles_combined")
        s_nt = sem("tiles_turned")
        s_nT = sem("tiles_in_place")

        HU = [(i, b, h) for i in range(TT) for b in range(NB) for h in range(HEADS)]
        PT_ = NB * HEADS
        AT_COMBINE, AT_TURN, AT_TURNED, AT_CS, AT_CX, AT_CM, AT_CT, AT_CP, AT_CW = 1, 1, 2, 3, 6, 8, 9, 10, 11

        with nc.Block() as block:
            @block.sync
            def _(sp):
                for n, kv in enumerate("kv"):
                    for g in range(KVG):
                        sp.dma_start(w1[g * HD:(g + 1) * HD, n], l0(f"nsa_w1_{kv}").rearrange("(l d) h -> d l h", d=HD)).then_inc(s_w1, 16)
                        sp.dma_start(pe_r[:, n, g], l0(f"nsa_pe_{kv}")).then_inc(s_w1, 16)
                for g in range(KVG):
                    sp.dma_start(w2k[:, g], l0("nsa_w2_k")).then_inc(s_w1, 16)
                sp.dma_start(w2v[:], l0("nsa_w2_v")).then_inc(s_w1, 16)

            @block.gpsimd
            def _(pool):
                n = [0]

                def step(ins):
                    n[0] += 1
                    ins.then_inc(s_tab, 1)
                    pool.wait_ge(s_tab, n[0])
                for h in range(HEADS):
                    last = pool.memset(slopes[:, h:h + 1], 2.0 ** (-8.0 * (h + 1) / HEADS))
                step(last)
                step(pool.iota(dist[:], [[1, S]], base=-(S - P), channel_multiplier=-1, allow_small_or_imprecise_dtypes=True))
                step(pool.affine_select(dist[:], dist[:], [[-1, S]], ALU.is_ge, NEG, base=S - P, channel_multiplier=1))
                step(pool.iota(distc[:], [[-P, TT], [CS, NC32]], base=CB - 1, channel_multiplier=-1, allow_small_or_imprecise_dtypes=True))
                step(pool.memset(maskc[:], 1.0))
                step(pool.affine_select(distc[:], distc[:], [[P, TT], [-CS, NC32]], ALU.is_ge, NEG, base=-(CB - 1), channel_multiplier=1))
                step(pool.affine_select(maskc[:], maskc[:], [[P, TT], [-CS, NC32]], ALU.is_ge, 0.0, base=-(CB - 1), channel_multiplier=1))
                step(pool.memset(vbd[:], 0.0))
                step(pool.memset(blk[:], 0.0))

            @block.scalar
            def _(act):
                act.activation(gate[:], vN[:, :, 2 * P:], ACT.Sigmoid).then_inc(s_gt, 1)
                for n in range(4):
                    act.wait_ge(s_hid, n + 1)
                    act.activation(hT[:, n // 2, n % 2], bank[n][:, 0:NC32], ACT.Gelu_apprx_tanh).then_inc(s_hT, 1)

                def turned(u):
                    i = HU[u][0]
                    act.wait_ge(s_tp, u + 1)
                    if u >= 2:
                        act.wait_ge(s_pv, u - 1)
                    act.activation(pT[:, u % 2, 0:P * (i + 1)], bank[2 + u % 2][:, 0:P * (i + 1)], ACT.Copy).then_inc(s_pt, 1)

                for u, (i, b, h) in enumerate(HU):
                    if u % PT_ == AT_CX + 1:
                        act.wait_ge(s_mxc, i + 1)
                        act.activation(p_c[:], sc_c[:], ACT.Exp).then_inc(s_exc, 1)
                    act.wait_ge(s_mx, u + 1)
                    if u >= 3:
                        act.wait_ge(s_tp, u - 2)
                    if i >= 2:
                        act.wait_ge(s_comb, i - 1)
                    L = P * (i + 1)
                    act.activation(pr[:, u % 3, 0:L], sc[:, u % 3, 0:L], ACT.Exp, bias=nmx[:, u % 3:u % 3 + 1],
                                   accum_out=den[:, i % 2, 1 + b, h:h + 1]).then_inc(s_ex, 1)
                    if u >= 1:
                        turned(u - 1)
                turned(len(HU) - 1)

            @block.tensor
            def _(pe):
                pe.wait_ge(s_w1, 16 * 11)
                for n in range(2):
                    last = pe.transpose(bank[4][:, n * CB:(n + 1) * CB], pe_r[:, n].rearrange("l g d -> l (g d)"), ident[0:CB, 0:CB])
                last.then_inc(s_pe3, 1)
                for n in range(2):
                    pe.wait_ge(s_blk, n + 1)
                    for g in range(KVG):
                        r = slice(g * HD, (g + 1) * HD)
                        for l in range(CB):
                            last = pe.matmul(bank[2 * n + g][:, 0:NC32], w1[r, n, l, :], blk[r, n, l, :],
                                             start=l == 0, stop=l == CB - 1)
                        last.then_inc(s_hid, 1)
                pe.wait_ge(s_hT, 2)
                pe.matmul(bank[5][:, 0:2 * NC32], w2k[:].rearrange("p g d -> p (g d)"),
                          hT[:, 0].rearrange("p g c -> p (g c)"), start=True, stop=True).then_inc(s_cmp, 1)
                pe.wait_ge(s_cin, 1)
                for g in range(KVG):
                    last = pe.matmul(bank[6 + g][:, 0:HD], h4[:, g].rearrange("p h c -> p (h c)"), w2v[:], start=True, stop=True)
                last.then_inc(s_cmp, 1)
                pe.wait_ge(s_cin, 3)

                def scores(u):
                    i, b, h = HU[u]
                    g, c = h // HPG, h % HPG
                    r = slice(g * HD, (g + 1) * HD)
                    if u >= 2:
                        pe.wait_ge(s_mx, u - 1)
                    pe.matmul(bank[u % 2][:, 0:P * (i + 1)], qT[r, c, i * P:(i + 1) * P], kT[r, 2 + b, 0:P * (i + 1)],
                              start=True, stop=True).then_inc(s_sc, 1)

                def turn(u):
                    i = HU[u][0]
                    pe.wait_ge(s_ex, u + 1)
                    if u >= 2:
                        pe.wait_ge(s_pt, u - 1)
                    for k in range(i + 1):
                        last = pe.transpose(bank[2 + u % 2][:, k * P:(k + 1) * P], pr[:, u % 3, k * P:(k + 1) * P], ident[:])
                    last.then_inc(s_tp, 1)

                def weigh(u):
                    i, b, h = HU[u]
                    g = h // HPG
                    pe.wait_ge(s_pt, u + 1)
                    if h == 0 and i:
                        pe.wait_ge(s_comb, i)
                    for k in range(i + 1):
                        last = pe.matmul(bank[4 + b][:, h * HD:(h + 1) * HD], pT[:, u % 2, k * P:(k + 1) * P],
                                         vN[:, k, b * P + g * HD:b * P + (g + 1) * HD], start=k == 0, stop=k == i)
                    last.then_inc(s_pv, 1)

                def cmp_scores(i):
                    if i:
                        pe.wait_ge(s_nT, i)
                        pe.wait_ge(s_comb, i)
                    for g in range(KVG):
                        r = slice(g * HD, (g + 1) * HD)
                        for c in range(HPG):
                            last = pe.matmul(bank[6 + g][:, c * NC32:(c + 1) * NC32], qT[r, c, i * P:(i + 1) * P],
                                             kcmp[r, :], start=True, stop=True)
                        last.then_inc(s_scc, 1)

                def cmp_turn(i):
                    pe.wait_ge(s_pc, i + 1)
                    for g in range(KVG):
                        last = pe.transpose(bank[6][:, g * P:(g + 1) * P],
                                            p_c[:, g * HPG:(g + 1) * HPG].rearrange("p h c -> p (h c)"), ident[:])
                    last.then_inc(s_tpc, 1)

                def cmp_weigh(i):
                    pe.wait_ge(s_ptc, i + 1)
                    for g in range(KVG):
                        last = pe.matmul(bank[7][:, g * 256:(g + 1) * 256], pTc[:, g, :],
                                         vbd[:, g].rearrange("p h d -> p (h d)"), start=True, stop=True)
                    last.then_inc(s_oc, 1)

                def tile_turn(i):
                    pe.wait_ge(s_comb, i + 1)
                    for c in range(CH):
                        last = pe.transpose(bank[6][:, c * P:(c + 1) * P],
                                            acc[:, 2 * c:2 * c + 2].rearrange("p h d -> p (h d)"), ident[:])
                    last.then_inc(s_nt, 1)

                scores(0)
                scores(1)
                for u, (i, b, h) in enumerate(HU):
                    turn(u)
                    if u + 2 < len(HU):
                        scores(u + 2)
                    if u >= 1:
                        weigh(u - 1)
                    at = u % PT_
                    if at == AT_TURN and i:
                        tile_turn(i - 1)
                    if at == AT_CS:
                        cmp_scores(i)
                    if at == AT_CT:
                        cmp_turn(i)
                    if at == AT_CW:
                        cmp_weigh(i)
                weigh(len(HU) - 1)
                tile_turn(TT - 1)

            @block.vector
            def _(dve):
                link = chained(dve, s_v3)
                dve.wait_ge(s_pe3, 1)
                link(dve.tensor_copy(peT[:], bank[4][:, 0:2 * CB].rearrange("p (n l) -> p n l", n=2)))
                dve.wait_ge(s_tab, 9)
                for n in range(2):
                    v = kT[:, n, :].rearrange("p (c s) -> p s c", s=CS)
                    for m in range(2):
                        pb = peT[:, n, m * CS:(m + 1) * CS].unsqueeze(2).broadcast_to([P, CS, NCMP])
                        last = dve.tensor_tensor(blk[:, n, m * CS:(m + 1) * CS, 0:NCMP], v[:, :, m:m + NCMP], pb, ALU.add)
                        link(last)
                    dve.sem_inc(s_blk, 1)
                dve.wait_ge(s_hT, 4)
                for g in range(KVG):
                    last = dve.tensor_copy(h4[:, g], hT[:, 1, g].unsqueeze(1).broadcast_to([P, HPG, NC32]))
                last.then_inc(s_cin, 1)
                dve.wait_ge(s_cmp, 1)
                for g in range(KVG):
                    r = slice(g * HD, (g + 1) * HD)
                    last = dve.tensor_copy(kcmp[r, :], bank[5][r, g * NC32:(g + 1) * NC32])
                last.then_inc(s_cin, 1)
                dve.wait_ge(s_cmp, 2)
                for g in range(KVG):
                    for h in range(HPG):
                        r = slice(h * NC32, (h + 1) * NC32)
                        last = dve.tensor_copy(vbd[r, g, h, :], bank[6 + g][r, 0:HD])
                last.then_inc(s_cin, 1)
                dve.wait_ge(s_gt, 1)

                def combine(i):
                    dve.wait_ge(s_pv, PT_ * (i + 1))
                    dve.wait_ge(s_oc, i + 1)
                    if i:
                        dve.wait_ge(s_nt, i)
                    link(dve.reciprocal(coef[:], den[:, i % 2]))
                    link(dve.tensor_tensor(coef[:], coef[:], gate[:, i].rearrange("p (h b) -> p b h", b=3), ALU.mult))
                    by = lambda n: coef[:, n, :].unsqueeze(2).broadcast_to([P, HEADS, HD])
                    o = lambda n: bank[n][:].rearrange("p (h d) -> p h d", d=HD)
                    link(dve.tensor_tensor(acc[:], o(7), by(0), ALU.mult))
                    for n in (4, 5):
                        link(dve.tensor_tensor(tmp3[:], o(n), by(n - 3), ALU.mult))
                        link(dve.tensor_tensor(acc[:], acc[:], tmp3[:], ALU.add))
                    dve.sem_inc(s_comb, 1)

                def take(i):
                    dve.wait_ge(s_nt, i + 1)
                    dve.tensor_copy(nsaT[:, :, i * P:(i + 1) * P], bank[6][:].rearrange("p (c t) -> p c t", c=CH)).then_inc(s_nT, 1)

                for u, (i, b, h) in enumerate(HU):
                    o, L = u % 3, P * (i + 1)
                    dve.wait_ge(s_sc, u + 1)
                    if u >= 3:
                        dve.wait_ge(s_ex, u - 2)
                    link(dve.scalar_tensor_tensor(sc[:, o, 0:L], dist[:, S - L:S], slopes[:, h:h + 1], bank[u % 2][:, 0:L],
                                                  ALU.mult, ALU.add))
                    dve.tensor_reduce(nmx[:, o:o + 1], sc[:, o, 0:L], AX.X, ALU.max, negate=True).then_inc(s_mx, 1)
                    at = u % PT_
                    if at == AT_COMBINE and i:
                        combine(i - 1)
                    if at == AT_TURNED and i:
                        take(i - 1)
                    if at == AT_CX:
                        dve.wait_ge(s_scc, 2 * (i + 1))
                        if i:
                            dve.wait_ge(s_tpc, i)
                        link(dve.tensor_tensor(sc_c[:], distc[:, i].unsqueeze(1).broadcast_to([P, HEADS, NC32]),
                                               slopes[:].unsqueeze(2).broadcast_to([P, HEADS, NC32]), ALU.mult))
                        for g in range(KVG):
                            hs = slice(g * HPG, (g + 1) * HPG)
                            last = dve.tensor_tensor(sc_c[:, hs], sc_c[:, hs],
                                                     bank[6 + g][:, 0:P].rearrange("p (h c) -> p h c", c=NC32), ALU.add)
                            link(last)
                        link(dve.tensor_reduce(mx_c[:], sc_c[:], AX.X, ALU.max))
                        dve.tensor_tensor(sc_c[:], sc_c[:], mx_c[:].unsqueeze(2).broadcast_to([P, HEADS, NC32]),
                                          ALU.subtract).then_inc(s_mxc, 1)
                    if at == AT_CM:
                        dve.wait_ge(s_exc, i + 1)
                        link(dve.tensor_tensor(p_c[:], p_c[:], maskc[:, i].unsqueeze(1).broadcast_to([P, HEADS, NC32]), ALU.mult))
                        dve.sem_inc(s_pc, 1)
                        link(dve.tensor_reduce(den[:, i % 2, 0], p_c[:], AX.X, ALU.add))
                        link(dve.tensor_scalar(den[:, i % 2, 0], den[:, i % 2, 0], 1e-30, None, ALU.max))
                    if at == AT_CP:
                        dve.wait_ge(s_tpc, i + 1)
                        dve.tensor_copy(pTc[:], bank[6][:, 0:2 * P].rearrange("p (g t) -> p g t", g=2)).then_inc(s_ptc, 1)
                combine(TT - 1)
                take(TT - 1)

        def row(name, n0, n1):
            return spread(l0(name)[n0:n1], n1 - n0)

        p4 = ExitStack()
        wu = sb("wu", [P, 2, CH, D], on=p4)
        wo = sb("wo", [P, KD, D], on=p4)
        xr2 = sb("xr2", [P, TT, D], on=p4)
        ln1 = sb("ln1", [P, 2, D], on=p4)
        mt = sb("mt", [P, 2, S], on=p4)
        st = sb("st", [P, 2, 6], on=p4)
        mv = sb("mv", [P, TT, 2], on=p4)
        rs = sb("rs", [P, TT], on=p4)
        p4.close()

        s_wu = sem("w_up_loaded")
        s_wo = sem("w_out_loaded")
        s_x2 = sem("x_loaded_again")
        s_up = sem("chunks_projected_up")
        s_mix = sem("chunks_merged")
        s_o = sem("halves_projected_out")
        s_res = sem("halves_added")
        s_var = sem("variances")
        s_std = sem("deviations")
        s_x1 = sem("x1_tiles")
        s_xt = sem("x1_turned")
        s_xT = sem("x1T_in_place")
        s_v4 = sem("dve_steps_4")

        with nc.Block() as block:
            @block.sync
            def _(sp):
                for n, name in enumerate(("w_up_ssm", "w_up_nsa")):
                    sp.dma_start(wu[:, n], l0(name).rearrange("(k p) n -> p k n", p=P)).then_inc(s_wu, 16)
                sp.dma_start(wo[:], l0("w_out").rearrange("(k p) n -> p k n", p=P)).then_inc(s_wo, 16)
                sp.dma_start(xr2[:], a["x"][0].rearrange("(t p) d -> p t d", p=P)).then_inc(s_x2, 16)
                sp.dma_start(ln1[:, 0, :], row("ln1_g", 0, D)).then_inc(s_x2, 16)
                sp.dma_start(ln1[:, 1, :], row("ln1_b", 0, D)).then_inc(s_x2, 16)

            @block.tensor
            def _(pe):
                pe.wait_ge(s_wu, 32)
                for c in range(KD):
                    if c >= 2:
                        pe.wait_ge(s_mix, c - 1)
                    for n, y in enumerate((gluT, nsaT)):
                        for k in range(CH):
                            last = pe.matmul(bank[2 * (c % 2) + n][:], wu[:, n, k, c * P:(c + 1) * P], y[:, k, :],
                                             start=k == 0, stop=k == CH - 1)
                    last.then_inc(s_up, 1)
                pe.wait_ge(s_wo, 16)
                pe.wait_ge(s_mix, KD)
                for t in range(TT):
                    for n in range(2):
                        m = 2 * t + n
                        if m >= 4:
                            pe.wait_ge(s_res, m - 3)
                        for k in range(KD):
                            last = pe.matmul(bank[4 + m % 4][:], gmT[:, k, t * P:(t + 1) * P], wo[:, k, n * 512:(n + 1) * 512],
                                             start=k == 0, stop=k == KD - 1)
                        last.then_inc(s_o, 1)
                for t in range(TT):
                    pe.wait_ge(s_x1, t + 1)
                    for n in range(2):
                        m = 2 * t + n
                        if m >= 4:
                            pe.wait_ge(s_xT, m - 3)
                        for k in range(4):
                            last = pe.transpose(bank[m % 4][:, k * P:(k + 1) * P], x1[:, t, (4 * n + k) * P:(4 * n + k + 1) * P], ident[:])
                        last.then_inc(s_xt, 1)

            @block.scalar
            def _(act):
                for t in range(TT):
                    act.wait_ge(s_var, t + 1)
                    act.activation(rs[:, t:t + 1], mv[:, t, 1:2], ACT.Sqrt).then_inc(s_std, 1)
                for m in range(2 * TT):
                    t, n = m // 2, m % 2
                    act.wait_ge(s_xt, m + 1)
                    act.activation(x1T[:, 4 * n:4 * n + 4, t * P:(t + 1) * P],
                                   bank[m % 4][:].rearrange("p (k t) -> p k t", k=4), ACT.Copy).then_inc(s_xT, 1)

            @block.vector
            def _(dve):
                link = chained(dve, s_v4)
                for c in range(KD):
                    dve.wait_ge(s_up, c + 1)
                    b = 2 * (c % 2)
                    dve.tensor_tensor(mt[:, 0], bank[b][:], gmT[:, c, :], ALU.mult)
                    link(dve.tensor_tensor(mt[:, 1], bank[b + 1][:], gmT[:, KD + c, :], ALU.mult))
                    link(dve.tensor_tensor(gmT[:, c, :], mt[:, 0], mt[:, 1], ALU.add))
                    dve.sem_inc(s_mix, 1)
                dve.wait_ge(s_x2, 48)
                for t in range(TT):
                    for n in range(2):
                        h = slice(n * 512, (n + 1) * 512)
                        dve.wait_ge(s_o, 2 * t + n + 1)
                        link(dve.scalar_tensor_tensor(x1[:, t, h], xr2[:, t, h], DN_ALPHA, bank[4 + (2 * t + n) % 4][:], ALU.mult, ALU.add))
                        dve.sem_inc(s_res, 1)
                        link(dve.bn_stats(st[:, n, :], x1[:, t, h]))
                    link(dve.bn_aggr(mv[:, t, :], st[:].rearrange("p n s -> p (n s)")))
                    dve.tensor_scalar(mv[:, t, 1:2], mv[:, t, 1:2], LN_EPS, None, ALU.add).then_inc(s_var, 1)
                    dve.wait_ge(s_std, t + 1)
                    link(dve.reciprocal(rs[:, t:t + 1], rs[:, t:t + 1]))
                    link(dve.tensor_scalar(x1[:, t, :], x1[:, t, :], mv[:, t, 0:1], rs[:, t:t + 1], ALU.subtract, ALU.mult))
                    link(dve.tensor_tensor(x1[:, t, :], x1[:, t, :], ln1[:, 0, :], ALU.mult))
                    dve.tensor_tensor(x1[:, t, :], x1[:, t, :], ln1[:, 1, :], ALU.add).then_inc(s_x1, 1)

        early.close()

        p5 = ExitStack()
        qp = sb("qp", [P, PH, S], on=p5)
        skT = sb("skT", [P, PH, PK], on=p5)
        p5a = ExitStack()
        wq = sb("wq", [P, KD, D], on=p5a)
        sk = sb("sk", [P, 2 * PH, HD], on=p5a)
        p5a.close()

        s_wq = sem("w_q_loaded")
        s_sk = sem("subkeys_loaded")
        s_skt = sem("subkeys_turned")
        s_skT = sem("subkeys_in_place")
        s_qp = sem("peer_queries")
        s_qpd = sem("peer_queries_in_place")

        with nc.Block() as block:
            @block.sync
            def _(sp):
                sp.dma_start(sk[:], l0("peer_subkeys").rearrange("h c k d -> k (h c) d")).then_inc(s_sk, 16)
                for k in range(KD):
                    sp.dma_start(wq[:, k, :], l0("peer_w_q")[k * P:(k + 1) * P, :]).then_inc(s_wq, 16)

            @block.tensor
            def _(pe):
                pe.wait_ge(s_sk, 16)
                for n in range(2):
                    for h in range(4):
                        last = pe.transpose(bank[n][:, h * P:(h + 1) * P],
                                            sk[:, 2 * (4 * n + h):2 * (4 * n + h) + 2].rearrange("p c d -> p (c d)"), ident[:])
                    last.then_inc(s_skt, 1)
                pe.wait_ge(s_wq, 16 * KD)
                for h in range(PH):
                    if h >= 4:
                        pe.wait_ge(s_qpd, h - 3)
                    for k in range(KD):
                        last = pe.matmul(bank[2 + h % 4][:], wq[:, k, h * P:(h + 1) * P], x1T[:, k, :],
                                         start=k == 0, stop=k == KD - 1)
                    last.then_inc(s_qp, 1)

            @block.scalar
            def _(act):
                for h in range(PH):
                    act.wait_ge(s_qp, h + 1)
                    act.activation(qp[:, h, :], bank[2 + h % 4][:], ACT.Copy).then_inc(s_qpd, 1)

            @block.vector
            def _(dve):
                for n in range(2):
                    dve.wait_ge(s_skt, n + 1)
                    dve.tensor_copy(skT[:, 4 * n:4 * n + 4, :], bank[n][:].rearrange("p (h k) -> p h k", h=4)).then_inc(s_skT, 1)

        LISTS = 2 * PH
        TB8 = 8
        STEPS = P // TB8
        gates = nc.dram_tensor("gates", [TT, P, P, P], F32, kind="Internal").ap()
        p6 = ExitStack()
        ss = sb("ss", [P, LISTS, PK], on=p6)
        sv = sb("sv", [P, LISTS, PE_TOP], on=p6)
        si = sb("si", [P, LISTS, PE_TOP], U32, on=p6)
        sif = sb("sif", [P, LISTS, PE_TOP], on=p6)
        cand = sb("cand", [P, PH, PE_TOP * PE_TOP], on=p6)
        best = sb("best", [P, PH, PE_TOP], on=p6)
        pos = sb("pos", [P, PH, PE_TOP], U32, on=p6)
        pab = sb("pab", [P, 2, PH, PE_TOP], U32, on=p6)
        pabf = sb("pabf", [P, 2, PH, PE_TOP], on=p6)
        eq = sb("eq", [P, PH * PE_TOP, PE_TOP], on=p6)
        picks = sb("picks", [P, 3, PH, PE_TOP], on=p6)
        gs = sb("gs", [P, 2, PH], on=p6)
        pkT = sb("pkT", [P, 2, 3, P], on=p6)
        iota = sb("iota", [P, P], on=p6)
        oh = sb("oh", [P, 2, TB8, P], on=p6)
        ohj = sb("ohj", [P, 2, TB8, P], on=p6)
        ohg = sb("ohg", [P, 2, TB8, P], on=p6)
        stg = sb("stg", [P, P, P], on=p6)
        p6.close()
        p5.close()

        s_io = sem("counters_made")
        s_ss = sem("peer_scores")
        s_ssd = sem("peer_scores_in_place")
        s_v6 = sem("dve_steps_6")
        s_dif = sem("best_less_maximum")
        s_gex = sem("gate_exponentials")
        s_pk = sem("picks_made")
        s_pkt = sem("picks_turned")
        s_pkT = sem("picks_in_place")
        s_hot = sem("one_hots")
        s_hotg = sem("gated_one_hots")
        s_gp = sem("gates_multiplied")
        s_ge = sem("gates_staged")
        s_gw = sem("gates_stored")

        with nc.Block() as block:
            @block.sync
            def _(sp):
                for t in range(TT):
                    sp.wait_ge(s_ge, 2 + STEPS * (t + 1))
                    sp.dma_start(gates[t].rearrange("i j t -> i (j t)"), stg[:].rearrange("p j t -> p (j t)")).then_inc(s_gw, 16)
                sp.wait_ge(s_gw, 16 * TT)

            @block.gpsimd
            def _(pool):
                pool.iota(iota[:], [[1, P]], base=0, channel_multiplier=0, allow_small_or_imprecise_dtypes=True).then_inc(s_io, 1)
                pool.sem_inc(s_hotg, 2)
                for t in range(TT):
                    pool.wait_ge(s_pkT, t + 1)
                    with pool.Fori(0, STEPS // 2) as i:
                        for o in range(2):
                            n = STEPS * t + 2 * i + o
                            pool.wait_ge(s_hot, 2 * n + 2)
                            pool.wait_ge(s_gp, n + 1)
                            g = pkT[:, t % 2, 2, bass.ds((2 * i + o) * TB8, TB8)]
                            pool.tensor_tensor(ohg[:, o], ohj[:, o], g.unsqueeze(2).broadcast_to([P, TB8, P]),
                                               ALU.mult).then_inc(s_hotg, 1)

            @block.scalar
            def _(act):
                act.sem_inc(s_ge, 2)

                def make(t):
                    for n in range(4):
                        act.wait_ge(s_ss, 4 * t + n + 1)
                        if t:
                            act.wait_ge(s_pk, t)
                        act.activation(ss[:, 4 * n:4 * n + 4, :], bank[n][:].rearrange("p (h k) -> p h k", h=4), ACT.Copy).then_inc(s_ssd, 1)
                    act.wait_ge(s_dif, t + 1)
                    act.activation(picks[:, 2], picks[:, 2], ACT.Exp).then_inc(s_gex, 1)

                make(0)
                for t in range(TT):
                    if t:
                        act.wait_ge(s_gw, 16 * t)
                    with act.Fori(0, STEPS // 2) as i:
                        for o in range(2):
                            n = STEPS * t + 2 * i + o
                            act.wait_ge(s_gp, 2 + n + 1)
                            for m in range(2):
                                dst = stg[:, :, bass.ds((2 * i + o) * TB8 + 4 * m, 4)].rearrange("p j t -> p t j")
                                last = act.activation(dst, bank[4 + 2 * o + m][:].rearrange("p (t j) -> p t j", t=4), ACT.Copy)
                            last.then_inc(s_ge, 1)
                    if t + 1 < TT:
                        make(t + 1)

            @block.tensor
            def _(pe):
                pe.sem_inc(s_gp, 2)

                def scores(t):
                    for n in range(4):
                        c = n // 2
                        if t:
                            pe.wait_ge(s_ssd, 4 * (t - 1) + n + 1)
                            if n == 0:
                                pe.wait_ge(s_pkT, t)
                        for h in range(4):
                            hh = 4 * (n % 2) + h
                            last = pe.matmul(bank[n][:, h * PK:(h + 1) * PK], qp[c * HD:(c + 1) * HD, hh, t * P:(t + 1) * P],
                                             skT[c * HD:(c + 1) * HD, hh, :], start=True, stop=True)
                        last.then_inc(s_ss, 1)

                def turn(t):
                    pe.wait_ge(s_pk, t + 1)
                    for n in range(3):
                        last = pe.transpose(bank[0][:, n * P:(n + 1) * P], picks[:, n].rearrange("p h k -> p (h k)"), ident[:])
                    last.then_inc(s_pkt, 1)

                scores(0)
                turn(0)
                for t in range(TT):
                    pe.wait_ge(s_pkT, t + 1)
                    if t + 1 < TT:
                        scores(t + 1)
                    with pe.Fori(0, STEPS // 2) as i:
                        for o in range(2):
                            n = STEPS * t + 2 * i + o
                            pe.wait_ge(s_hotg, 2 + n + 1)
                            pe.wait_ge(s_ge, n + 1)
                            for m in range(TB8):
                                last = pe.matmul(bank[4 + 2 * o + m // 4][:, (m % 4) * P:(m % 4 + 1) * P], oh[:, o, m, :],
                                                 ohg[:, o, m, :], start=True, stop=True)
                            last.then_inc(s_gp, 1)
                    if t + 1 < TT:
                        turn(t + 1)

            @block.vector
            def _(dve):
                link = chained(dve, s_v6)
                LOW = -3.0e38

                def top16(vals, idx, lst):
                    link(dve.max(vals[:, 0:8], lst))
                    dve.max_index(idx[:, 0:8], vals[:, 0:8], lst)
                    link(dve.match_replace(lst, vals[:, 0:8], lst, LOW))
                    link(dve.max(vals[:, 8:16], lst))
                    link(dve.max_index(idx[:, 8:16], vals[:, 8:16], lst))

                def pick(t):
                    for n in range(4):
                        dve.wait_ge(s_ssd, 4 * t + n + 1)
                        for l in range(4 * n, 4 * n + 4):
                            top16(sv[:, l, :], si[:, l, :], ss[:, l, :])
                    link(dve.tensor_copy(sif[:], si[:]))
                    link(dve.tensor_tensor(cand[:].rearrange("p h (a b) -> p h a b", a=PE_TOP),
                                           sv[:, 0:PH].unsqueeze(3).broadcast_to([P, PH, PE_TOP, PE_TOP]),
                                           sv[:, PH:].unsqueeze(2).broadcast_to([P, PH, PE_TOP, PE_TOP]), ALU.add))
                    for h in range(PH):
                        top16(best[:, h, :], pos[:, h, :], cand[:, h, :])
                    link(dve.tensor_scalar(pab[:, 0], pos[:], 4, None, ALU.logical_shift_right))
                    link(dve.tensor_scalar(pab[:, 1], pos[:], 15, None, ALU.bitwise_and))
                    link(dve.tensor_copy(pabf[:], pab[:]))
                    if t:
                        dve.wait_ge(s_pkt, t)
                    e4 = eq[:].rearrange("p (h k) a -> p h k a", h=PH)
                    for c in range(2):
                        link(dve.tensor_tensor(eq[:], pabf[:, c].rearrange("p h k -> p (h k)").unsqueeze(2).broadcast_to([P, PH * PE_TOP, PE_TOP]),
                                               iota[:, 0:PE_TOP].unsqueeze(1).broadcast_to([P, PH * PE_TOP, PE_TOP]), ALU.is_equal))
                        link(dve.tensor_tensor(e4, e4, sif[:, c * PH:(c + 1) * PH].unsqueeze(2).broadcast_to([P, PH, PE_TOP, PE_TOP]), ALU.mult))
                        link(dve.tensor_reduce(picks[:, c].rearrange("p h k -> p (h k)"), eq[:], AX.X, ALU.add))
                    link(dve.tensor_tensor(picks[:, 2], best[:], best[:, :, 0:1].broadcast_to([P, PH, PE_TOP]), ALU.subtract))
                    dve.sem_inc(s_dif, 1)
                    dve.wait_ge(s_gex, t + 1)
                    link(dve.tensor_reduce(gs[:, 0], picks[:, 2], AX.X, ALU.add))
                    link(dve.reciprocal(gs[:, 1], gs[:, 0]))
                    link(dve.tensor_tensor(picks[:, 2], picks[:, 2], gs[:, 1].unsqueeze(2).broadcast_to([P, PH, PE_TOP]), ALU.mult))
                    dve.sem_inc(s_pk, 1)
                    dve.wait_ge(s_pkt, t + 1)
                    if t >= 2:
                        dve.wait_ge(s_hotg, 2 + STEPS * (t - 1))
                    dve.tensor_copy(pkT[:, t % 2], bank[0][:, 0:3 * P].rearrange("p (n t) -> p n t", n=3)).then_inc(s_pkT, 1)
                    dve.wait_ge(s_pkT, t + 1)

                dve.wait_ge(s_io, 1)
                pick(0)
                for t in range(TT):
                    with dve.Fori(0, STEPS // 2) as i:
                        for o in range(2):
                            n = STEPS * t + 2 * i + o
                            at = bass.ds((2 * i + o) * TB8, TB8)
                            row3 = iota[:].unsqueeze(1).broadcast_to([P, TB8, P])
                            dve.wait_ge(s_gp, n + 1)
                            dve.tensor_tensor(oh[:, o], row3, pkT[:, t % 2, 0, at].unsqueeze(2).broadcast_to([P, TB8, P]),
                                              ALU.is_equal).then_inc(s_hot, 1)
                            dve.wait_ge(s_hotg, n + 1)
                            dve.tensor_tensor(ohj[:, o], row3, pkT[:, t % 2, 1, at].unsqueeze(2).broadcast_to([P, TB8, P]),
                                              ALU.is_equal).then_inc(s_hot, 1)
                    if t + 1 < TT:
                        pick(t + 1)

        JG = 4
        NG = PK // JG
        p7 = ExitStack()
        ub = sb("ub", [P, 2, JG, D], on=p7)
        vb = sb("vb", [P, 2, JG, D], on=p7)
        gb = sb("gb", [P, 2, TT, JG, P], on=p7)
        uTb = sb("uTb", [P, 2, KD, P], on=p7)
        hb = sb("hb", [P, 2, S], on=p7)
        wb = sb("wb", [P, 2, JG, S], on=p7)
        p7.close()

        s_u = [sem(f"u_loaded{n}") for n in range(2)]
        s_v = [sem(f"v_loaded{n}") for n in range(2)]
        s_g = [sem(f"gates_loaded{n}") for n in range(2)]
        s_t = sem("experts_turned")
        s_ua = sem("turned_taken_by_act")
        s_ud = sem("turned_taken_by_dve")
        s_h = sem("experts_multiplied")
        s_hr = sem("experts_gelu")
        s_wt = sem("experts_weighed")
        s_y = sem("sums_made")
        s_ya = sem("sums_added")
        s_sc7 = sem("residual_scaled")
        ug = l0("peer_u").rearrange("(i g j) d -> g i (j d)", i=P, j=JG)
        vg = l0("peer_v").rearrange("(i g j) d -> g i (j d)", i=P, j=JG)
        gg = gates.rearrange("t i (g j) k -> g i t (j k)", j=JG)

        with nc.Block() as block:
            @block.sync
            def _(sp):
                def load_u(g, o):
                    sp.dma_start(ub[:, o].rearrange("p j d -> p (j d)"), ug[g]).then_inc(s_u[o], 16)

                def load_g(g, o):
                    sp.dma_start(gb[:, o].rearrange("p t j k -> p t (j k)"), gg[g]).then_inc(s_g[o], 16)

                def load_v(g, o):
                    sp.dma_start(vb[:, o].rearrange("p j d -> p (j d)"), vg[g]).then_inc(s_v[o], 16)

                for g in range(2):
                    load_u(g, g)
                    load_g(g, g)
                    load_v(g, g)
                with sp.Fori(0, NG // 2 - 1) as i:
                    for o in range(2):
                        g = 2 * i + o
                        sp.wait_ge(s_t, JG * g + JG)
                        load_u(g + 2, o)
                        sp.wait_ge(s_wt, JG * g + JG + 2)
                        load_g(g + 2, o)
                        sp.wait_ge(s_y, 8 * g + 24)
                        load_v(g + 2, o)

            @block.tensor
            def _(pe):
                pe.sem_inc(s_h, 2)
                pe.sem_inc(s_y, 16)

                def turn(g, half, o, j):
                    n = JG * g + j
                    if j == 0:
                        pe.wait_ge(s_u[o], 16 * half + 16)
                    pe.wait_ge(s_ua, n)
                    pe.wait_ge(s_ud, n)
                    for k in range(KD):
                        last = pe.transpose(bank[k // 4][:, (k % 4) * P:(k % 4 + 1) * P], ub[:, o, j, k * P:(k + 1) * P], ident[:])
                    last.then_inc(s_t, 1)

                def group(g, half, o, last_group=False):
                    for j in range(JG):
                        n = JG * g + j
                        if j + 1 < JG:
                            turn(g, half, o, j + 1)
                        elif not last_group:
                            turn(g + 1, half + o, 1 - o, 0)
                        pe.wait_ge(s_ua, n + 1)
                        pe.wait_ge(s_ud, n + 1)
                        pe.wait_ge(s_hr, n + 1)
                        for k in range(KD):
                            last = pe.matmul(bank[2 + j % 2][:], uTb[:, j % 2, k, :], x1T[:, k, :], start=k == 0, stop=k == KD - 1)
                        last.then_inc(s_h, 1)
                    pe.wait_ge(s_v[o], 16 * half + 16)
                    for m in range(8):
                        t, c = m // 2, m % 2
                        pe.wait_ge(s_ya, 8 * g + m + 1)
                        for j in range(JG):
                            if m == 0:
                                pe.wait_ge(s_wt, JG * g + j + 3)
                            last = pe.matmul(bank[4 + m % 4][:], wb[:, o, j, t * P:(t + 1) * P], vb[:, o, j, c * 512:(c + 1) * 512],
                                             start=j == 0, stop=j == JG - 1)
                        last.then_inc(s_y, 1)

                turn(0, 0, 0, 0)
                with pe.Fori(0, NG // 2 - 1) as i:
                    group(2 * i, i, 0)
                    group(2 * i + 1, i, 1)
                group(NG - 2, NG // 2 - 1, 0)
                group(NG - 1, NG // 2 - 1, 1, last_group=True)

            @block.scalar
            def _(act):
                act.sem_inc(s_hr, 2)

                def take(n, o):
                    act.wait_ge(s_t, n + 1)
                    act.wait_ge(s_h, n + 1)
                    act.activation(uTb[:, o, 0:4, :], bank[0][:].rearrange("p (k i) -> p k i", k=4), ACT.Copy).then_inc(s_ua, 1)

                def tile(n, j, last=False):
                    if not last:
                        take(n + 1, (j + 1) % 2)
                    act.wait_ge(s_h, n + 3)
                    act.wait_ge(s_wt, n + 1)
                    act.activation(hb[:, j % 2, :], bank[2 + j % 2][:], ACT.Gelu_apprx_tanh).then_inc(s_hr, 1)

                take(0, 0)
                with act.Fori(0, NG - 1) as g:
                    for j in range(JG):
                        tile(JG * g + j, j)
                for j in range(JG):
                    tile(PK - JG + j, j, last=j == JG - 1)

            @block.vector
            def _(dve):
                dve.sem_inc(s_wt, 2)
                dve.tensor_scalar(x1[:], x1[:], DN_ALPHA, None, ALU.mult).then_inc(s_sc7, 1)
                dve.wait_ge(s_sc7, 1)
                dve.sem_inc(s_ya, 4)

                def take(n, o):
                    dve.wait_ge(s_t, n + 1)
                    dve.wait_ge(s_h, n + 1)
                    dve.tensor_copy(uTb[:, o, 4:8, :], bank[1][:].rearrange("p (k i) -> p k i", k=4)).then_inc(s_ud, 1)

                def group(g, half, o, last_group=False):
                    for j in range(JG):
                        n = JG * g + j
                        if not (last_group and j == JG - 1):
                            take(n + 1, (j + 1) % 2)
                        if j == 0:
                            dve.wait_ge(s_g[o], 16 * half + 16)
                            dve.wait_ge(s_y, 8 * g + 8)
                        dve.wait_ge(s_hr, n + 3)
                        dve.tensor_tensor(wb[:, o, j, :].rearrange("p (t k) -> p t k", t=TT),
                                          hb[:, j % 2, :].rearrange("p (t k) -> p t k", t=TT), gb[:, o, :, j, :],
                                          ALU.mult).then_inc(s_wt, 1)
                    dve.wait_ge(s_ya, 8 * g + 4)
                    for m in range(8):
                        t, c = m // 2, m % 2
                        dve.wait_ge(s_y, 8 * g + m + 17)
                        h = slice(c * 512, (c + 1) * 512)
                        dve.tensor_tensor(x1[:, t, h], x1[:, t, h], bank[4 + m % 4][:], ALU.add).then_inc(s_ya, 1)

                take(0, 0)
                with dve.Fori(0, NG // 2 - 1) as i:
                    group(2 * i, i, 0)
                    group(2 * i + 1, i, 1)
                group(NG - 2, NG // 2 - 1, 0)
                group(NG - 1, NG // 2 - 1, 1, last_group=True)

        p8 = ExitStack()
        ln2 = sb("ln2", [P, 2, D], on=p8)
        st8 = sb("st8", [P, TT, 2, 6], on=p8)
        mv8 = sb("mv8", [P, TT, 2], on=p8)
        rs8 = sb("rs8", [P, TT], on=p8)
        p8.close()

        s_ln = sem("ln2_loaded")
        s_v8 = sem("dve_steps_8")
        s_var8 = sem("variances_8")
        s_std8 = sem("deviations_8")
        s_fin = sem("tiles_finished")
        s_out = sem("output_stored")

        with nc.Block() as block:
            @block.sync
            def _(sp):
                sp.dma_start(ln2[:, 0, :], row("ln2_g", 0, D)).then_inc(s_ln, 16)
                sp.dma_start(ln2[:, 1, :], row("ln2_b", 0, D)).then_inc(s_ln, 16)
                for t in range(TT):
                    sp.wait_ge(s_fin, t + 1)
                    sp.dma_start(out[0, t * P:(t + 1) * P, :], x1[:, t, :]).then_inc(s_out, 16)
                sp.wait_ge(s_out, 16 * TT)

            @block.scalar
            def _(act):
                act.wait_ge(s_var8, 1)
                act.activation(rs8[:], mv8[:, :, 1], ACT.Sqrt).then_inc(s_std8, 1)

            @block.vector
            def _(dve):
                link = chained(dve, s_v8)
                for t in range(TT):
                    for n in range(2):
                        last = dve.bn_stats(st8[:, t, n, :], x1[:, t, n * 512:(n + 1) * 512])
                    link(last)
                for t in range(TT):
                    last = dve.bn_aggr(mv8[:, t, :], st8[:, t].rearrange("p n s -> p (n s)"))
                link(last)
                dve.tensor_scalar(mv8[:, :, 1], mv8[:, :, 1], LN_EPS, None, ALU.add).then_inc(s_var8, 1)
                dve.wait_ge(s_std8, 1)
                link(dve.reciprocal(rs8[:], rs8[:]))
                dve.wait_ge(s_ln, 32)
                for t in range(TT):
                    link(dve.tensor_scalar(x1[:, t, :], x1[:, t, :], mv8[:, t, 0:1], rs8[:, t:t + 1], ALU.subtract, ALU.mult))
                    link(dve.tensor_tensor(x1[:, t, :], x1[:, t, :], ln2[:, 0, :], ALU.mult))
                    dve.tensor_tensor(x1[:, t, :], x1[:, t, :], ln2[:, 1, :], ALU.add).then_inc(s_fin, 1)


_INS = ['x', 'w_in', 'b_in', 'ssm_a_re', 'ssm_a_im', 'ssm_log_dt', 'ssm_b_re', 'ssm_b_im', 'ssm_c_re', 'ssm_c_im',
        'ssm_d', 'w_glu', 'w_up_ssm', 'nsa_pe_k', 'nsa_w1_k', 'nsa_w2_k', 'nsa_pe_v', 'nsa_w1_v', 'nsa_w2_v',
        'w_up_nsa', 'w_out', 'ln1_g', 'ln1_b', 'peer_w_q', 'peer_subkeys', 'peer_u', 'peer_v', 'ln2_g', 'ln2_b']


def kernel(**inputs):
    import numpy as _np
    import concourse.bacc as _bacc
    from concourse import mybir as _mybir
    from concourse.bass_utils import run_bass_kernel_spmd as _run

    nc = _bacc.Bacc("TRN2", target_bir_lowering=False, num_devices=1)
    arrays, args = {}, {}
    for name in _INS:
        v = _np.ascontiguousarray(inputs[name])
        arrays[f"in_{name}_dram"] = v
        args[name] = nc.dram_tensor(f"in_{name}_dram", v.shape, _mybir.dt.from_np(v.dtype), kind="ExternalInput").ap()
    out = nc.dram_tensor("out_0_dram", (1, S, D), F32, kind="ExternalOutput").ap()
    build(nc, args, out)
    r = _run(nc, [arrays], core_ids=[0])
    return r.results[0]["out_0_dram"]
```

```python
from contextlib import ExitStack
import math

import numpy as np

import concourse.bass as bass
from concourse import mybir

F32 = mybir.dt.float32
F32R = mybir.dt.float32r
U32 = mybir.dt.uint32
ALU = mybir.AluOpType
ACT = mybir.ActivationFunctionType
AX = mybir.AxisListType

P = 128
D = 1024
S = 512
KD = D // P
TT = S // P
SSM = D // 2
SG, SH, SP = 32, 16, 64
NPAIR = SG // 2
CH = SSM // P
HEADS, KVG, HD = 8, 2, 64
HPG = HEADS // KVG
CB, CS = 32, 16
NCMP = (S - CB) // CS + 1
NC32 = 32
GATES = 3 * HEADS
PH, PK, PE_TOP = 8, 128, 16
NEG = -1e30
DN_ALPHA = 2.0 ** 0.25
LN_EPS = 1e-5

C_U, C_Q = 0, SSM
C_KC = C_Q + SSM
C_VC, C_KS, C_VS, C_KW, C_VW, C_G = (C_KC + P * n for n in range(1, 7))
C_M = C_G + GATES
C_END = C_M + 2 * D
W_GROUPS = [(0, 512), (512, 1024), (1024, 1536), (1536, C_M)] + [(C_M + 512 * n, C_M + 512 * (n + 1)) for n in range(4)]
W_RING = 3
G_Q = 1
R_U, R_Q, R_KC, R_VC, R_KS, R_KW, R_M, R_D = 0, 4, 8, 9, 10, 11, 12, 28
PI2_A = 6.28125
PI2_B = float(np.round((2 * math.pi - PI2_A) * 2 ** 20) / 2 ** 20)
PI2_C = 2 * math.pi - PI2_A - PI2_B
ROUND = 1.5 * 2.0 ** 23

UNITS = (
    [("u", 0, P * c, c) for c in range(4)]
    + [("q", 1, P * c, c) for c in range(4)]
    + [("kc", 2, 0, 0), ("vc", 2, P, 0), ("ks", 2, 2 * P, 0), ("kw", 3, 0, 0)]
    + [("vg", 3, 0, t) for t in range(TT)]
    + [("m", 4 + c // 4, P * (c % 4), c) for c in range(16)]
)
BY_ACT = ("u", "m")
NX = 2 * TT


def build(nc: bass.Bass, a, out, dbg=None):
    l0 = lambda name: a[name][0]
    ctx = ExitStack()
    with ctx:
        def sb(name, shape, dt=F32, on=ctx):
            return on.enter_context(nc.sbuf_tensor(name, shape, dt))

        def sem(name):
            return ctx.enter_context(nc.semaphore(name))

        def spread(vec, n):
            return vec.rearrange("(a n) -> a n", a=1).broadcast_to([P, n])

        bank = [ctx.enter_context(nc.psum_tensor(f"bank{i}", [P, 512], F32)) for i in range(8)]

        def chained(eng, sem_):
            n = [0]

            def link(ins):
                n[0] += 1
                ins.then_inc(sem_, 1)
                eng.wait_ge(sem_, n[0])
            return link

        ident = sb("ident", [P, P])
        col = sb("col", [P, 32])
        x1 = sb("x1", [P, TT, D])
        qp = sb("qp", [P, PH, S])
        skT = sb("skT", [P, PH, PK])
        parts = ExitStack()
        xh = sb("xh", [P, KD, S], F32R, on=parts)
        xl = sb("xl", [P, KD, S], F32R, on=parts)
        parts.close()
        late = ExitStack()
        sb("places_below_w_q", [P, 2 * KD * S + 8 * S], on=late)
        wq = sb("wq", [P, KD, D], on=late)
        late.close()
        early = ExitStack()
        uT = sb("uT", [P, CH, S], on=early)
        qT = sb("qT", [P, 4, S], on=early)
        kT = sb("kT", [P, 4, S], on=early)
        vN = sb("vN", [P, TT, 2 * P + GATES], on=early)
        sb("rest_of_parts", [P, 2 * KD * S - 12 * S - TT * (2 * P + GATES)], on=early)
        gmT = sb("gmT", [P, 16, S], on=early)
        gluT = sb("gluT", [P, CH, S], on=early)
        nsaT = sb("nsaT", [P, CH, S], on=early)
        x1T = sb("x1T", [P, KD, S], on=early)

        p1 = ExitStack()
        xN = x1
        xT = sb("xT", [P, KD, S], on=p1)
        wr = sb("wr", [P, W_RING, KD, 512], on=p1)
        rows = sb("rows", [32, P], on=p1)
        vbias = sb("vbias", [P, 2 * P + GATES], on=p1)
        iota_d = sb("iota_d", [P, P], on=p1)
        p1.close()

        s_x = sem("x_loaded")
        s_rows = sem("rows_loaded")
        s_w = [sem(f"w_in_loaded{n}") for n in range(W_RING)]
        s_iota = sem("iota_made")
        s_id = sem("identity_made")
        s_unit = sem("units_made")
        s_act = sem("units_taken_by_act")
        s_dve = sem("units_taken_by_dve")
        s_v1 = sem("dve_steps_1")

        w_in, b_in = l0("w_in"), l0("b_in")
        taken = [("dve", 0)] * (NX + 1) + [("act" if k in BY_ACT else "dve", 0) for k, *_ in UNITS]
        nth = []
        seen = {"act": 0, "dve": 0}
        for e, _ in taken:
            seen[e] += 1
            nth.append((e, seen[e]))
        w_landed = [16 * sum(KD * KVG if h == G_Q else 1 for h in range(g % W_RING, g + 1, W_RING)) for g in range(len(W_GROUPS))]
        last_unit = {}
        for n, (_, g, _, _) in enumerate(UNITS):
            last_unit[g] = NX + 1 + n + 1
        last_unit[2] = last_unit[3]

        with nc.Block() as block:
            @block.sync
            def _(sp):
                for t in range(TT):
                    sp.dma_start(xN[:, t, :], a["x"][0, t * P:(t + 1) * P, :]).then_inc(s_x, 16)
                sp.dma_start(rows[R_U:R_U + 4, :], b_in[C_U:C_U + SSM].rearrange("(r c) -> r c", c=P)).then_inc(s_rows, 16)
                for g in range(KVG):
                    sp.dma_start(rows[R_Q:R_Q + 4, g * HD:(g + 1) * HD],
                                 b_in[C_Q + 256 * g:C_Q + 256 * (g + 1)].rearrange("(r c) -> r c", c=HD)).then_inc(s_rows, 16)
                for r, c, n in ((R_KC, C_KC, 3), (R_KW, C_KW, 1), (R_M, C_M, 16)):
                    sp.dma_start(rows[r:r + n, :], b_in[c:c + n * P].rearrange("(r c) -> r c", c=P)).then_inc(s_rows, 16)
                sp.dma_start(rows[R_D:R_D + 4, :], l0("ssm_d").rearrange("(r c) -> r c", c=P)).then_inc(s_rows, 16)
                sp.dma_start(vbias[:, 0:P], spread(b_in[C_VS:C_VS + P], P)).then_inc(s_rows, 16)
                sp.dma_start(vbias[:, P:], spread(b_in[C_VW:C_M], P + GATES)).then_inc(s_rows, 16)
                for g, (c0, c1) in enumerate(W_GROUPS):
                    if g >= W_RING:
                        sp.wait_ge(s_unit, last_unit[g - W_RING])
                    if g == G_Q:
                        for k in range(KD):
                            for j in range(KVG):
                                sp.dma_start(wr[:, g % W_RING, k].rearrange("p (r j d) -> p j r d", j=KVG, d=HD)[:, j],
                                             w_in[k * P:(k + 1) * P, c0 + 256 * j:c0 + 256 * (j + 1)]
                                             .rearrange("p (r d) -> p r d", d=HD)).then_inc(s_w[g % W_RING], 16)
                        continue
                    sp.dma_start(wr[:, g % W_RING, :, 0:c1 - c0],
                                 w_in[:, c0:c1].rearrange("(k p) c -> p k c", p=P)).then_inc(s_w[g % W_RING], 16)

            @block.gpsimd
            def _(pool):
                pool.iota(iota_d[:], [[1, P]], base=0, channel_multiplier=-1,
                          allow_small_or_imprecise_dtypes=True).then_inc(s_iota, 1)

            @block.tensor
            def _(pe):
                pe.wait_ge(s_id, 1)

                def free(n):
                    if n >= 8:
                        e, m = nth[n - 8]
                        pe.wait_ge(s_act if e == "act" else s_dve, m)
                for t in range(TT):
                    pe.wait_ge(s_x, 16 * (TT))
                    for h in range(2):
                        n = 2 * t + h
                        for k in range(4):
                            last = pe.transpose(bank[n][:, k * P:(k + 1) * P],
                                                xN[:, t, (4 * h + k) * P:(4 * h + k + 1) * P], ident[:])
                        last.then_inc(s_unit, 1)
                pe.wait_ge(s_rows, 16 * 9)
                free(NX)
                pe.transpose(bank[NX % 8][:, 0:32], rows[:], ident[0:32, 0:32]).then_inc(s_unit, 1)
                pe.wait_ge(s_dve, NX)
                for m, (kind, g, c0, i) in enumerate(UNITS):
                    n = NX + 1 + m
                    b = bank[n % 8]
                    pe.wait_ge(s_w[g % W_RING], w_landed[g])
                    free(n)
                    w = wr[:, g % W_RING]
                    for k in range(KD):
                        first, end = k == 0, k == KD - 1
                        if kind == "vg":
                            xt = xT[:, k, i * P:(i + 1) * P]
                            w2 = wr[:, 2 % W_RING, k, 3 * P:4 * P]
                            pe.matmul(b[:, 0:P], xt, w2, start=first, stop=end)
                        else:
                            last = pe.matmul(b[:], w[:, k, c0:c0 + P], xT[:, k, :], start=first, stop=end)
                    if kind == "vg":
                        for k in range(KD):
                            xt = xT[:, k, i * P:(i + 1) * P]
                            last = pe.matmul(b[:, P:2 * P + GATES], xt, w[:, k, P:2 * P + GATES],
                                             start=k == 0, stop=k == KD - 1)
                    last.then_inc(s_unit, 1)

            @block.scalar
            def _(act):
                act.wait_ge(s_dve, NX + 1)
                for m, (kind, g, c0, i) in enumerate(UNITS):
                    n = NX + 1 + m
                    if kind == "u":
                        act.wait_ge(s_unit, n + 1)
                        act.activation(uT[:, i, :], bank[n % 8][:], ACT.Identity,
                                       bias=col[:, R_U + i:R_U + i + 1]).then_inc(s_act, 1)
                    elif kind == "m":
                        act.wait_ge(s_unit, n + 1)
                        act.activation(gmT[:, i, :], bank[n % 8][:], ACT.Sigmoid,
                                       bias=col[:, R_M + i:R_M + i + 1]).then_inc(s_act, 1)

            @block.vector
            def _(dve):
                dve.wait_ge(s_iota, 1)
                dve.tensor_scalar(ident[:], iota_d[:], 0.0, None, ALU.is_equal).then_inc(s_id, 1)
                for n in range(NX):
                    t, h = n // 2, n % 2
                    dve.wait_ge(s_unit, n + 1)
                    dve.tensor_copy(xT[:, 4 * h:4 * h + 4, t * P:(t + 1) * P],
                                    bank[n][:].rearrange("p (k t) -> p k t", k=4)).then_inc(s_dve, 1)
                dve.wait_ge(s_unit, NX + 1)
                dve.tensor_copy(col[:], bank[NX % 8][:, 0:32]).then_inc(s_dve, 1)
                dve.wait_ge(s_dve, NX + 1)
                for m, (kind, g, c0, i) in enumerate(UNITS):
                    n = NX + 1 + m
                    b = bank[n % 8]
                    if kind in BY_ACT:
                        continue
                    dve.wait_ge(s_unit, n + 1)
                    if kind == "q":
                        ins = dve.tensor_scalar(qT[:, i, :], b[:], col[:, R_Q + i:R_Q + i + 1], HD ** -0.5, ALU.add, ALU.mult)
                    elif kind == "vg":
                        ins = dve.tensor_tensor(vN[:, i, :], b[:, 0:2 * P + GATES], vbias[:], ALU.add)
                    else:
                        j = ("kc", "vc", "ks", "kw").index(kind)
                        ins = dve.tensor_scalar(kT[:, j, :], b[:], col[:, R_KC + j:R_KC + j + 1], None, ALU.add)
                    ins.then_inc(s_dve, 1)


        TA, TB = 16, 32
        p2 = ExitStack()
        sa = sb("sa", [NPAIR, 2, P], on=p2)
        sdt = sb("sdt", [NPAIR, 2], on=p2)
        sdtx = sb("sdtx", [NPAIR, 2, SP], on=p2)
        prm = sb("prm", [NPAIR, 5, P], on=p2)
        wk = sb("wk", [NPAIR, 8, P], on=p2)
        prT = sb("prT", [P, 5, NPAIR], on=p2)
        ea = sb("ea", [P, 2, NPAIR, TA], on=p2)
        eb = sb("eb", [P, 2, NPAIR, TB], on=p2)
        pw = sb("pw", [P, 2, NPAIR], on=p2)
        wp = sb("wp", [P, 4, NPAIR, TB], on=p2)
        braw = sb("braw", [P, 2, NPAIR, SH], on=p2)
        bbar = sb("bbar", [P, 2, NPAIR, 2, SH], on=p2)
        bT = sb("bT", [P, 2, CH, P], on=p2)
        craw = sb("craw", [P, 2, CH, SP], on=p2)
        cw = sb("cw", [P, 2, CH, 2, SP], on=p2)
        cT = sb("cT", [P, 2, CH, P], on=p2)
        half_i = sb("half_i", [P, 1], mybir.dt.int32, on=p2)
        half = sb("half", [P, 2], on=p2)
        et = sb("et", [P, 2, 2, S], on=p2)
        er, br = qp[:, 0:4], qp[:, 4:8]
        zin = sb("zin", [P, 2, S], on=p2)
        z = x1T[:, 0:4].rearrange("p (o n) s -> p o n s", n=2)
        xr = sb("xr", [P, 4, S], on=p2)
        xs = sb("xs", [P, 2, 2, S], on=p2)
        wg, sg = x1, x1T[:, CH:2 * CH]
        p2.close()

        s_par = sem("s5_params_loaded")
        s_bc = sem("s5_b_c_loaded")
        s_wg = sem("w_glu_loaded")
        s_v2 = sem("dve_steps_2")
        s_a2 = sem("act_steps_2")
        s_p2 = sem("pool_steps_2")
        s_prm = sem("params_ready_to_turn")
        s_turn = sem("params_turned")
        s_bbar = sem("b_ready_to_turn")
        s_cw = sem("c_ready_to_turn")
        s_bct = sem("b_c_turned")
        s_bcs = sem("b_c_in_place")
        s_half = sem("halves_made")
        s_table = sem("tables_of_pairs")
        s_bu = sem("inputs_of_pairs")
        s_rot = sem("inputs_rotated")
        s_scan = sem("pairs_scanned")
        s_back = sem("pairs_rotated_back")
        s_yc = sem("pairs_projected")
        s_ys = sem("skip_added")
        s_gel = sem("gelu_done")
        s_glu = sem("glu_units")
        s_sig = sem("glu_gates")
        s_out2 = sem("glu_products")

        with nc.Block() as block:
            @block.sync
            def _(sp):
                sp.dma_start(sa[:, 0, :], l0("ssm_a_re").rearrange("(q g) s -> q (g s)", g=2)).then_inc(s_par, 16)
                sp.dma_start(sa[:, 1, :], l0("ssm_a_im").rearrange("(q g) s -> q (g s)", g=2)).then_inc(s_par, 16)
                sp.dma_start(sdt[:], l0("ssm_log_dt").rearrange("(q g) -> q g", g=2)).then_inc(s_par, 16)
                for n, name in enumerate(("ssm_b_re", "ssm_b_im")):
                    sp.dma_start(braw[:, n], l0(name).rearrange("(q g) s h -> (g s) q h", g=2)).then_inc(s_bc, 16)
                for n, name in enumerate(("ssm_c_re", "ssm_c_im")):
                    sp.dma_start(craw[:, n], l0(name).rearrange("(c g) h s -> (g h) c s", c=CH)).then_inc(s_bc, 16)
                sp.dma_start(wg[:], l0("w_glu").rearrange("(k p) n -> p k n", p=P)).then_inc(s_wg, 16)

            @block.gpsimd
            def _(pool):
                link = chained(pool, s_p2)
                pool.iota(half_i[:], [[0, 1]], base=0, channel_multiplier=1).then_inc(s_half, 1)
                pool.memset(bbar[:], 0.0).then_inc(s_half, 1)
                for q in range(NPAIR):
                    o = q % 2
                    pool.wait_ge(s_scan, q + 1)
                    if q >= 2:
                        pool.wait_ge(s_yc, q - 1)
                    zr, zi, c, s = z[:, o, 0], z[:, o, 1], et[:, o, 0], et[:, o, 1]
                    pool.tensor_tensor(xr[:, 0], zr, c, ALU.mult)
                    pool.tensor_tensor(xr[:, 1], zi, s, ALU.mult)
                    pool.tensor_tensor(xr[:, 2], zr, s, ALU.mult)
                    link(pool.tensor_tensor(xr[:, 3], zi, c, ALU.mult))
                    pool.tensor_tensor(xs[:, o, 0], xr[:, 0], xr[:, 1], ALU.subtract)
                    link(pool.tensor_tensor(xs[:, o, 1], xr[:, 2], xr[:, 3], ALU.add))
                    pool.sem_inc(s_back, 1)

            @block.scalar
            def _(act):
                link = chained(act, s_a2)
                act.wait_ge(s_par, 48)
                link(act.activation(sdt[:], sdt[:], ACT.Exp))
                act.wait_ge(s_v2, 2)
                link(act.activation(prm[:, 0, :], wk[:, 0, :], ACT.Exp))
                act.wait_ge(s_v2, 9)
                link(act.activation(wk[:, 3, :], wk[:, 2, :], ACT.Sin))
                link(act.activation(wk[:, 4, :], wk[:, 2, :], ACT.Sin, scale=0.5))
                for c in range(CH):
                    act.wait_ge(s_ys, c + 1)
                    act.activation(uT[:, c, :], uT[:, c, :], ACT.Gelu_apprx_tanh).then_inc(s_gel, 1)
                for c in range(CH):
                    act.wait_ge(s_glu, c + 1)
                    act.activation(sg[:, c, :], bank[c][:], ACT.Sigmoid).then_inc(s_sig, 1)

            @block.tensor
            def _(pe):
                pe.wait_ge(s_prm, 1)
                for n in range(5):
                    last = pe.transpose(bank[0][:, n * NPAIR:(n + 1) * NPAIR], prm[:, n, :], ident[0:NPAIR, 0:NPAIR])
                last.then_inc(s_turn, 1)
                pe.wait_ge(s_bbar, 1)
                for n in range(2):
                    for c in range(CH):
                        last = pe.transpose(bank[1 + n][:, c * P:(c + 1) * P],
                                            bbar[:, n, 4 * c:4 * c + 4].rearrange("p q g h -> p (q g h)"), ident[:])
                last.then_inc(s_bct, 1)
                pe.wait_ge(s_cw, 1)
                for n in range(2):
                    for c in range(CH):
                        last = pe.transpose(bank[3 + n][:, c * P:(c + 1) * P],
                                            cw[:, n, c].rearrange("p g s -> p (g s)"), ident[:])
                last.then_inc(s_bct, 1)
                pe.wait_ge(s_bcs, 4)

                def inputs(q):
                    if q >= 2:
                        pe.wait_ge(s_rot, q - 1)
                    c, r = q // 4, 32 * (q % 4)
                    for n in range(2):
                        last = pe.matmul(bank[2 * (q % 2) + n][:], bT[r:r + 32, n, c, :], uT[r:r + 32, c, :],
                                         start=True, stop=True)
                    last.then_inc(s_bu, 1)

                inputs(0)
                for q in range(NPAIR):
                    if q + 1 < NPAIR:
                        inputs(q + 1)
                    pe.wait_ge(s_back, q + 1)
                    c, r = q // 4, 32 * (q % 4)
                    for n in range(2):
                        last = pe.matmul(bank[4 + c][r:r + 32, :], cT[:, n, c, r:r + 32], xs[:, q % 2, n, :],
                                         start=n == 0, stop=n == 1)
                    last.then_inc(s_yc, 1)
                pe.wait_ge(s_wg, 16)
                for half_ in (1, 0):
                    for c in range(CH):
                        for k in range(CH):
                            pe.wait_ge(s_gel, k + 1)
                            last = pe.matmul(bank[4 * (1 - half_) + c][:], wg[:, k, half_ * SSM + c * P:half_ * SSM + (c + 1) * P],
                                             uT[:, k, :], start=k == 0, stop=k == CH - 1)
                        last.then_inc(s_glu, 1)

            @block.vector
            def _(dve):
                link = chained(dve, s_v2)
                dve.wait_ge(s_a2, 1)
                dtb = sdt[:].unsqueeze(2).broadcast_to([NPAIR, 2, SP])
                w = lambda n: wk[:, n, :]
                link(dve.tensor_copy(sdtx[:], dtb))
                dts = sdtx[:].rearrange("p g s -> p (g s)")
                link(dve.tensor_tensor(w(0), sa[:, 0, :], dts, ALU.mult))
                link(dve.tensor_tensor(w(1), sa[:, 1, :], dts, ALU.mult))
                link(dve.tensor_scalar(w(5), w(1), 1 / (2 * math.pi), ROUND, ALU.mult, ALU.add))
                link(dve.tensor_scalar(w(5), w(5), ROUND, None, ALU.subtract))
                link(dve.scalar_tensor_tensor(w(1), w(5), -PI2_A, w(1), ALU.mult, ALU.add))
                link(dve.scalar_tensor_tensor(w(6), w(5), -PI2_B, w(1), ALU.mult, ALU.add))
                link(dve.scalar_tensor_tensor(w(6), w(5), -PI2_C, w(6), ALU.mult, ALU.add))
                link(dve.tensor_scalar(w(2), w(6), 3.1415925, -3.1415925, ALU.min, ALU.max))
                dve.wait_ge(s_a2, 4)
                link(dve.tensor_tensor(w(5), w(4), w(4), ALU.mult))
                link(dve.tensor_scalar(w(5), w(5), -2.0, 1.0, ALU.mult, ALU.add))
                link(dve.tensor_tensor(w(6), w(5), w(5), ALU.mult))
                link(dve.tensor_tensor(w(7), w(3), w(3), ALU.mult))
                link(dve.tensor_tensor(w(6), w(6), w(7), ALU.add))
                link(dve.tensor_scalar(w(6), w(6), -0.5, 1.5, ALU.mult, ALU.add))
                link(dve.tensor_tensor(prm[:, 1, :], w(5), w(6), ALU.mult))
                link(dve.tensor_tensor(prm[:, 2, :], w(3), w(6), ALU.mult))
                link(dve.tensor_tensor(w(0), prm[:, 0, :], prm[:, 1, :], ALU.mult))
                link(dve.tensor_scalar(w(0), w(0), 1.0, None, ALU.subtract))
                link(dve.tensor_tensor(w(1), prm[:, 0, :], prm[:, 2, :], ALU.mult))
                link(dve.tensor_tensor(w(2), sa[:, 0, :], sa[:, 0, :], ALU.mult))
                link(dve.tensor_tensor(w(3), sa[:, 1, :], sa[:, 1, :], ALU.mult))
                link(dve.tensor_tensor(w(2), w(2), w(3), ALU.add))
                link(dve.reciprocal(w(2), w(2)))
                link(dve.tensor_tensor(w(4), w(0), sa[:, 0, :], ALU.mult))
                link(dve.tensor_tensor(w(5), w(1), sa[:, 1, :], ALU.mult))
                link(dve.tensor_tensor(w(4), w(4), w(5), ALU.add))
                link(dve.tensor_tensor(w(6), w(1), sa[:, 0, :], ALU.mult))
                link(dve.tensor_tensor(w(7), w(0), sa[:, 1, :], ALU.mult))
                link(dve.tensor_tensor(w(6), w(6), w(7), ALU.subtract))
                link(dve.tensor_tensor(prm[:, 3, :], w(4), w(2), ALU.mult))
                link(dve.tensor_tensor(prm[:, 4, :], w(6), w(2), ALU.mult))
                dve.sem_inc(s_prm, 1)
                dve.wait_ge(s_half, 2)
                link(dve.tensor_scalar(half_i[:], half_i[:], 4, 1, ALU.arith_shift_right, ALU.bitwise_and))
                link(dve.tensor_copy(half[:, 1:2], half_i[:]))
                link(dve.tensor_scalar(half[:, 0:1], half[:, 1:2], -1.0, 1.0, ALU.mult, ALU.add))
                dve.wait_ge(s_bc, 64)
                for n in range(2):
                    for g in range(2):
                        link(dve.tensor_scalar(cw[:, n, :, g, :], craw[:, n], half[:, g:g + 1],
                                               1.0 - 2.0 * n, ALU.mult, ALU.mult))
                dve.sem_inc(s_cw, 1)
                dve.wait_ge(s_turn, 1)
                link(dve.tensor_copy(prT[:], bank[0][:, 0:5 * NPAIR].rearrange("p (n q) -> p n q", n=5)))
                fr = prT[:, 3, :].unsqueeze(2).broadcast_to([P, NPAIR, SH])
                fi = prT[:, 4, :].unsqueeze(2).broadcast_to([P, NPAIR, SH])
                t = lambda n: wp[:, n, :, 0:SH]
                for n, (x, y, op) in enumerate(((fr, fi, ALU.subtract), (fi, fr, ALU.add))):
                    link(dve.tensor_tensor(t(0), x, braw[:, 0], ALU.mult))
                    link(dve.tensor_tensor(t(1), y, braw[:, 1], ALU.mult))
                    for g in range(2):
                        h = slice(g * SP, (g + 1) * SP)
                        link(dve.tensor_tensor(bbar[h, n, :, g, :], wp[h, 0, :, 0:SH], wp[h, 1, :, 0:SH], op))
                dve.sem_inc(s_bbar, 1)

                def cmul(oc, os, ac, as_, bc, bs, tmp):
                    link(dve.tensor_tensor(tmp(0), ac, bc, ALU.mult))
                    link(dve.tensor_tensor(tmp(1), as_, bs, ALU.mult))
                    link(dve.tensor_tensor(tmp(2), ac, bs, ALU.mult))
                    link(dve.tensor_tensor(tmp(3), as_, bc, ALU.mult))
                    link(dve.tensor_tensor(oc, tmp(0), tmp(1), ALU.subtract))
                    link(dve.tensor_tensor(os, tmp(2), tmp(3), ALU.add))

                def powers(tab, count):
                    link(dve.memset(tab[:, 0, :, 0:1], 1.0))
                    link(dve.memset(tab[:, 1, :, 0:1], 0.0))
                    n = 1
                    while n < count:
                        bc = pw[:, 0, :].unsqueeze(2).broadcast_to([P, NPAIR, n])
                        bs = pw[:, 1, :].unsqueeze(2).broadcast_to([P, NPAIR, n])
                        cmul(tab[:, 0, :, n:2 * n], tab[:, 1, :, n:2 * n], tab[:, 0, :, 0:n], tab[:, 1, :, 0:n],
                             bc, bs, lambda m: wp[:, m, :, 0:n])
                        cmul(pw[:, 0, :], pw[:, 1, :], pw[:, 0, :], pw[:, 1, :], pw[:, 0, :], pw[:, 1, :],
                             lambda m: wp[:, m, :, 0])
                        link(dve.tensor_tensor(wp[:, 0, :, 0], pw[:, 0, :], pw[:, 0, :], ALU.mult))
                        link(dve.tensor_tensor(wp[:, 1, :, 0], pw[:, 1, :], pw[:, 1, :], ALU.mult))
                        link(dve.tensor_tensor(wp[:, 0, :, 0], wp[:, 0, :, 0], wp[:, 1, :, 0], ALU.add))
                        link(dve.tensor_scalar(wp[:, 0, :, 0], wp[:, 0, :, 0], -0.5, 1.5, ALU.mult, ALU.add))
                        link(dve.tensor_tensor(pw[:, 0, :], pw[:, 0, :], wp[:, 0, :, 0], ALU.mult))
                        link(dve.tensor_tensor(pw[:, 1, :], pw[:, 1, :], wp[:, 0, :, 0], ALU.mult))
                        n *= 2

                link(dve.tensor_copy(pw[:], prT[:, 1:3, :]))
                powers(eb, TB)
                powers(ea, TA)
                for n, (dst, src) in enumerate(((bT, 1), (cT, 3))):
                    dve.wait_ge(s_bct, n + 1)
                    for m in range(2):
                        dve.tensor_copy(dst[:, m], bank[src + m][:].rearrange("p (c x) -> p c x", c=CH)).then_inc(s_bcs, 1)

                def table(q):
                    o = q % 2
                    if q >= 2:
                        dve.wait_ge(s_back, q - 1)
                    A = lambda n: ea[:, n, q, :].unsqueeze(2).broadcast_to([P, TA, TB])
                    B = lambda n: eb[:, n, q, :].unsqueeze(1).broadcast_to([P, TA, TB])
                    v = lambda x: x.rearrange("p (a b) -> p a b", b=TB)
                    dve.tensor_tensor(v(er[:, 0]), A(0), B(0), ALU.mult)
                    dve.tensor_tensor(v(er[:, 1]), A(1), B(1), ALU.mult)
                    dve.tensor_tensor(v(er[:, 2]), A(0), B(1), ALU.mult)
                    link(dve.tensor_tensor(v(er[:, 3]), A(1), B(0), ALU.mult))
                    dve.tensor_tensor(et[:, o, 0], er[:, 0], er[:, 1], ALU.subtract)
                    link(dve.tensor_tensor(et[:, o, 1], er[:, 2], er[:, 3], ALU.add))

                for q in range(NPAIR):
                    o = q % 2
                    table(q)
                    c, s = et[:, o, 0], et[:, o, 1]
                    dve.wait_ge(s_bu, q + 1)
                    bre, bim = bank[2 * o][:], bank[2 * o + 1][:]
                    dve.tensor_tensor(br[:, 0], bre, c, ALU.mult)
                    dve.tensor_tensor(br[:, 1], bim, s, ALU.mult)
                    dve.tensor_tensor(br[:, 2], bim, c, ALU.mult)
                    link(dve.tensor_tensor(br[:, 3], bre, s, ALU.mult))
                    dve.sem_inc(s_rot, 1)
                    dve.tensor_tensor(zin[:, 0], br[:, 0], br[:, 1], ALU.add)
                    link(dve.tensor_tensor(zin[:, 1], br[:, 2], br[:, 3], ALU.subtract))
                    rr = prT[:, 0, q:q + 1].broadcast_to([P, S])
                    dve.tensor_tensor_scan(z[:, o, 0], rr, zin[:, 0], 0.0, ALU.mult, ALU.add)
                    link(dve.tensor_tensor_scan(z[:, o, 1], rr, zin[:, 1], 0.0, ALU.mult, ALU.add))
                    dve.sem_inc(s_scan, 1)
                for c in range(CH):
                    dve.wait_ge(s_yc, 4 * (c + 1))
                    dve.scalar_tensor_tensor(uT[:, c, :], uT[:, c, :], col[:, R_D + c:R_D + c + 1], bank[4 + c][:],
                                             ALU.mult, ALU.add).then_inc(s_ys, 1)
                for c in range(CH):
                    dve.wait_ge(s_sig, c + 1)
                    dve.wait_ge(s_glu, CH + c + 1)
                    dve.tensor_tensor(gluT[:, c, :], bank[4 + c][:], sg[:, c, :], ALU.mult).then_inc(s_out2, 1)

        NB = 2
        p3 = ExitStack()
        w1 = sb("w1", [P, 2, CB, P], on=p3)
        w2k = sb("w2k", [P, 2, HD], on=p3)
        w2v = sb("w2v", [P, HD], on=p3)
        pe_r = sb("pe_r", [CB, 2, 2, HD], on=p3)
        peT = sb("peT", [P, 2, CB], on=p3)
        blk = sb("blk", [P, 2, CB, NC32], on=p3)
        hT = sb("hT", [P, 2, KVG, NC32], on=p3)
        h4 = sb("h4", [P, KVG, HPG, NC32], on=p3)
        kcmp = sb("kcmp", [P, NC32], on=p3)
        vbd = sb("vbd", [P, KVG, HPG, HD], on=p3)
        slopes = sb("slopes", [P, HEADS], on=p3)
        dist = sb("dist", [P, S], on=p3)
        distc = sb("distc", [P, TT, NC32], on=p3)
        maskc = sb("maskc", [P, TT, NC32], on=p3)
        gate = sb("gate", [P, TT, GATES], on=p3)
        sc_c = sb("sc_c", [P, HEADS, NC32], on=p3)
        p_c = sb("p_c", [P, HEADS, NC32], on=p3)
        mx_c = sb("mx_c", [P, HEADS], on=p3)
        pTc = sb("pTc", [P, 2, P], on=p3)
        den = sb("den", [P, 2, 3, HEADS], on=p3)
        coef = sb("coef", [P, 3, HEADS], on=p3)
        sc = sb("sc", [P, 3, S], on=p3)
        nmx = sb("nmx", [P, 3], on=p3)
        pr = sb("pr", [P, 3, S], on=p3)
        pT = sb("pT", [P, 2, S], on=p3)
        acc = sb("acc", [P, HEADS, HD], on=p3)
        tmp3 = sb("tmp3", [P, HEADS, HD], on=p3)
        p3.close()

        wu = (x1, qp[:].rearrange("p (k a) s -> p k (a s)", a=2))
        s_wu = sem("w_up_loaded")
        s_w1 = sem("compression_loaded")
        s_tab = sem("distances_made")
        s_v3 = sem("dve_steps_3")
        s_pe3 = sem("pe_positions_turned")
        s_blk = sem("blocks_made")
        s_hid = sem("hidden_made")
        s_hT = sem("hidden_gelu")
        s_cmp = sem("compressed_made")
        s_cin = sem("compressed_in_place")
        s_gt = sem("gates_made")
        s_sc = sem("scores_made")
        s_mx = sem("scores_shifted")
        s_ex = sem("exponentials")
        s_tp = sem("probs_turned")
        s_pt = sem("probs_in_place")
        s_pv = sem("heads_weighed")
        s_scc = sem("cmp_scores_made")
        s_mxc = sem("cmp_scores_shifted")
        s_exc = sem("cmp_exponentials")
        s_pc = sem("cmp_probs_masked")
        s_tpc = sem("cmp_probs_turned")
        s_ptc = sem("cmp_probs_in_place")
        s_oc = sem("cmp_output_made")
        s_comb = sem("tiles_combined")
        s_nt = sem("tiles_turned")
        s_nT = sem("tiles_in_place")

        HU = [(i, b, h) for i in range(TT) for b in range(NB) for h in range(HEADS)]
        PT_ = NB * HEADS
        AT_COMBINE, AT_TURN, AT_TURNED, AT_CS, AT_CX, AT_CM, AT_CT, AT_CP, AT_CW = 1, 1, 2, 3, 6, 8, 9, 10, 11

        with nc.Block() as block:
            @block.sync
            def _(sp):
                for n, kv in enumerate("kv"):
                    for g in range(KVG):
                        sp.dma_start(w1[g * HD:(g + 1) * HD, n], l0(f"nsa_w1_{kv}").rearrange("(l d) h -> d l h", d=HD)).then_inc(s_w1, 16)
                        sp.dma_start(pe_r[:, n, g], l0(f"nsa_pe_{kv}")).then_inc(s_w1, 16)
                for g in range(KVG):
                    sp.dma_start(w2k[:, g], l0("nsa_w2_k")).then_inc(s_w1, 16)
                sp.dma_start(w2v[:], l0("nsa_w2_v")).then_inc(s_w1, 16)
                sp.dma_start(wu[0][:], l0("w_up_ssm").rearrange("(k p) n -> p k n", p=P)).then_inc(s_wu, 16)
                sp.dma_start(wu[1], l0("w_up_nsa").rearrange("(k p) n -> p k n", p=P)).then_inc(s_wu, 16)

            @block.gpsimd
            def _(pool):
                n = [0]

                def step(ins):
                    n[0] += 1
                    ins.then_inc(s_tab, 1)
                    pool.wait_ge(s_tab, n[0])
                for h in range(HEADS):
                    last = pool.memset(slopes[:, h:h + 1], 2.0 ** (-8.0 * (h + 1) / HEADS))
                step(last)
                step(pool.iota(dist[:], [[1, S]], base=-(S - P), channel_multiplier=-1, allow_small_or_imprecise_dtypes=True))
                step(pool.affine_select(dist[:], dist[:], [[-1, S]], ALU.is_ge, NEG, base=S - P, channel_multiplier=1))
                step(pool.iota(distc[:], [[-P, TT], [CS, NC32]], base=CB - 1, channel_multiplier=-1, allow_small_or_imprecise_dtypes=True))
                step(pool.memset(maskc[:], 1.0))
                step(pool.affine_select(distc[:], distc[:], [[P, TT], [-CS, NC32]], ALU.is_ge, NEG, base=-(CB - 1), channel_multiplier=1))
                step(pool.affine_select(maskc[:], maskc[:], [[P, TT], [-CS, NC32]], ALU.is_ge, 0.0, base=-(CB - 1), channel_multiplier=1))
                step(pool.memset(vbd[:], 0.0))
                step(pool.memset(blk[:], 0.0))

            @block.scalar
            def _(act):
                act.activation(gate[:], vN[:, :, 2 * P:], ACT.Sigmoid).then_inc(s_gt, 1)
                for n in range(4):
                    act.wait_ge(s_hid, n + 1)
                    act.activation(hT[:, n // 2, n % 2], bank[n][:, 0:NC32], ACT.Gelu_apprx_tanh).then_inc(s_hT, 1)

                def turned(u):
                    i = HU[u][0]
                    act.wait_ge(s_tp, u + 1)
                    if u >= 2:
                        act.wait_ge(s_pv, u - 1)
                    act.activation(pT[:, u % 2, 0:P * (i + 1)], bank[2 + u % 2][:, 0:P * (i + 1)], ACT.Copy).then_inc(s_pt, 1)

                for u, (i, b, h) in enumerate(HU):
                    if u % PT_ == AT_CX + 1:
                        act.wait_ge(s_mxc, i + 1)
                        act.activation(p_c[:], sc_c[:], ACT.Exp).then_inc(s_exc, 1)
                    act.wait_ge(s_mx, u + 1)
                    if u >= 3:
                        act.wait_ge(s_tp, u - 2)
                    if i >= 2:
                        act.wait_ge(s_comb, i - 1)
                    L = P * (i + 1)
                    act.activation(pr[:, u % 3, 0:L], sc[:, u % 3, 0:L], ACT.Exp, bias=nmx[:, u % 3:u % 3 + 1],
                                   accum_out=den[:, i % 2, 1 + b, h:h + 1]).then_inc(s_ex, 1)
                    if u >= 1:
                        turned(u - 1)
                turned(len(HU) - 1)

            @block.tensor
            def _(pe):
                pe.wait_ge(s_w1, 16 * 11)
                for n in range(2):
                    last = pe.transpose(bank[4][:, n * CB:(n + 1) * CB], pe_r[:, n].rearrange("l g d -> l (g d)"), ident[0:CB, 0:CB])
                last.then_inc(s_pe3, 1)
                for n in range(2):
                    pe.wait_ge(s_blk, n + 1)
                    for g in range(KVG):
                        r = slice(g * HD, (g + 1) * HD)
                        for l in range(CB):
                            last = pe.matmul(bank[2 * n + g][:, 0:NC32], w1[r, n, l, :], blk[r, n, l, :],
                                             start=l == 0, stop=l == CB - 1)
                        last.then_inc(s_hid, 1)
                pe.wait_ge(s_hT, 2)
                pe.matmul(bank[5][:, 0:2 * NC32], w2k[:].rearrange("p g d -> p (g d)"),
                          hT[:, 0].rearrange("p g c -> p (g c)"), start=True, stop=True).then_inc(s_cmp, 1)
                pe.wait_ge(s_cin, 1)
                for g in range(KVG):
                    last = pe.matmul(bank[6 + g][:, 0:HD], h4[:, g].rearrange("p h c -> p (h c)"), w2v[:], start=True, stop=True)
                last.then_inc(s_cmp, 1)
                pe.wait_ge(s_cin, 3)

                def scores(u):
                    i, b, h = HU[u]
                    g, c = h // HPG, h % HPG
                    r = slice(g * HD, (g + 1) * HD)
                    if u >= 2:
                        pe.wait_ge(s_mx, u - 1)
                    pe.matmul(bank[u % 2][:, 0:P * (i + 1)], qT[r, c, i * P:(i + 1) * P], kT[r, 2 + b, 0:P * (i + 1)],
                              start=True, stop=True).then_inc(s_sc, 1)

                def turn(u):
                    i = HU[u][0]
                    pe.wait_ge(s_ex, u + 1)
                    if u >= 2:
                        pe.wait_ge(s_pt, u - 1)
                    for k in range(i + 1):
                        last = pe.transpose(bank[2 + u % 2][:, k * P:(k + 1) * P], pr[:, u % 3, k * P:(k + 1) * P], ident[:])
                    last.then_inc(s_tp, 1)

                def weigh(u):
                    i, b, h = HU[u]
                    g = h // HPG
                    pe.wait_ge(s_pt, u + 1)
                    if h == 0 and i:
                        pe.wait_ge(s_comb, i)
                    for k in range(i + 1):
                        last = pe.matmul(bank[4 + b][:, h * HD:(h + 1) * HD], pT[:, u % 2, k * P:(k + 1) * P],
                                         vN[:, k, b * P + g * HD:b * P + (g + 1) * HD], start=k == 0, stop=k == i)
                    last.then_inc(s_pv, 1)

                def cmp_scores(i):
                    if i:
                        pe.wait_ge(s_nT, i)
                        pe.wait_ge(s_comb, i)
                    for g in range(KVG):
                        r = slice(g * HD, (g + 1) * HD)
                        for c in range(HPG):
                            last = pe.matmul(bank[6 + g][:, c * NC32:(c + 1) * NC32], qT[r, c, i * P:(i + 1) * P],
                                             kcmp[r, :], start=True, stop=True)
                        last.then_inc(s_scc, 1)

                def cmp_turn(i):
                    pe.wait_ge(s_pc, i + 1)
                    for g in range(KVG):
                        last = pe.transpose(bank[6][:, g * P:(g + 1) * P],
                                            p_c[:, g * HPG:(g + 1) * HPG].rearrange("p h c -> p (h c)"), ident[:])
                    last.then_inc(s_tpc, 1)

                def cmp_weigh(i):
                    pe.wait_ge(s_ptc, i + 1)
                    for g in range(KVG):
                        last = pe.matmul(bank[7][:, g * 256:(g + 1) * 256], pTc[:, g, :],
                                         vbd[:, g].rearrange("p h d -> p (h d)"), start=True, stop=True)
                    last.then_inc(s_oc, 1)

                def tile_turn(i):
                    pe.wait_ge(s_comb, i + 1)
                    for c in range(CH):
                        last = pe.transpose(bank[6][:, c * P:(c + 1) * P],
                                            acc[:, 2 * c:2 * c + 2].rearrange("p h d -> p (h d)"), ident[:])
                    last.then_inc(s_nt, 1)

                scores(0)
                scores(1)
                for u, (i, b, h) in enumerate(HU):
                    turn(u)
                    if u + 2 < len(HU):
                        scores(u + 2)
                    if u >= 1:
                        weigh(u - 1)
                    at = u % PT_
                    if at == AT_TURN and i:
                        tile_turn(i - 1)
                    if at == AT_CS:
                        cmp_scores(i)
                    if at == AT_CT:
                        cmp_turn(i)
                    if at == AT_CW:
                        cmp_weigh(i)
                weigh(len(HU) - 1)
                tile_turn(TT - 1)

            @block.vector
            def _(dve):
                link = chained(dve, s_v3)
                dve.wait_ge(s_pe3, 1)
                link(dve.tensor_copy(peT[:], bank[4][:, 0:2 * CB].rearrange("p (n l) -> p n l", n=2)))
                dve.wait_ge(s_tab, 9)
                for n in range(2):
                    v = kT[:, n, :].rearrange("p (c s) -> p s c", s=CS)
                    for m in range(2):
                        pb = peT[:, n, m * CS:(m + 1) * CS].unsqueeze(2).broadcast_to([P, CS, NCMP])
                        last = dve.tensor_tensor(blk[:, n, m * CS:(m + 1) * CS, 0:NCMP], v[:, :, m:m + NCMP], pb, ALU.add)
                        link(last)
                    dve.sem_inc(s_blk, 1)
                dve.wait_ge(s_hT, 4)
                for g in range(KVG):
                    last = dve.tensor_copy(h4[:, g], hT[:, 1, g].unsqueeze(1).broadcast_to([P, HPG, NC32]))
                last.then_inc(s_cin, 1)
                dve.wait_ge(s_cmp, 1)
                for g in range(KVG):
                    r = slice(g * HD, (g + 1) * HD)
                    last = dve.tensor_copy(kcmp[r, :], bank[5][r, g * NC32:(g + 1) * NC32])
                last.then_inc(s_cin, 1)
                dve.wait_ge(s_cmp, 2)
                for g in range(KVG):
                    for h in range(HPG):
                        r = slice(h * NC32, (h + 1) * NC32)
                        last = dve.tensor_copy(vbd[r, g, h, :], bank[6 + g][r, 0:HD])
                last.then_inc(s_cin, 1)
                dve.wait_ge(s_gt, 1)

                def combine(i):
                    dve.wait_ge(s_pv, PT_ * (i + 1))
                    dve.wait_ge(s_oc, i + 1)
                    if i:
                        dve.wait_ge(s_nt, i)
                    link(dve.reciprocal(coef[:], den[:, i % 2]))
                    link(dve.tensor_tensor(coef[:], coef[:], gate[:, i].rearrange("p (h b) -> p b h", b=3), ALU.mult))
                    by = lambda n: coef[:, n, :].unsqueeze(2).broadcast_to([P, HEADS, HD])
                    o = lambda n: bank[n][:].rearrange("p (h d) -> p h d", d=HD)
                    link(dve.tensor_tensor(acc[:], o(7), by(0), ALU.mult))
                    for n in (4, 5):
                        link(dve.tensor_tensor(tmp3[:], o(n), by(n - 3), ALU.mult))
                        link(dve.tensor_tensor(acc[:], acc[:], tmp3[:], ALU.add))
                    dve.sem_inc(s_comb, 1)

                def take(i):
                    dve.wait_ge(s_nt, i + 1)
                    dve.tensor_copy(nsaT[:, :, i * P:(i + 1) * P], bank[6][:].rearrange("p (c t) -> p c t", c=CH)).then_inc(s_nT, 1)

                for u, (i, b, h) in enumerate(HU):
                    o, L = u % 3, P * (i + 1)
                    dve.wait_ge(s_sc, u + 1)
                    if u >= 3:
                        dve.wait_ge(s_ex, u - 2)
                    link(dve.scalar_tensor_tensor(sc[:, o, 0:L], dist[:, S - L:S], slopes[:, h:h + 1], bank[u % 2][:, 0:L],
                                                  ALU.mult, ALU.add))
                    dve.tensor_reduce(nmx[:, o:o + 1], sc[:, o, 0:L], AX.X, ALU.max, negate=True).then_inc(s_mx, 1)
                    at = u % PT_
                    if at == AT_COMBINE and i:
                        combine(i - 1)
                    if at == AT_TURNED and i:
                        take(i - 1)
                    if at == AT_CX:
                        dve.wait_ge(s_scc, 2 * (i + 1))
                        if i:
                            dve.wait_ge(s_tpc, i)
                        link(dve.tensor_tensor(sc_c[:], distc[:, i].unsqueeze(1).broadcast_to([P, HEADS, NC32]),
                                               slopes[:].unsqueeze(2).broadcast_to([P, HEADS, NC32]), ALU.mult))
                        for g in range(KVG):
                            hs = slice(g * HPG, (g + 1) * HPG)
                            last = dve.tensor_tensor(sc_c[:, hs], sc_c[:, hs],
                                                     bank[6 + g][:, 0:P].rearrange("p (h c) -> p h c", c=NC32), ALU.add)
                            link(last)
                        link(dve.tensor_reduce(mx_c[:], sc_c[:], AX.X, ALU.max))
                        dve.tensor_tensor(sc_c[:], sc_c[:], mx_c[:].unsqueeze(2).broadcast_to([P, HEADS, NC32]),
                                          ALU.subtract).then_inc(s_mxc, 1)
                    if at == AT_CM:
                        dve.wait_ge(s_exc, i + 1)
                        link(dve.tensor_tensor(p_c[:], p_c[:], maskc[:, i].unsqueeze(1).broadcast_to([P, HEADS, NC32]), ALU.mult))
                        dve.sem_inc(s_pc, 1)
                        link(dve.tensor_reduce(den[:, i % 2, 0], p_c[:], AX.X, ALU.add))
                        link(dve.tensor_scalar(den[:, i % 2, 0], den[:, i % 2, 0], 1e-30, None, ALU.max))
                    if at == AT_CP:
                        dve.wait_ge(s_tpc, i + 1)
                        dve.tensor_copy(pTc[:], bank[6][:, 0:2 * P].rearrange("p (g t) -> p g t", g=2)).then_inc(s_ptc, 1)
                combine(TT - 1)
                take(TT - 1)

        def row(name, n0, n1):
            return spread(l0(name)[n0:n1], n1 - n0)

        p4 = ExitStack()
        xr2 = sb("xr2", [P, TT, D], on=p4)
        wo = sb("wo", [P, KD, D], on=p4)
        sk = sb("sk", [P, 2 * PH, HD], on=p4)
        ln1 = sb("ln1", [P, 2, D], on=p4)
        mt = x1T[:, 0:2]
        st = sb("st", [P, 2, 6], on=p4)
        mv = sb("mv", [P, TT, 2], on=p4)
        rs = sb("rs", [P, TT], on=p4)
        p4.close()

        s_wo = sem("w_out_loaded")
        s_wq = sem("w_q_loaded")
        s_sk = sem("subkeys_loaded")
        s_x2 = sem("x_loaded_again")
        s_up = sem("chunks_projected_up")
        s_mix = sem("chunks_merged")
        s_o = sem("halves_projected_out")
        s_res = sem("halves_added")
        s_var = sem("variances")
        s_std = sem("deviations")
        s_x1 = sem("x1_tiles")
        s_xt = sem("x1_turned")
        s_xT = sem("x1T_in_place")
        s_v4 = sem("dve_steps_4")
        s_xhl = sem("x1_parts_made")

        with nc.Block() as block:
            @block.sync
            def _(sp):
                sp.dma_start(wo[:], l0("w_out").rearrange("(k p) n -> p k n", p=P)).then_inc(s_wo, 16)
                sp.dma_start(xr2[:], a["x"][0].rearrange("(t p) d -> p t d", p=P)).then_inc(s_x2, 16)
                sp.dma_start(ln1[:, 0, :], row("ln1_g", 0, D)).then_inc(s_x2, 16)
                sp.dma_start(ln1[:, 1, :], row("ln1_b", 0, D)).then_inc(s_x2, 16)
                sp.dma_start(sk[:], l0("peer_subkeys").rearrange("h c k d -> k (h c) d")).then_inc(s_sk, 16)
                sp.wait_ge(s_mix, KD)
                sp.dma_start(wq[:], l0("peer_w_q").rearrange("(k p) n -> p k n", p=P)).then_inc(s_wq, 16)

            @block.tensor
            def _(pe):
                pe.wait_ge(s_wu, 32)
                for c in range(KD):
                    if c >= 2:
                        pe.wait_ge(s_mix, c - 1)
                    for n, y in enumerate((gluT, nsaT)):
                        for k in range(CH):
                            last = pe.matmul(bank[2 * (c % 2) + n][:], wu[n][:, k, c * P:(c + 1) * P], y[:, k, :],
                                             start=k == 0, stop=k == CH - 1)
                    last.then_inc(s_up, 1)
                pe.wait_ge(s_wo, 16)
                pe.wait_ge(s_mix, KD)
                for t in range(TT):
                    for n in range(2):
                        m = 2 * t + n
                        if m >= 4:
                            pe.wait_ge(s_res, m - 3)
                        for k in range(KD):
                            last = pe.matmul(bank[4 + m % 4][:], gmT[:, k, t * P:(t + 1) * P], wo[:, k, n * 512:(n + 1) * 512],
                                             start=k == 0, stop=k == KD - 1)
                        last.then_inc(s_o, 1)
                for t in range(TT):
                    pe.wait_ge(s_x1, t + 1)
                    for n in range(2):
                        m = 2 * t + n
                        if m >= 4:
                            pe.wait_ge(s_xT, m - 3)
                            pe.wait_ge(s_xhl, m - 3)
                        for k in range(4):
                            last = pe.transpose(bank[m % 4][:, k * P:(k + 1) * P], x1[:, t, (4 * n + k) * P:(4 * n + k + 1) * P], ident[:])
                        last.then_inc(s_xt, 1)

            @block.scalar
            def _(act):
                for t in range(TT):
                    act.wait_ge(s_var, t + 1)
                    act.activation(rs[:, t:t + 1], mv[:, t, 1:2], ACT.Sqrt).then_inc(s_std, 1)
                for m in range(2 * TT):
                    t, n = m // 2, m % 2
                    act.wait_ge(s_xt, m + 1)
                    b = bank[m % 4][:].rearrange("p (k t) -> p k t", k=4)
                    act.activation(xh[:, 4 * n:4 * n + 4, t * P:(t + 1) * P], b, ACT.Copy)
                    act.activation(x1T[:, 4 * n:4 * n + 4, t * P:(t + 1) * P], b, ACT.Copy).then_inc(s_xT, 1)

            @block.vector
            def _(dve):
                link = chained(dve, s_v4)
                for c in range(KD):
                    dve.wait_ge(s_up, c + 1)
                    b = 2 * (c % 2)
                    dve.tensor_tensor(mt[:, 0], bank[b][:], gmT[:, c, :], ALU.mult)
                    link(dve.tensor_tensor(mt[:, 1], bank[b + 1][:], gmT[:, KD + c, :], ALU.mult))
                    link(dve.tensor_tensor(gmT[:, c, :], mt[:, 0], mt[:, 1], ALU.add))
                    dve.sem_inc(s_mix, 1)
                dve.wait_ge(s_x2, 48)
                for t in range(TT):
                    for n in range(2):
                        h = slice(n * 512, (n + 1) * 512)
                        dve.wait_ge(s_o, 2 * t + n + 1)
                        link(dve.scalar_tensor_tensor(x1[:, t, h], xr2[:, t, h], DN_ALPHA, bank[4 + (2 * t + n) % 4][:], ALU.mult, ALU.add))
                        dve.sem_inc(s_res, 1)
                        link(dve.bn_stats(st[:, n, :], x1[:, t, h]))
                    link(dve.bn_aggr(mv[:, t, :], st[:].rearrange("p n s -> p (n s)")))
                    dve.tensor_scalar(mv[:, t, 1:2], mv[:, t, 1:2], LN_EPS, None, ALU.add).then_inc(s_var, 1)
                    dve.wait_ge(s_std, t + 1)
                    link(dve.reciprocal(rs[:, t:t + 1], rs[:, t:t + 1]))
                    link(dve.tensor_scalar(x1[:, t, :], x1[:, t, :], mv[:, t, 0:1], rs[:, t:t + 1], ALU.subtract, ALU.mult))
                    link(dve.tensor_tensor(x1[:, t, :], x1[:, t, :], ln1[:, 0, :], ALU.mult))
                    dve.tensor_tensor(x1[:, t, :], x1[:, t, :], ln1[:, 1, :], ALU.add).then_inc(s_x1, 1)
                for m in range(2 * TT):
                    t, n = m // 2, m % 2
                    dve.wait_ge(s_xT, m + 1)
                    at = (slice(None), slice(4 * n, 4 * n + 4), slice(t * P, (t + 1) * P))
                    dve.tensor_tensor(xl[at], bank[m % 4][:].rearrange("p (k t) -> p k t", k=4), xh[at].bitcast(F32),
                                      ALU.subtract).then_inc(s_xhl, 1)

        early.close()

        LISTS = 2 * PH
        TG = 8
        HT = P // 2
        STEPS = HT // TG
        IT = 4
        TURNS = PK // IT
        fence = ExitStack()
        sb("place_of_parts", [P, 2 * KD * S], on=fence)
        p6 = ExitStack()
        ub = sb("ub", [P, IT, D], on=p6)
        uTh = sb("uTh", [P, 2, KD, P], F32R, on=p6)
        uTl = sb("uTl", [P, 2, KD, P], F32R, on=p6)
        hb = sb("hb", [P, IT, S], on=p6)
        ss = sb("ss", [P, LISTS, PK], on=p6)
        sv = sb("sv", [P, LISTS, PE_TOP], on=p6)
        si = sb("si", [P, LISTS, PE_TOP], U32, on=p6)
        sif = sb("sif", [P, LISTS, PE_TOP], on=p6)
        cand = sb("cand", [P, PH * PE_TOP, PE_TOP], on=p6)
        best = sb("best", [P, PH, PE_TOP], on=p6)
        pos = sb("pos", [P, PH, PE_TOP], U32, on=p6)
        pab = sb("pab", [P, 2, PH, PE_TOP], U32, on=p6)
        pabf = sb("pabf", [P, 2, PH, PE_TOP], on=p6)
        picks = sb("picks", [P, 3, PH, PE_TOP], on=p6)
        gs = sb("gs", [P, 2, PH], on=p6)
        pkT = sb("pkT", [P, 2, 3, P], on=p6)
        gh = sb("gh", [P, 2, P], F32R, on=p6)
        gl = sb("gl", [P, 2, P], F32R, on=p6)
        iota = sb("iota", [P, P], on=p6)
        oh = sb("oh", [P, 2, TG, P], F32R, on=p6)
        ohj = sb("ohj", [P, 2, TG, P], on=p6)
        ogh = sb("ogh", [P, 2, TG, P], F32R, on=p6)
        ogl = sb("ogl", [P, 2, TG, P], F32R, on=p6)
        stg = sb("stg", [P, PK, HT], on=p6)
        p6.close()
        fence.close()
        p7 = ExitStack()
        wf = sb("wf", [P, 4, S], on=p7)
        wh = sb("wh", [P, 2, 4, S], F32R, on=p7)
        wl = sb("wl", [P, 2, 4, S], F32R, on=p7)
        vh = sb("vh", [P, 2, 4, D], F32R, on=p7)
        vb = sb("vb", [P, 2, 4, D], on=p7)
        vl = sb("vl", [P, 2, 4, D], F32R, on=p7)
        gb = sb("gb", [P, 2, 2 * TT, 4 * HT], on=p7)
        hg = sb("hg", [P, 2, 4, S], on=p7)
        p7.close()

        s_u = [sem(f"u_loaded{n}") for n in range(IT)]
        ut = l0("peer_u").rearrange("(i j) d -> j i d", j=PK)
        s_skt = sem("subkeys_turned")
        s_skT = sem("subkeys_in_place")
        s_qp = sem("peer_queries")
        s_qpd = sem("peer_queries_in_place")

        with nc.Block() as block:
            @block.sync
            def _(sp):
                for r in range(IT):
                    sp.dma_start(ub[:, r, :], ut[r]).then_inc(s_u[r], 16)

            @block.tensor
            def _(pe):
                pe.wait_ge(s_sk, 16)
                for n in range(2):
                    for h in range(4):
                        last = pe.transpose(bank[n][:, h * P:(h + 1) * P],
                                            sk[:, 2 * (4 * n + h):2 * (4 * n + h) + 2].rearrange("p c d -> p (c d)"), ident[:])
                    last.then_inc(s_skt, 1)
                pe.wait_ge(s_wq, 16)
                for h in range(PH):
                    if h >= 4:
                        pe.wait_ge(s_qpd, h - 3)
                    for k in range(KD):
                        last = pe.matmul(bank[2 + h % 4][:], wq[:, k, h * P:(h + 1) * P], x1T[:, k, :],
                                         start=k == 0, stop=k == KD - 1)
                    last.then_inc(s_qp, 1)

            @block.scalar
            def _(act):
                for h in range(PH):
                    act.wait_ge(s_qp, h + 1)
                    act.activation(qp[:, h, :], bank[2 + h % 4][:], ACT.Copy).then_inc(s_qpd, 1)

            @block.vector
            def _(dve):
                for n in range(2):
                    dve.wait_ge(s_skt, n + 1)
                    dve.tensor_copy(skT[:, 4 * n:4 * n + 4, :], bank[n][:].rearrange("p (h k) -> p h k", h=4)).then_inc(s_skT, 1)

        gates = nc.dram_tensor("gates", [2 * TT, P, PK, HT], F32, kind="Internal").ap()
        hidden = nc.dram_tensor("hidden", [PK // 2, P, 2, S], F32, kind="Internal").ap()
        SEQ = [("pick", 0, 0), ("pick", 0, 1)]
        for t_ in range(TT):
            for part_ in range(2):
                SEQ.append(("gates", 2 * t_ + part_))
                SEQ.append(("pick", t_ + 1, part_) if t_ + 1 < TT else ("only", 1 if part_ == 0 else None))
        PICK_TURNS = 2
        used = sum({"pick": PICK_TURNS, "gates": 1, "only": 1}[s[0]] for s in SEQ[:-1])
        SEQ[-1] = ("only", TURNS - used)

        def turns_of(s):
            return {"pick": PICK_TURNS, "gates": 1, "only": s[1]}[s[0]]

        JG = 4
        NG = PK // JG
        s_v = [sem(f"v_loaded{n}") for n in range(2)]
        vg = l0("peer_v").rearrange("(i g j) d -> g i (j d)", i=P, j=JG)

        s_io = sem("counters_made")
        s_ss = sem("peer_scores")
        s_ssd = sem("peer_scores_in_place")
        s_v6 = sem("dve_steps_6")
        s_dif = sem("best_less_maximum")
        s_gex = sem("gate_exponentials")
        s_pk = sem("picks_made")
        s_pkt = sem("picks_turned")
        s_pkT = sem("picks_in_place")
        s_hot = sem("one_hots")
        s_ogh = sem("one_hots_by_high_gate")
        s_ogl = sem("one_hots_by_low_gate")
        s_gp = sem("gates_multiplied")
        s_ge = sem("gates_staged")
        s_gw = sem("gates_stored")
        s_t = sem("experts_turned")
        s_ua = sem("turned_high_parts")
        s_ud = sem("turned_low_parts")
        s_h = sem("experts_multiplied")
        s_hr = sem("experts_gelu")
        s_hs = [sem(f"hidden_stored{n}") for n in range(2)]

        with nc.Block() as block:
            @block.sync
            def _(sp):
                def store(m, q):
                    sp.wait_ge(s_hr, IT * m + 2 * q + 4)
                    sp.dma_start(hidden[2 * m + q], hb[:, 2 * q:2 * q + 2, :]).then_inc(s_hs[q], 16)

                with sp.Fori(0, TURNS - 1) as m:
                    for r in range(IT):
                        sp.wait_ge(s_t, IT * m + r + 1)
                        sp.dma_start(ub[:, r, :], ut[IT * (m + 1) + r]).then_inc(s_u[r], 16)
                        if r == 2:
                            store(m, 0)
                    store(m, 1)
                store(TURNS - 1, 0)
                store(TURNS - 1, 1)
                for q in range(2):
                    sp.wait_ge(s_hs[q], 16 * (TURNS + 1))

            @block.gpsimd
            def _(pool):
                pool.iota(iota[:], [[1, P]], base=0, channel_multiplier=0, allow_small_or_imprecise_dtypes=True).then_inc(s_io, 1)
                pool.sem_inc(s_ogh, 2)
                for t in range(TT):
                    pool.wait_ge(s_pkT, t + 1)
                    with pool.Fori(0, STEPS) as i:
                        for o in range(2):
                            n = 2 * STEPS * t + 2 * i + o
                            pool.wait_ge(s_hot, 2 * n + 2)
                            pool.wait_ge(s_gp, n + 1)
                            g = gh[:, t % 2, bass.ds((2 * i + o) * TG, TG)].bitcast(F32)
                            if o == 1:
                                low = gl[:, t % 2, bass.ds((2 * i + o) * TG, TG)].bitcast(F32)
                                pool.tensor_tensor(ogl[:, o], ohj[:, o], low.unsqueeze(2).broadcast_to([P, TG, P]), ALU.mult)
                            pool.tensor_tensor(ogh[:, o], ohj[:, o], g.unsqueeze(2).broadcast_to([P, TG, P]),
                                               ALU.mult).then_inc(s_ogh, 1)

            @block.scalar
            def _(act):
                act.sem_inc(s_ge, 2)
                act.sem_inc(s_hr, 2)

                def take(n, r):
                    act.wait_ge(s_t, n + 1)
                    act.wait_ge(s_h, n + 1)
                    for q in range(2):
                        last = act.activation(uTh[:, r % 2, 4 * q:4 * q + 4, :], bank[q][:].rearrange("p (k i) -> p k i", k=4), ACT.Copy)
                    last.then_inc(s_ua, 1)

                def tile(m, r, last=False, between=None):
                    n = IT * m + r
                    if not last:
                        take(n + 1, (r + 1) % IT)
                    if between:
                        between()
                    act.wait_ge(s_h, n + 3)
                    act.wait_ge(s_hs[r // 2], 16 * m + 16)
                    act.activation(hb[:, r, :], bank[2 + r % 2][:], ACT.Gelu_apprx_tanh).then_inc(s_hr, 1)

                def turns(m, count, final=False):
                    if count - final > 0:
                        with act.Fori(0, count - final) as i:
                            for r in range(IT):
                                tile(m + i, r)
                    if final:
                        for r in range(IT):
                            tile(TURNS - 1, r, last=r == IT - 1)

                def bring(t, c):
                    for n in range(2):
                        act.wait_ge(s_ss, 4 * t + 2 * c + n + 1)
                        act.activation(ss[:, 8 * c + 4 * n:8 * c + 4 * n + 4, :], bank[6 + n][:].rearrange("p (h k) -> p h k", h=4),
                                       ACT.Copy).then_inc(s_ssd, 1)

                take(0, 0)
                m = 0
                for s in SEQ:
                    if s[0] == "pick":
                        _, t, part = s
                        if part == 0:
                            if t:
                                act.wait_ge(s_pk, t)
                            bring(t, 0)
                            bring(t, 1)
                        turns(m, PICK_TURNS)
                        if part == 1:
                            act.wait_ge(s_dif, t + 1)
                            act.activation(picks[:, 2], picks[:, 2], ACT.Exp).then_inc(s_gex, 1)
                    elif s[0] == "gates":
                        k = s[1]
                        if k:
                            act.wait_ge(s_gw, 16 * k)

                        def stage(r):
                            for i in range(2):
                                n = STEPS * k + 2 * r + i
                                act.wait_ge(s_gp, 2 + n + 1)
                                for b in range(2):
                                    dst = stg[:, :, (2 * r + i) * TG + 4 * b:(2 * r + i) * TG + 4 * b + 4].rearrange("p j t -> p t j")
                                    act.activation(dst, bank[4 + b][:].rearrange("p (t j) -> p t j", t=4), ACT.Copy).then_inc(s_ge, 1)

                        for r in range(IT):
                            tile(m, r, between=lambda: stage(r))
                        act.wait_ge(s_ge, 2 + 2 * STEPS * (k + 1))
                        act.dma_start(gates[k].rearrange("i j t -> i (j t)"), stg[:].rearrange("p j t -> p (j t)")).then_inc(s_gw, 16)
                        if k == 2 * TT - 1:
                            for o in range(2):
                                act.dma_start(vb[:, o].rearrange("p j d -> p (j d)"), vg[o]).then_inc(s_v[o], 16)
                    else:
                        turns(m, s[1], final=m + s[1] == TURNS)
                    m += turns_of(s)
                act.wait_ge(s_gw, 16 * 2 * TT)

            @block.tensor
            def _(pe):
                pe.sem_inc(s_gp, 2)
                pe.sem_inc(s_h, 2)
                for q in range(2):
                    pe.sem_inc(s_hs[q], 16)

                def turn(m, r):
                    n = IT * m + r
                    pe.wait_ge(s_u[r], 16 * m + 16)
                    pe.wait_ge(s_ud, n)
                    for k in range(KD):
                        last = pe.transpose(bank[k // 4][:, (k % 4) * P:(k % 4 + 1) * P], ub[:, r, k * P:(k + 1) * P], ident[:])
                    last.then_inc(s_t, 1)

                def tile(m, r, last_tile=False, between=None):
                    n = IT * m + r
                    if r + 1 < IT:
                        turn(m, r + 1)
                    elif not last_tile:
                        turn(m + 1, 0)
                    if between:
                        between()
                    pe.wait_ge(s_ud, n + 1)
                    pe.wait_ge(s_hr, n + 1)
                    for k in range(KD):
                        for q, (x, y) in enumerate(((uTh, xh), (uTh, xl), (uTl, xh))):
                            last = pe.matmul(bank[2 + r % 2][:], x[:, r % 2, k, :], y[:, k, :],
                                             start=k == 0 and q == 0, stop=k == KD - 1 and q == 2)
                    last.then_inc(s_h, 1)

                def turns(m, count, final=False):
                    if count - final > 0:
                        with pe.Fori(0, count - final) as i:
                            for r in range(IT):
                                tile(m + i, r)
                    if final:
                        for r in range(IT):
                            tile(TURNS - 1, r, last_tile=r == IT - 1)

                def scores(t, c):
                    for n in range(2):
                        if t or c:
                            pe.wait_ge(s_ssd, 4 * t + 2 * (c - 1) + n + 1)
                        if t and c == 0 and n == 0:
                            pe.wait_ge(s_pkT, t)
                        for h in range(4):
                            hh = 4 * n + h
                            last = pe.matmul(bank[6 + n][:, h * PK:(h + 1) * PK], qp[c * HD:(c + 1) * HD, hh, t * P:(t + 1) * P],
                                             skT[c * HD:(c + 1) * HD, hh, :], start=True, stop=True)
                        last.then_inc(s_ss, 1)

                turn(0, 0)
                m = 0
                for s in SEQ:
                    if s[0] == "pick":
                        _, t, part = s
                        if part == 0:
                            scores(t, 0)
                            scores(t, 1)
                        turns(m, PICK_TURNS)
                        if part == 1:
                            pe.wait_ge(s_pk, t + 1)
                            for n in range(3):
                                last = pe.transpose(bank[6][:, n * P:(n + 1) * P], picks[:, n].rearrange("p h k -> p (h k)"), ident[:])
                            last.then_inc(s_pkt, 1)
                    elif s[0] == "gates":
                        k = s[1]

                        def steps(r):
                            for i in range(2):
                                n, o = STEPS * k + 2 * r + i, i
                                pe.wait_ge(s_ogh, 2 + n + 1)
                                if i == 0:
                                    pe.wait_ge(s_ogl, n // 2 + 1)
                                for b in range(2):
                                    pe.wait_ge(s_ge, 2 * n + b + 1)
                                    for w in range(4):
                                        at = bank[4 + b][:, w * P:(w + 1) * P]
                                        pe.matmul(at, oh[:, o, 4 * b + w, :], ogh[:, o, 4 * b + w, :], start=True, stop=False)
                                        last = pe.matmul(at, oh[:, o, 4 * b + w, :], ogl[:, o, 4 * b + w, :], start=False, stop=True)
                                last.then_inc(s_gp, 1)

                        for r in range(IT):
                            tile(m, r, between=lambda: steps(r))
                    else:
                        turns(m, s[1], final=m + s[1] == TURNS)
                    m += turns_of(s)

            @block.vector
            def _(dve):
                link = chained(dve, s_v6)
                LOW = -3.0e38

                def take(n, r):
                    dve.wait_ge(s_ua, n + 1)
                    for q in range(2):
                        h = slice(4 * q, 4 * q + 4)
                        last = dve.tensor_tensor(uTl[:, r % 2, h, :], bank[q][:].rearrange("p (k i) -> p k i", k=4),
                                                 uTh[:, r % 2, h, :].bitcast(F32), ALU.subtract)
                    last.then_inc(s_ud, 1)

                def top16(vals, idx, lst):
                    link(dve.max(vals[:, 0:8], lst))
                    dve.max_index(idx[:, 0:8], vals[:, 0:8], lst)
                    link(dve.match_replace(lst, vals[:, 0:8], lst, LOW))
                    link(dve.max(vals[:, 8:16], lst))
                    link(dve.max_index(idx[:, 8:16], vals[:, 8:16], lst))

                def lists(t, c, h):
                    dve.wait_ge(s_ssd, 4 * t + 2 * c + h // 4 + 1)
                    l = PH * c + h
                    top16(sv[:, l, :], si[:, l, :], ss[:, l, :])

                def candidates():
                    link(dve.tensor_copy(sif[:], si[:]))
                    link(dve.tensor_tensor(cand[:].rearrange("p (h a) b -> p h a b", h=PH),
                                           sv[:, 0:PH].unsqueeze(3).broadcast_to([P, PH, PE_TOP, PE_TOP]),
                                           sv[:, PH:].unsqueeze(2).broadcast_to([P, PH, PE_TOP, PE_TOP]), ALU.add))

                def places():
                    link(dve.tensor_scalar(pab[:, 0], pos[:], 4, None, ALU.logical_shift_right))
                    link(dve.tensor_scalar(pab[:, 1], pos[:], 15, None, ALU.bitwise_and))
                    link(dve.tensor_copy(pabf[:], pab[:]))

                def keys(c):
                    e4 = cand[:].rearrange("p (h k) a -> p h k a", h=PH)
                    link(dve.tensor_tensor(cand[:], pabf[:, c].rearrange("p h k -> p (h k)").unsqueeze(2).broadcast_to([P, PH * PE_TOP, PE_TOP]),
                                           iota[:, 0:PE_TOP].unsqueeze(1).broadcast_to([P, PH * PE_TOP, PE_TOP]), ALU.is_equal))
                    link(dve.tensor_tensor(e4, e4, sif[:, c * PH:(c + 1) * PH].unsqueeze(2).broadcast_to([P, PH, PE_TOP, PE_TOP]), ALU.mult))
                    link(dve.tensor_reduce(picks[:, c].rearrange("p h k -> p (h k)"), cand[:], AX.X, ALU.add))

                def softmax_1():
                    link(dve.tensor_tensor(picks[:, 2], best[:], best[:, :, 0:1].broadcast_to([P, PH, PE_TOP]), ALU.subtract))
                    dve.sem_inc(s_dif, 1)

                def softmax_2(t):
                    dve.wait_ge(s_gex, t + 1)
                    link(dve.tensor_reduce(gs[:, 0], picks[:, 2], AX.X, ALU.add))
                    link(dve.reciprocal(gs[:, 1], gs[:, 0]))
                    link(dve.tensor_tensor(picks[:, 2], picks[:, 2], gs[:, 1].unsqueeze(2).broadcast_to([P, PH, PE_TOP]), ALU.mult))
                    dve.sem_inc(s_pk, 1)

                def place(t):
                    o = t % 2
                    dve.wait_ge(s_pkt, t + 1)
                    if t >= 2:
                        dve.wait_ge(s_ogh, 2 + 2 * STEPS * (t - 1))
                    link(dve.tensor_copy(pkT[:, o], bank[6][:, 0:3 * P].rearrange("p (n t) -> p n t", n=3)))
                    link(dve.tensor_copy(gh[:, o], pkT[:, o, 2]))
                    dve.tensor_tensor(gl[:, o], pkT[:, o, 2], gh[:, o].bitcast(F32), ALU.subtract).then_inc(s_pkT, 1)
                    dve.wait_ge(s_pkT, t + 1)

                def spread(t, n, half_step, o):
                    at = slice(half_step * TG, (half_step + 1) * TG)
                    row3 = iota[:].unsqueeze(1).broadcast_to([P, TG, P])
                    dve.wait_ge(s_gp, n + 1)
                    dve.tensor_tensor(oh[:, o], row3, pkT[:, t % 2, 0, at].unsqueeze(2).broadcast_to([P, TG, P]),
                                      ALU.is_equal).then_inc(s_hot, 1)
                    dve.wait_ge(s_ogh, n + 1)
                    dve.tensor_tensor(ohj[:, o], row3, pkT[:, t % 2, 1, at].unsqueeze(2).broadcast_to([P, TG, P]),
                                      ALU.is_equal).then_inc(s_hot, 1)
                    if o == 1:
                        return
                    dve.wait_ge(s_hot, 2 * n + 2)
                    dve.tensor_tensor(ogl[:, o], ohj[:, o], gl[:, t % 2, at].bitcast(F32).unsqueeze(2).broadcast_to([P, TG, P]),
                                      ALU.mult).then_inc(s_ogl, 1)

                dve.wait_ge(s_io, 1)
                take(0, 0)
                m = 0
                for s in SEQ:
                    if s[0] == "pick":
                        _, t, part = s
                        if part == 0:
                            todo = [[lambda l=l: lists(t, l // PH, l % PH) for l in (2 * e, 2 * e + 1)] for e in range(8)]
                        else:
                            cands = [lambda h=h: top16(best[:, h, :], pos[:, h, :],
                                                       cand[:, h * PE_TOP:(h + 1) * PE_TOP, :].rearrange("p a b -> p (a b)")) for h in range(PH)]
                            todo = [[candidates, cands[0]], cands[1:3], cands[3:4], cands[4:6], cands[6:7], [cands[7], softmax_1, places],
                                    [lambda: keys(0)], [lambda: keys(1)]]
                        for e in range(8):
                            for piece in todo[e]:
                                piece()
                            take(IT * m + e + 1, (e + 1) % IT)
                        if part == 1:
                            softmax_2(t)
                            place(t)
                    elif s[0] == "gates":
                        k = s[1]
                        for r in range(-1, IT):
                            if r >= 0:
                                take(IT * m + r + 1, (r + 1) % IT)
                            if r + 1 < IT:
                                for i in range(2):
                                    e = 2 * (r + 1) + i
                                    spread(k // 2, STEPS * k + e, STEPS * (k % 2) + e, i)
                    else:
                        last = m + s[1] == TURNS
                        if s[1] - last > 0:
                            with dve.Fori(0, s[1] - last) as i:
                                for r in range(IT):
                                    take(IT * (m + i) + r + 1, (r + 1) % IT)
                        if last:
                            for r in range(IT - 1):
                                take(IT * (TURNS - 1) + r + 1, (r + 1) % IT)
                    m += turns_of(s)

        s_g = [sem(f"gates_and_hidden_loaded{n}") for n in range(2)]
        s_vh = sem("v_high_parts")
        s_vl = sem("v_low_parts")
        s_w = sem("experts_weighed")
        s_wh = sem("weighed_high_parts")
        s_wl = sem("weighed_low_parts")
        s_y = sem("sums_made")
        s_ya = sem("sums_added")
        s_sc7 = sem("residual_scaled")
        gg = gates.rearrange("t i (g j) k -> g i t (j k)", j=JG)
        hh_ = hidden.rearrange("(g a) i b s -> g i a (b s)", a=JG // 2)

        with nc.Block() as block:
            @block.sync
            def _(sp):
                def load_g(g, o):
                    sp.dma_start(gb[:, o], gg[g]).then_inc(s_g[o], 16)
                    sp.dma_start(hg[:, o].rearrange("p (a b) s -> p a (b s)", b=2), hh_[g]).then_inc(s_g[o], 16)

                def load_v(g, o):
                    sp.dma_start(vb[:, o].rearrange("p j d -> p (j d)"), vg[g]).then_inc(s_v[o], 16)

                for g in range(2):
                    load_g(g, g)
                with sp.Fori(0, NG // 2 - 1) as i:
                    for o in range(2):
                        g = 2 * i + o
                        sp.wait_ge(s_w, JG * g + JG)
                        load_g(g + 2, o)
                        sp.wait_ge(s_vl, JG * g + JG)
                        load_v(g + 2, o)

            @block.tensor
            def _(pe):
                pe.sem_inc(s_y, 16)

                def group(g, o):
                    pe.wait_ge(s_wl, JG * g + 2 * JG)
                    pe.wait_ge(s_vl, JG * g + JG)
                    for m in range(8):
                        t, c = m // 2, m % 2
                        pe.wait_ge(s_ya, 8 * g + m + 1)
                        for j in range(JG):
                            for q, (x, y) in enumerate(((wh, vh), (wh, vl), (wl, vh))):
                                last = pe.matmul(bank[m][:], x[:, o, j, t * P:(t + 1) * P], y[:, o, j, c * 512:(c + 1) * 512],
                                                 start=j == 0 and q == 0, stop=j == JG - 1 and q == 2)
                        last.then_inc(s_y, 1)

                with pe.Fori(0, NG // 2) as i:
                    for o in range(2):
                        group(2 * i + o, o)

            @block.scalar
            def _(act):
                with act.Fori(0, NG // 2) as i:
                    for o in range(2):
                        g = 2 * i + o
                        act.wait_ge(s_v[o], 16 * i + 16)
                        act.wait_ge(s_y, 8 * g + 8)
                        for j in range(JG):
                            act.activation(vh[:, o, j, :], vb[:, o, j, :], ACT.Copy).then_inc(s_vh, 1)
                            act.wait_ge(s_w, JG * g + j + 1)
                            act.activation(wh[:, o, j, :], wf[:, j, :], ACT.Copy).then_inc(s_wh, 1)

            @block.gpsimd
            def _(pool):
                pool.sem_inc(s_wl, JG)
                with pool.Fori(0, NG // 2) as i:
                    for o in range(2):
                        g = 2 * i + o
                        for j in range(JG):
                            pool.wait_ge(s_vh, JG * g + j + 1)
                            pool.tensor_tensor(vl[:, o, j, :], vb[:, o, j, :], vh[:, o, j, :].bitcast(F32), ALU.subtract).then_inc(s_vl, 1)
                            pool.wait_ge(s_wh, JG * g + j + 1)
                            pool.tensor_tensor(wl[:, o, j, :], wf[:, j, :], wh[:, o, j, :].bitcast(F32), ALU.subtract).then_inc(s_wl, 1)

            @block.vector
            def _(dve):
                dve.tensor_scalar(x1[:], x1[:], DN_ALPHA, None, ALU.mult).then_inc(s_sc7, 1)
                dve.wait_ge(s_sc7, 1)
                dve.sem_inc(s_ya, 8)

                def prepare(g, half, o, j):
                    if j == 0:
                        dve.wait_ge(s_g[o], 32 * half + 32)
                    dve.wait_ge(s_wl, JG * g + j + 1)
                    dve.tensor_tensor(wf[:, j, :].rearrange("p (t k) -> p t k", k=HT),
                                      hg[:, o, j, :].rearrange("p (t k) -> p t k", k=HT), gb[:, o, :, j * HT:(j + 1) * HT],
                                      ALU.mult).then_inc(s_w, 1)

                def add(g, m):
                    t, h = m // 2, slice((m % 2) * 512, (m % 2 + 1) * 512)
                    dve.wait_ge(s_y, 8 * g + m + 17)
                    dve.tensor_tensor(x1[:, t, h], x1[:, t, h], bank[m][:], ALU.add).then_inc(s_ya, 1)

                def group(g, ahead=None):
                    dve.wait_ge(s_ya, 8 * g + 8)
                    for j in range(JG):
                        if ahead:
                            prepare(g + 1, *ahead, j)
                        add(g, 2 * j)
                        add(g, 2 * j + 1)

                for j in range(JG):
                    prepare(0, 0, 0, j)
                with dve.Fori(0, NG // 2 - 1) as i:
                    group(2 * i, (i, 1))
                    group(2 * i + 1, (i + 1, 0))
                group(NG - 2, (NG // 2 - 1, 1))
                group(NG - 1)

        p8 = ExitStack()
        ln2 = sb("ln2", [P, 2, D], on=p8)
        st8 = sb("st8", [P, TT, 2, 6], on=p8)
        mv8 = sb("mv8", [P, TT, 2], on=p8)
        rs8 = sb("rs8", [P, TT], on=p8)
        p8.close()

        s_ln = sem("ln2_loaded")
        s_v8 = sem("dve_steps_8")
        s_var8 = sem("variances_8")
        s_std8 = sem("deviations_8")
        s_fin = sem("tiles_finished")
        s_out = sem("output_stored")

        with nc.Block() as block:
            @block.sync
            def _(sp):
                sp.dma_start(ln2[:, 0, :], row("ln2_g", 0, D)).then_inc(s_ln, 16)
                sp.dma_start(ln2[:, 1, :], row("ln2_b", 0, D)).then_inc(s_ln, 16)
                for t in range(TT):
                    sp.wait_ge(s_fin, t + 1)
                    sp.dma_start(out[0, t * P:(t + 1) * P, :], x1[:, t, :]).then_inc(s_out, 16)
                sp.wait_ge(s_out, 16 * TT)

            @block.scalar
            def _(act):
                act.wait_ge(s_var8, 1)
                act.activation(rs8[:], mv8[:, :, 1], ACT.Sqrt).then_inc(s_std8, 1)

            @block.vector
            def _(dve):
                link = chained(dve, s_v8)
                for t in range(TT):
                    for n in range(2):
                        last = dve.bn_stats(st8[:, t, n, :], x1[:, t, n * 512:(n + 1) * 512])
                    link(last)
                for t in range(TT):
                    last = dve.bn_aggr(mv8[:, t, :], st8[:, t].rearrange("p n s -> p (n s)"))
                link(last)
                dve.tensor_scalar(mv8[:, :, 1], mv8[:, :, 1], LN_EPS, None, ALU.add).then_inc(s_var8, 1)
                dve.wait_ge(s_std8, 1)
                link(dve.reciprocal(rs8[:], rs8[:]))
                dve.wait_ge(s_ln, 32)
                for t in range(TT):
                    link(dve.tensor_scalar(x1[:, t, :], x1[:, t, :], mv8[:, t, 0:1], rs8[:, t:t + 1], ALU.subtract, ALU.mult))
                    link(dve.tensor_tensor(x1[:, t, :], x1[:, t, :], ln2[:, 0, :], ALU.mult))
                    dve.tensor_tensor(x1[:, t, :], x1[:, t, :], ln2[:, 1, :], ALU.add).then_inc(s_fin, 1)


_INS = ['x', 'w_in', 'b_in', 'ssm_a_re', 'ssm_a_im', 'ssm_log_dt', 'ssm_b_re', 'ssm_b_im', 'ssm_c_re', 'ssm_c_im',
        'ssm_d', 'w_glu', 'w_up_ssm', 'nsa_pe_k', 'nsa_w1_k', 'nsa_w2_k', 'nsa_pe_v', 'nsa_w1_v', 'nsa_w2_v',
        'w_up_nsa', 'w_out', 'ln1_g', 'ln1_b', 'peer_w_q', 'peer_subkeys', 'peer_u', 'peer_v', 'ln2_g', 'ln2_b']


def kernel(**inputs):
    import numpy as _np
    import concourse.bacc as _bacc
    from concourse import mybir as _mybir
    from concourse.bass_utils import run_bass_kernel_spmd as _run

    nc = _bacc.Bacc("TRN2", target_bir_lowering=False, num_devices=1)
    arrays, args = {}, {}
    for name in _INS:
        v = _np.ascontiguousarray(inputs[name])
        arrays[f"in_{name}_dram"] = v
        args[name] = nc.dram_tensor(f"in_{name}_dram", v.shape, _mybir.dt.from_np(v.dtype), kind="ExternalInput").ap()
    out = nc.dram_tensor("out_0_dram", (1, S, D), F32, kind="ExternalOutput").ap()
    build(nc, args, out)
    r = _run(nc, [arrays], core_ids=[0])
    return r.results[0]["out_0_dram"]
```

```python
from contextlib import ExitStack
import math

import numpy as np

import concourse.bass as bass
from concourse import mybir

F32 = mybir.dt.float32
F32R = mybir.dt.float32r
U32 = mybir.dt.uint32
ALU = mybir.AluOpType
ACT = mybir.ActivationFunctionType
AX = mybir.AxisListType

P = 128
D = 1024
S = 512
KD = D // P
TT = S // P
SSM = D // 2
SG, SH, SP = 32, 16, 64
NPAIR = SG // 2
CH = SSM // P
HEADS, KVG, HD = 8, 2, 64
HPG = HEADS // KVG
CB, CS = 32, 16
NCMP = (S - CB) // CS + 1
NC32 = 32
GATES = 3 * HEADS
PH, PK, PE_TOP = 8, 128, 16
NEG = -1e30
DN_ALPHA = 2.0 ** 0.25
LN_EPS = 1e-5

C_U, C_Q = 0, SSM
C_KC = C_Q + SSM
C_VC, C_KS, C_VS, C_KW, C_VW, C_G = (C_KC + P * n for n in range(1, 7))
C_M = C_G + GATES
C_END = C_M + 2 * D
W_GROUPS = [(0, 512), (512, 1024), (1024, 1536), (1536, C_M)] + [(C_M + 512 * n, C_M + 512 * (n + 1)) for n in range(4)]
W_RING = 3
G_Q = 1
R_U, R_Q, R_KC, R_VC, R_KS, R_KW, R_M, R_D = 0, 4, 8, 9, 10, 11, 12, 28
PI2_A = 6.28125
PI2_B = float(np.round((2 * math.pi - PI2_A) * 2 ** 20) / 2 ** 20)
PI2_C = 2 * math.pi - PI2_A - PI2_B
ROUND = 1.5 * 2.0 ** 23

UNITS = (
    [("u", 0, P * c, c) for c in range(4)]
    + [("q", 1, P * c, c) for c in range(4)]
    + [("kc", 2, 0, 0), ("vc", 2, P, 0), ("ks", 2, 2 * P, 0), ("kw", 3, 0, 0)]
    + [("vg", 3, 0, t) for t in range(TT)]
    + [("m", 4 + c // 4, P * (c % 4), c) for c in range(6)]
    + [("prm", None, None, 0), ("ct", None, None, 0), ("ct", None, None, 1)]
    + [("m", 4 + c // 4, P * (c % 4), c) for c in range(6, 10)]
    + [("bt", None, None, 0), ("bt", None, None, 1)]
    + [("m", 4 + c // 4, P * (c % 4), c) for c in range(10, 16)]
)
BY_ACT = ("u", "m")
NX = 2 * TT


def build(nc: bass.Bass, a, out, dbg=None):
    l0 = lambda name: a[name][0]
    ctx = ExitStack()
    with ctx:
        def sb(name, shape, dt=F32, on=ctx):
            return on.enter_context(nc.sbuf_tensor(name, shape, dt))

        def sem(name):
            return ctx.enter_context(nc.semaphore(name))

        def spread(vec, n):
            return vec.rearrange("(a n) -> a n", a=1).broadcast_to([P, n])

        bank = [ctx.enter_context(nc.psum_tensor(f"bank{i}", [P, 512], F32)) for i in range(8)]

        def chained(eng, sem_):
            n = [0]

            def link(ins):
                n[0] += 1
                ins.then_inc(sem_, 1)
                eng.wait_ge(sem_, n[0])
            return link

        ident = sb("ident", [P, P])
        col = sb("col", [P, 32])
        w_parts = ExitStack()
        wul = sb("wul", [P, 4, KD, P], F32R, on=w_parts)
        wuh = sb("wuh", [P, 4, KD, P], F32R, on=w_parts)
        w_parts.close()
        x1 = sb("x1", [P, TT, D])
        qp = sb("qp", [P, PH, S])
        skT = sb("skT", [P, PH, PK])
        parts = ExitStack()
        xh = sb("xh", [P, KD, S], F32R, on=parts)
        xl = sb("xl", [P, KD, S], F32R, on=parts)
        parts.close()
        late = ExitStack()
        sb("places_below_w_q", [P, 2 * KD * S + 8 * S], on=late)
        wq = sb("wq", [P, KD, D], on=late)
        late.close()
        x_parts = ExitStack()
        sb("places_below_x_parts", [P, 2 * KD * S + 16 * S], on=x_parts)
        xTh = sb("xTh", [P, KD, S], F32R, on=x_parts)
        xTl = sb("xTl", [P, KD, S], F32R, on=x_parts)
        x_parts.close()
        early = ExitStack()
        uT = sb("uT", [P, CH, S], on=early)
        qT = sb("qT", [P, 4, S], on=early)
        kT = sb("kT", [P, 4, S], on=early)
        vN = sb("vN", [P, TT, 2 * P + GATES], on=early)
        REST = 2 * KD * S - 12 * S - TT * (2 * P + GATES)
        sb("rest_of_parts", [P, REST - 2 * NPAIR * SH - 7 * NPAIR - 2 * P], on=early)
        sa = sb("sa", [NPAIR, 2, P], on=early)
        braw = sb("braw", [P, 2, NPAIR, SH], on=early)
        prT = sb("prT", [P, 5, NPAIR], on=early)
        pw = sb("pw", [P, 2, NPAIR], on=early)
        gmT = sb("gmT", [P, 16, S], on=early)
        gluT = sb("gluT", [P, CH, S], on=early)
        nsaT = sb("nsaT", [P, CH, S], on=early)
        x1T = sb("x1T", [P, KD, S], on=early)

        p1 = ExitStack()
        xN = x1
        xT = gmT[:, 8:16, :]
        wr = sb("wr", [P, W_RING, KD, 512], on=p1)
        rows = sb("rows", [32, P], on=p1)
        vbias = sb("vbias", [P, 2 * P + GATES], on=p1)
        iota_d = sb("iota_d", [P, P], on=p1)
        TA, TB = 16, 32
        sdt = sb("sdt", [NPAIR, 2], on=p1)
        sdtx = sb("sdtx", [NPAIR, 2, SP], on=p1)
        prm = sb("prm", [NPAIR, 5, P], on=p1)
        wp = sb("wp", [P, 4, NPAIR, TB], on=p1)
        wk = wp[0:NPAIR, 0:2].rearrange("p n q b -> p (n q b)").rearrange("p (n s) -> p n s", s=P)
        cw = sb("cw", [P, 2, CH, 2, SP], on=p1)
        eb = cw[:].rearrange("p n c g s -> p n (c g s)").rearrange("p n (q b) -> p n q b", b=TB)
        craw = sb("craw", [P, 2, CH, SP], on=p1)
        ea = craw[:].rearrange("p n c s -> p n (c s)").rearrange("p n (q a) -> p n q a", a=TA)
        bbar = sb("bbar", [P, 2, NPAIR, 2, SH], on=p1)
        bT = sb("bT", [P, 2, CH, P], on=p1)
        cT = skT[:].rearrange("p (n c) k -> p n c k", n=2)
        half_i = sb("half_i", [P, 1], mybir.dt.int32, on=p1)
        half = sb("half", [P, 2], on=p1)
        p1.close()

        s_x = sem("x_loaded")
        s_rows = sem("rows_loaded")
        s_w = [sem(f"w_in_loaded{n}") for n in range(W_RING)]
        s_iota = sem("iota_made")
        s_id = sem("identity_made")
        s_unit = sem("units_made")
        s_act = sem("units_taken_by_act")
        s_dve = sem("units_taken_by_dve")
        s_par = sem("s5_params_loaded")
        s_bc = sem("s5_b_c_loaded")
        s_a2 = sem("act_steps_2")
        s_prm = sem("params_ready_to_turn")
        s_bbar = sem("b_ready_to_turn")
        s_cw = sem("c_ready_to_turn")
        s_half = sem("halves_made")
        s_s5 = sem("dve_steps_of_s5_params")
        s_wlm = sem("merge_weights_low_parts")
        s_xh = sem("turned_x_high_parts")
        s_xT = sem("turned_x_whole")
        s_wuh = sem("unit_weights_high_parts")
        s_wul = sem("unit_weights_low_parts")

        w_in, b_in = l0("w_in"), l0("b_in")
        taken = [("dve", 0)] * (NX + 1) + [("act" if k in BY_ACT else "dve", 0) for k, *_ in UNITS]
        nth = []
        seen = {"act": 0, "dve": 0}
        for e, _ in taken:
            seen[e] += 1
            nth.append((e, seen[e]))
        w_landed = [16 * sum(KD * KVG if h == G_Q else 1 for h in range(g % W_RING, g + 1, W_RING)) for g in range(len(W_GROUPS))]
        last_unit = {}
        for n, (_, g, _, _) in enumerate(UNITS):
            if g is not None:
                last_unit[g] = NX + 1 + n + 1
        last_unit[2] = last_unit[3]

        AHEAD = 3
        PARTED = [n for n, (kind, *_) in enumerate(UNITS) if kind not in ("vg", "prm", "ct", "bt")]
        FIRST_M = sum(UNITS[n][0] != "m" for n in PARTED)

        def parted_before(m):
            return sum(n < m for n in PARTED)

        def parts_due(m):
            lo, hi = (min(parted_before(x) + AHEAD, len(PARTED)) for x in (m, m + 1))
            return range(lo, hi)

        def raw(u):
            _, g, c0, _ = UNITS[PARTED[u]]
            return wr[:, g % W_RING, :, c0:c0 + P]

        with nc.Block() as block:
            @block.sync
            def _(sp):
                for t in range(TT):
                    sp.dma_start(xN[:, t, :], a["x"][0, t * P:(t + 1) * P, :]).then_inc(s_x, 16)
                sp.dma_start(rows[R_U:R_U + 4, :], b_in[C_U:C_U + SSM].rearrange("(r c) -> r c", c=P)).then_inc(s_rows, 16)
                for g in range(KVG):
                    sp.dma_start(rows[R_Q:R_Q + 4, g * HD:(g + 1) * HD],
                                 b_in[C_Q + 256 * g:C_Q + 256 * (g + 1)].rearrange("(r c) -> r c", c=HD)).then_inc(s_rows, 16)
                for r, c, n in ((R_KC, C_KC, 3), (R_KW, C_KW, 1), (R_M, C_M, 16)):
                    sp.dma_start(rows[r:r + n, :], b_in[c:c + n * P].rearrange("(r c) -> r c", c=P)).then_inc(s_rows, 16)
                sp.dma_start(rows[R_D:R_D + 4, :], l0("ssm_d").rearrange("(r c) -> r c", c=P)).then_inc(s_rows, 16)
                sp.dma_start(vbias[:, 0:P], spread(b_in[C_VS:C_VS + P], P)).then_inc(s_rows, 16)
                sp.dma_start(vbias[:, P:], spread(b_in[C_VW:C_M], P + GATES)).then_inc(s_rows, 16)
                for g, (c0, c1) in enumerate(W_GROUPS):
                    if g == W_RING:
                        sp.dma_start(sa[:, 0, :], l0("ssm_a_re").rearrange("(q g) s -> q (g s)", g=2)).then_inc(s_par, 16)
                        sp.dma_start(sa[:, 1, :], l0("ssm_a_im").rearrange("(q g) s -> q (g s)", g=2)).then_inc(s_par, 16)
                        sp.dma_start(sdt[:], l0("ssm_log_dt").rearrange("(q g) -> q g", g=2)).then_inc(s_par, 16)
                        for n, name in enumerate(("ssm_b_re", "ssm_b_im")):
                            sp.dma_start(braw[:, n], l0(name).rearrange("(q g) s h -> (g s) q h", g=2)).then_inc(s_bc, 16)
                        for n, name in enumerate(("ssm_c_re", "ssm_c_im")):
                            sp.dma_start(craw[:, n], l0(name).rearrange("(c g) h s -> (g h) c s", c=CH)).then_inc(s_bc, 16)
                    if g >= W_RING:
                        sp.wait_ge(s_unit, last_unit[g - W_RING])
                    if g == G_Q:
                        for k in range(KD):
                            for j in range(KVG):
                                sp.dma_start(wr[:, g % W_RING, k].rearrange("p (r j d) -> p j r d", j=KVG, d=HD)[:, j],
                                             w_in[k * P:(k + 1) * P, c0 + 256 * j:c0 + 256 * (j + 1)]
                                             .rearrange("p (r d) -> p r d", d=HD)).then_inc(s_w[g % W_RING], 16)
                        continue
                    sp.dma_start(wr[:, g % W_RING, :, 0:c1 - c0],
                                 w_in[:, c0:c1].rearrange("(k p) c -> p k c", p=P)).then_inc(s_w[g % W_RING], 16)

            @block.gpsimd
            def _(pool):
                pool.iota(iota_d[:], [[1, P]], base=0, channel_multiplier=-1,
                          allow_small_or_imprecise_dtypes=True).then_inc(s_iota, 1)
                pool.wait_ge(s_dve, NX)
                pool.tensor_tensor(xT[:], xTh[:].bitcast(F32), xTl[:].bitcast(F32), ALU.add).then_inc(s_xT, 1)
                pool.iota(half_i[:], [[0, 1]], base=0, channel_multiplier=1).then_inc(s_half, 1)
                pool.memset(bbar[:], 0.0).then_inc(s_half, 1)
                for u in range(FIRST_M, len(PARTED)):
                    pool.wait_ge(s_wuh, u + 1)
                    pool.tensor_tensor(wul[:, u % 4], raw(u), wuh[:, u % 4].bitcast(F32), ALU.subtract).then_inc(s_wlm, 1)

            @block.tensor
            def _(pe):
                pe.wait_ge(s_id, 1)

                def free(n):
                    if n >= 8:
                        e, m = nth[n - 8]
                        pe.wait_ge(s_act if e == "act" else s_dve, m)
                for t in range(TT):
                    pe.wait_ge(s_x, 16 * (TT))
                    for h in range(2):
                        n = 2 * t + h
                        for k in range(4):
                            last = pe.transpose(bank[n][:, k * P:(k + 1) * P],
                                                xN[:, t, (4 * h + k) * P:(4 * h + k + 1) * P], ident[:])
                        last.then_inc(s_unit, 1)
                pe.wait_ge(s_rows, 16 * 9)
                free(NX)
                pe.transpose(bank[NX % 8][:, 0:32], rows[:], ident[0:32, 0:32]).then_inc(s_unit, 1)
                pe.wait_ge(s_dve, NX)
                for m, (kind, g, c0, i) in enumerate(UNITS):
                    n = NX + 1 + m
                    b = bank[n % 8]
                    free(n)
                    if kind == "prm":
                        pe.wait_ge(s_prm, 1)
                        for r in range(5):
                            last = pe.transpose(b[:, r * NPAIR:(r + 1) * NPAIR], prm[:, r, :], ident[0:NPAIR, 0:NPAIR])
                    elif kind in ("bt", "ct"):
                        pe.wait_ge(s_bbar if kind == "bt" else s_cw, 1)
                        for c in range(CH):
                            src = (bbar[:, i, 4 * c:4 * c + 4].rearrange("p q g h -> p (q g h)") if kind == "bt"
                                   else cw[:, i, c].rearrange("p g s -> p (g s)"))
                            last = pe.transpose(b[:, c * P:(c + 1) * P], src, ident[:])
                    elif kind != "vg":
                        u = parted_before(m)
                        if u < FIRST_M:
                            pe.wait_ge(s_wul, u + 1)
                        else:
                            pe.wait_ge(s_wlm, u - FIRST_M + 1)
                        for k in range(KD):
                            for q, (w, x) in enumerate(((wuh, xTh), (wuh, xTl), (wul, xTh))):
                                last = pe.matmul(b[:], w[:, u % 4, k, :], x[:, k, :],
                                                 start=k == 0 and q == 0, stop=k == KD - 1 and q == 2)
                    else:
                        pe.wait_ge(s_w[g % W_RING], w_landed[g])
                        pe.wait_ge(s_xT, 1)
                        w = wr[:, g % W_RING]
                        for k in range(KD):
                            xt = xT[:, k, i * P:(i + 1) * P]
                            w2 = wr[:, 2 % W_RING, k, 3 * P:4 * P]
                            pe.matmul(b[:, 0:P], xt, w2, start=k == 0, stop=k == KD - 1)
                        for k in range(KD):
                            xt = xT[:, k, i * P:(i + 1) * P]
                            last = pe.matmul(b[:, P:2 * P + GATES], xt, w[:, k, P:2 * P + GATES],
                                             start=k == 0, stop=k == KD - 1)
                    last.then_inc(s_unit, 1)

            @block.scalar
            def _(act):
                def high(u):
                    act.wait_ge(s_w[UNITS[PARTED[u]][1] % W_RING], w_landed[UNITS[PARTED[u]][1]])
                    if u >= 4:
                        act.wait_ge(s_unit, NX + 1 + PARTED[u - 4] + 1)
                    act.activation(wuh[:, u % 4], raw(u), ACT.Copy).then_inc(s_wuh, 1)

                link = chained(act, s_a2)

                def s5_step(i):
                    if i == 0:
                        act.wait_ge(s_par, 48)
                        link(act.activation(sdt[:], sdt[:], ACT.Exp))
                    elif i == 1:
                        act.wait_ge(s_s5, 2)
                        link(act.activation(prm[:, 0, :], wk[:, 0, :], ACT.Exp))
                    else:
                        act.wait_ge(s_s5, 9)
                        link(act.activation(wk[:, 3, :], wk[:, 2, :], ACT.Sin))
                        link(act.activation(wk[:, 4, :], wk[:, 2, :], ACT.Sin, scale=0.5))

                for n in range(NX):
                    t, h = n // 2, n % 2
                    act.wait_ge(s_unit, n + 1)
                    act.activation(xTh[:, 4 * h:4 * h + 4, t * P:(t + 1) * P],
                                   bank[n][:].rearrange("p (k t) -> p k t", k=4), ACT.Copy).then_inc(s_xh, 1)
                for u in range(AHEAD):
                    high(u)
                act.wait_ge(s_dve, NX + 1)
                for m, (kind, g, c0, i) in enumerate(UNITS):
                    n = NX + 1 + m
                    for u in parts_due(m):
                        high(u)
                    if kind == "u":
                        act.wait_ge(s_unit, n + 1)
                        act.activation(uT[:, i, :], bank[n % 8][:], ACT.Identity,
                                       bias=col[:, R_U + i:R_U + i + 1]).then_inc(s_act, 1)
                    elif kind == "m":
                        if i < 3:
                            s5_step(i)
                        act.wait_ge(s_unit, n + 1)
                        act.activation(gmT[:, i, :], bank[n % 8][:], ACT.Sigmoid,
                                       bias=col[:, R_M + i:R_M + i + 1]).then_inc(s_act, 1)

            @block.vector
            def _(dve):
                dve.wait_ge(s_iota, 1)
                dve.tensor_scalar(ident[:], iota_d[:], 0.0, None, ALU.is_equal).then_inc(s_id, 1)
                for n in range(NX):
                    t, h = n // 2, n % 2
                    at = (slice(None), slice(4 * h, 4 * h + 4), slice(t * P, (t + 1) * P))
                    dve.wait_ge(s_xh, n + 1)
                    dve.tensor_tensor(xTl[at], bank[n][:].rearrange("p (k t) -> p k t", k=4), xTh[at].bitcast(F32),
                                      ALU.subtract).then_inc(s_dve, 1)
                dve.wait_ge(s_unit, NX + 1)
                dve.tensor_copy(col[:], bank[NX % 8][:, 0:32]).then_inc(s_dve, 1)
                dve.wait_ge(s_dve, NX + 1)

                def low(u):
                    dve.wait_ge(s_wuh, u + 1)
                    dve.tensor_tensor(wul[:, u % 4], raw(u), wuh[:, u % 4].bitcast(F32), ALU.subtract).then_inc(s_wul, 1)

                for u in range(AHEAD):
                    low(u)
                for m, (kind, g, c0, i) in enumerate(UNITS):
                    n = NX + 1 + m
                    b = bank[n % 8]
                    for u in parts_due(m):
                        if u < FIRST_M:
                            low(u)
                    if kind in BY_ACT or kind in ("prm", "ct", "bt"):
                        continue
                    dve.wait_ge(s_unit, n + 1)
                    if kind == "q":
                        ins = dve.tensor_scalar(qT[:, i, :], b[:], col[:, R_Q + i:R_Q + i + 1], HD ** -0.5, ALU.add, ALU.mult)
                    elif kind == "vg":
                        ins = dve.tensor_tensor(vN[:, i, :], b[:, 0:2 * P + GATES], vbias[:], ALU.add)
                    else:
                        j = ("kc", "vc", "ks", "kw").index(kind)
                        ins = dve.tensor_scalar(kT[:, j, :], b[:], col[:, R_KC + j:R_KC + j + 1], None, ALU.add)
                    ins.then_inc(s_dve, 1)

                link = chained(dve, s_s5)
                place_of = {(kind, i): NX + 1 + m for m, (kind, _, _, i) in enumerate(UNITS)}

                def take_turned(kind, dst):
                    for i in range(2):
                        n = place_of[(kind, i)]
                        dve.wait_ge(s_unit, n + 1)
                        dve.tensor_copy(dst[:, i], bank[n % 8][:].rearrange("p (c x) -> p c x", c=CH)).then_inc(s_dve, 1)
                    dve.wait_ge(s_dve, nth[n][1])

                dve.wait_ge(s_a2, 1)
                dtb = sdt[:].unsqueeze(2).broadcast_to([NPAIR, 2, SP])
                w = lambda n: wk[:, n, :]
                link(dve.tensor_copy(sdtx[:], dtb))
                dts = sdtx[:].rearrange("p g s -> p (g s)")
                link(dve.tensor_tensor(w(0), sa[:, 0, :], dts, ALU.mult))
                link(dve.tensor_tensor(w(1), sa[:, 1, :], dts, ALU.mult))
                link(dve.tensor_scalar(w(5), w(1), 1 / (2 * math.pi), ROUND, ALU.mult, ALU.add))
                link(dve.tensor_scalar(w(5), w(5), ROUND, None, ALU.subtract))
                link(dve.scalar_tensor_tensor(w(1), w(5), -PI2_A, w(1), ALU.mult, ALU.add))
                link(dve.scalar_tensor_tensor(w(6), w(5), -PI2_B, w(1), ALU.mult, ALU.add))
                link(dve.scalar_tensor_tensor(w(6), w(5), -PI2_C, w(6), ALU.mult, ALU.add))
                link(dve.tensor_scalar(w(2), w(6), 3.1415925, -3.1415925, ALU.min, ALU.max))
                dve.wait_ge(s_a2, 4)
                link(dve.tensor_tensor(w(5), w(4), w(4), ALU.mult))
                link(dve.tensor_scalar(w(5), w(5), -2.0, 1.0, ALU.mult, ALU.add))
                link(dve.tensor_tensor(w(6), w(5), w(5), ALU.mult))
                link(dve.tensor_tensor(w(7), w(3), w(3), ALU.mult))
                link(dve.tensor_tensor(w(6), w(6), w(7), ALU.add))
                link(dve.tensor_scalar(w(6), w(6), -0.5, 1.5, ALU.mult, ALU.add))
                link(dve.tensor_tensor(prm[:, 1, :], w(5), w(6), ALU.mult))
                link(dve.tensor_tensor(prm[:, 2, :], w(3), w(6), ALU.mult))
                link(dve.tensor_tensor(w(0), prm[:, 0, :], prm[:, 1, :], ALU.mult))
                link(dve.tensor_scalar(w(0), w(0), 1.0, None, ALU.subtract))
                link(dve.tensor_tensor(w(1), prm[:, 0, :], prm[:, 2, :], ALU.mult))
                link(dve.tensor_tensor(w(2), sa[:, 0, :], sa[:, 0, :], ALU.mult))
                link(dve.tensor_tensor(w(3), sa[:, 1, :], sa[:, 1, :], ALU.mult))
                link(dve.tensor_tensor(w(2), w(2), w(3), ALU.add))
                link(dve.reciprocal(w(2), w(2)))
                link(dve.tensor_tensor(w(4), w(0), sa[:, 0, :], ALU.mult))
                link(dve.tensor_tensor(w(5), w(1), sa[:, 1, :], ALU.mult))
                link(dve.tensor_tensor(w(4), w(4), w(5), ALU.add))
                link(dve.tensor_tensor(w(6), w(1), sa[:, 0, :], ALU.mult))
                link(dve.tensor_tensor(w(7), w(0), sa[:, 1, :], ALU.mult))
                link(dve.tensor_tensor(w(6), w(6), w(7), ALU.subtract))
                link(dve.tensor_tensor(prm[:, 3, :], w(4), w(2), ALU.mult))
                link(dve.tensor_tensor(prm[:, 4, :], w(6), w(2), ALU.mult))
                dve.sem_inc(s_prm, 1)
                dve.wait_ge(s_half, 2)
                link(dve.tensor_scalar(half_i[:], half_i[:], 4, 1, ALU.arith_shift_right, ALU.bitwise_and))
                link(dve.tensor_copy(half[:, 1:2], half_i[:]))
                link(dve.tensor_scalar(half[:, 0:1], half[:, 1:2], -1.0, 1.0, ALU.mult, ALU.add))
                dve.wait_ge(s_bc, 64)
                for n in range(2):
                    for g in range(2):
                        link(dve.tensor_scalar(cw[:, n, :, g, :], craw[:, n], half[:, g:g + 1],
                                               1.0 - 2.0 * n, ALU.mult, ALU.mult))
                dve.sem_inc(s_cw, 1)
                n = place_of[("prm", 0)]
                dve.wait_ge(s_unit, n + 1)
                dve.tensor_copy(prT[:], bank[n % 8][:, 0:5 * NPAIR].rearrange("p (n q) -> p n q", n=5)).then_inc(s_dve, 1)
                dve.wait_ge(s_dve, nth[n][1])
                take_turned("ct", cT)
                fr = prT[:, 3, :].unsqueeze(2).broadcast_to([P, NPAIR, SH])
                fi = prT[:, 4, :].unsqueeze(2).broadcast_to([P, NPAIR, SH])
                t = lambda n: wp[:, n, :, 0:SH]
                for n, (x, y, op) in enumerate(((fr, fi, ALU.subtract), (fi, fr, ALU.add))):
                    link(dve.tensor_tensor(t(0), x, braw[:, 0], ALU.mult))
                    link(dve.tensor_tensor(t(1), y, braw[:, 1], ALU.mult))
                    for g in range(2):
                        h = slice(g * SP, (g + 1) * SP)
                        link(dve.tensor_tensor(bbar[h, n, :, g, :], wp[h, 0, :, 0:SH], wp[h, 1, :, 0:SH], op))
                dve.sem_inc(s_bbar, 1)

                def cmul(oc, os, ac, as_, bc, bs, tmp):
                    link(dve.tensor_tensor(tmp(0), ac, bc, ALU.mult))
                    link(dve.tensor_tensor(tmp(1), as_, bs, ALU.mult))
                    link(dve.tensor_tensor(tmp(2), ac, bs, ALU.mult))
                    link(dve.tensor_tensor(tmp(3), as_, bc, ALU.mult))
                    link(dve.tensor_tensor(oc, tmp(0), tmp(1), ALU.subtract))
                    link(dve.tensor_tensor(os, tmp(2), tmp(3), ALU.add))

                def powers(tab, count):
                    link(dve.memset(tab[:, 0, :, 0:1], 1.0))
                    link(dve.memset(tab[:, 1, :, 0:1], 0.0))
                    n = 1
                    while n < count:
                        bc = pw[:, 0, :].unsqueeze(2).broadcast_to([P, NPAIR, n])
                        bs = pw[:, 1, :].unsqueeze(2).broadcast_to([P, NPAIR, n])
                        cmul(tab[:, 0, :, n:2 * n], tab[:, 1, :, n:2 * n], tab[:, 0, :, 0:n], tab[:, 1, :, 0:n],
                             bc, bs, lambda m: wp[:, m, :, 0:n])
                        cmul(pw[:, 0, :], pw[:, 1, :], pw[:, 0, :], pw[:, 1, :], pw[:, 0, :], pw[:, 1, :],
                             lambda m: wp[:, m, :, 0])
                        link(dve.tensor_tensor(wp[:, 0, :, 0], pw[:, 0, :], pw[:, 0, :], ALU.mult))
                        link(dve.tensor_tensor(wp[:, 1, :, 0], pw[:, 1, :], pw[:, 1, :], ALU.mult))
                        link(dve.tensor_tensor(wp[:, 0, :, 0], wp[:, 0, :, 0], wp[:, 1, :, 0], ALU.add))
                        link(dve.tensor_scalar(wp[:, 0, :, 0], wp[:, 0, :, 0], -0.5, 1.5, ALU.mult, ALU.add))
                        link(dve.tensor_tensor(pw[:, 0, :], pw[:, 0, :], wp[:, 0, :, 0], ALU.mult))
                        link(dve.tensor_tensor(pw[:, 1, :], pw[:, 1, :], wp[:, 0, :, 0], ALU.mult))
                        n *= 2

                link(dve.tensor_copy(pw[:], prT[:, 1:3, :]))
                powers(eb, TB)
                take_turned("bt", bT)
                powers(ea, TA)

        p2 = ExitStack()
        et = sb("et", [P, 2, 2, S], on=p2)
        er, br = qp[:, 0:4], qp[:, 4:8]
        zin = sb("zin", [P, 2, S], on=p2)
        z = x1T[:, 0:4].rearrange("p (o n) s -> p o n s", n=2)
        xr = sb("xr", [P, 4, S], on=p2)
        xs = sb("xs", [P, 2, 2, S], on=p2)
        wg, sg = x1, x1T[:, CH:2 * CH]
        p2.close()

        s_wg = sem("w_glu_loaded")
        s_v2 = sem("dve_steps_2")
        s_p2 = sem("pool_steps_2")
        s_table = sem("tables_of_pairs")
        s_bu = sem("inputs_of_pairs")
        s_rot = sem("inputs_rotated")
        s_scan = sem("pairs_scanned")
        s_back = sem("pairs_rotated_back")
        s_yc = sem("pairs_projected")
        s_ys = sem("skip_added")
        s_gel = sem("gelu_done")
        s_glu = sem("glu_units")
        s_sig = sem("glu_gates")
        s_out2 = sem("glu_products")

        with nc.Block() as block:
            @block.sync
            def _(sp):
                sp.dma_start(wg[:], l0("w_glu").rearrange("(k p) n -> p k n", p=P)).then_inc(s_wg, 16)

            @block.gpsimd
            def _(pool):
                link = chained(pool, s_p2)
                for q in range(NPAIR):
                    o = q % 2
                    pool.wait_ge(s_scan, q + 1)
                    if q >= 2:
                        pool.wait_ge(s_yc, q - 1)
                    zr, zi, c, s = z[:, o, 0], z[:, o, 1], et[:, o, 0], et[:, o, 1]
                    pool.tensor_tensor(xr[:, 0], zr, c, ALU.mult)
                    pool.tensor_tensor(xr[:, 1], zi, s, ALU.mult)
                    pool.tensor_tensor(xr[:, 2], zr, s, ALU.mult)
                    link(pool.tensor_tensor(xr[:, 3], zi, c, ALU.mult))
                    pool.tensor_tensor(xs[:, o, 0], xr[:, 0], xr[:, 1], ALU.subtract)
                    link(pool.tensor_tensor(xs[:, o, 1], xr[:, 2], xr[:, 3], ALU.add))
                    pool.sem_inc(s_back, 1)

            @block.scalar
            def _(act):
                for c in range(CH):
                    act.wait_ge(s_ys, c + 1)
                    act.activation(uT[:, c, :], uT[:, c, :], ACT.Gelu_apprx_tanh).then_inc(s_gel, 1)
                for c in range(CH):
                    act.wait_ge(s_glu, c + 1)
                    act.activation(sg[:, c, :], bank[c][:], ACT.Sigmoid).then_inc(s_sig, 1)

            @block.tensor
            def _(pe):
                def inputs(q):
                    if q >= 2:
                        pe.wait_ge(s_rot, q - 1)
                    c, r = q // 4, 32 * (q % 4)
                    for n in range(2):
                        last = pe.matmul(bank[2 * (q % 2) + n][:], bT[r:r + 32, n, c, :], uT[r:r + 32, c, :],
                                         start=True, stop=True)
                    last.then_inc(s_bu, 1)

                inputs(0)
                for q in range(NPAIR):
                    if q + 1 < NPAIR:
                        inputs(q + 1)
                    pe.wait_ge(s_back, q + 1)
                    c, r = q // 4, 32 * (q % 4)
                    for n in range(2):
                        last = pe.matmul(bank[4 + c][r:r + 32, :], cT[:, n, c, r:r + 32], xs[:, q % 2, n, :],
                                         start=n == 0, stop=n == 1)
                    last.then_inc(s_yc, 1)
                pe.wait_ge(s_wg, 16)
                for half_ in (1, 0):
                    for c in range(CH):
                        for k in range(CH):
                            pe.wait_ge(s_gel, k + 1)
                            last = pe.matmul(bank[4 * (1 - half_) + c][:], wg[:, k, half_ * SSM + c * P:half_ * SSM + (c + 1) * P],
                                             uT[:, k, :], start=k == 0, stop=k == CH - 1)
                        last.then_inc(s_glu, 1)

            @block.vector
            def _(dve):
                link = chained(dve, s_v2)
                def table(q):
                    o = q % 2
                    if q >= 2:
                        dve.wait_ge(s_back, q - 1)
                    A = lambda n: ea[:, n, q, :].unsqueeze(2).broadcast_to([P, TA, TB])
                    B = lambda n: eb[:, n, q, :].unsqueeze(1).broadcast_to([P, TA, TB])
                    v = lambda x: x.rearrange("p (a b) -> p a b", b=TB)
                    dve.tensor_tensor(v(er[:, 0]), A(0), B(0), ALU.mult)
                    dve.tensor_tensor(v(er[:, 1]), A(1), B(1), ALU.mult)
                    dve.tensor_tensor(v(er[:, 2]), A(0), B(1), ALU.mult)
                    link(dve.tensor_tensor(v(er[:, 3]), A(1), B(0), ALU.mult))
                    dve.tensor_tensor(et[:, o, 0], er[:, 0], er[:, 1], ALU.subtract)
                    link(dve.tensor_tensor(et[:, o, 1], er[:, 2], er[:, 3], ALU.add))

                for q in range(NPAIR):
                    o = q % 2
                    table(q)
                    c, s = et[:, o, 0], et[:, o, 1]
                    dve.wait_ge(s_bu, q + 1)
                    bre, bim = bank[2 * o][:], bank[2 * o + 1][:]
                    dve.tensor_tensor(br[:, 0], bre, c, ALU.mult)
                    dve.tensor_tensor(br[:, 1], bim, s, ALU.mult)
                    dve.tensor_tensor(br[:, 2], bim, c, ALU.mult)
                    link(dve.tensor_tensor(br[:, 3], bre, s, ALU.mult))
                    dve.sem_inc(s_rot, 1)
                    dve.tensor_tensor(zin[:, 0], br[:, 0], br[:, 1], ALU.add)
                    link(dve.tensor_tensor(zin[:, 1], br[:, 2], br[:, 3], ALU.subtract))
                    rr = prT[:, 0, q:q + 1].broadcast_to([P, S])
                    dve.tensor_tensor_scan(z[:, o, 0], rr, zin[:, 0], 0.0, ALU.mult, ALU.add)
                    link(dve.tensor_tensor_scan(z[:, o, 1], rr, zin[:, 1], 0.0, ALU.mult, ALU.add))
                    dve.sem_inc(s_scan, 1)
                for c in range(CH):
                    dve.wait_ge(s_yc, 4 * (c + 1))
                    dve.scalar_tensor_tensor(uT[:, c, :], uT[:, c, :], col[:, R_D + c:R_D + c + 1], bank[4 + c][:],
                                             ALU.mult, ALU.add).then_inc(s_ys, 1)
                for c in range(CH):
                    dve.wait_ge(s_sig, c + 1)
                    dve.wait_ge(s_glu, CH + c + 1)
                    dve.tensor_tensor(gluT[:, c, :], bank[4 + c][:], sg[:, c, :], ALU.mult).then_inc(s_out2, 1)

        NB = 2
        p3 = ExitStack()
        w1 = sb("w1", [P, 2, CB, P], on=p3)
        w2k = sb("w2k", [P, 2, HD], on=p3)
        w2v = sb("w2v", [P, HD], on=p3)
        pe_r = sb("pe_r", [CB, 2, 2, HD], on=p3)
        peT = sb("peT", [P, 2, CB], on=p3)
        hT = sb("hT", [P, 2, KVG, NC32], on=p3)
        h4 = sb("h4", [P, KVG, HPG, NC32], on=p3)
        kcmp = sb("kcmp", [P, NC32], on=p3)
        vbd = sb("vbd", [P, KVG, HPG, HD], on=p3)
        slopes = sb("slopes", [P, HEADS], on=p3)
        dist = sb("dist", [P, S], on=p3)
        distc = sb("distc", [P, TT, NC32], on=p3)
        maskc = sb("maskc", [P, TT, NC32], on=p3)
        gate = sb("gate", [P, TT, GATES], on=p3)
        sc_c = sb("sc_c", [P, HEADS, NC32], on=p3)
        p_c = sb("p_c", [P, HEADS, NC32], on=p3)
        mx_c = sb("mx_c", [P, HEADS], on=p3)
        pTc = sb("pTc", [P, 2, P], on=p3)
        den = sb("den", [P, 2, 3, HEADS], on=p3)
        coef = sb("coef", [P, 3, HEADS], on=p3)
        blocks = ExitStack()
        blk = sb("blk", [P, 2, CB, KVG, NC32], on=blocks)
        blocks.close()
        sc = sb("sc", [P, 3, S], on=p3)
        nmx = sb("nmx", [P, 3], on=p3)
        pr = sb("pr", [P, 3, S], on=p3)
        pT = sb("pT", [P, 2, S], on=p3)
        acc = sb("acc", [P, HEADS, HD], on=p3)
        tmp3 = sb("tmp3", [P, HEADS, HD], on=p3)
        p3.close()

        wu = (x1, qp[:].rearrange("p (k a) s -> p k (a s)", a=2))
        s_wu = sem("w_up_loaded")
        s_w1 = sem("compression_loaded")
        s_tab = sem("distances_made")
        s_v3 = sem("dve_steps_3")
        s_pe3 = sem("pe_positions_turned")
        s_blk = sem("blocks_made")
        s_hid = sem("hidden_made")
        s_hT = sem("hidden_gelu")
        s_cmp = sem("compressed_made")
        s_cin = sem("compressed_in_place")
        s_gt = sem("gates_made")
        s_sc = sem("scores_made")
        s_mx = sem("scores_shifted")
        s_ex = sem("exponentials")
        s_tp = sem("probs_turned")
        s_pt = sem("probs_in_place")
        s_pv = sem("heads_weighed")
        s_scc = sem("cmp_scores_made")
        s_mxc = sem("cmp_scores_shifted")
        s_exc = sem("cmp_exponentials")
        s_pc = sem("cmp_probs_masked")
        s_tpc = sem("cmp_probs_turned")
        s_ptc = sem("cmp_probs_in_place")
        s_oc = sem("cmp_output_made")
        s_comb = sem("tiles_combined")
        s_nt = sem("tiles_turned")
        s_nT = sem("tiles_in_place")

        HU = [(i, b, h) for i in range(TT) for b in range(NB) for h in range(HEADS)]
        PT_ = NB * HEADS
        AT_COMBINE, AT_TURN, AT_TURNED, AT_CS, AT_CX, AT_CM, AT_CT, AT_CP, AT_CW = 1, 1, 2, 3, 6, 8, 9, 10, 11

        with nc.Block() as block:
            @block.sync
            def _(sp):
                for n, kv in enumerate("kv"):
                    for g in range(KVG):
                        sp.dma_start(w1[g * HD:(g + 1) * HD, n], l0(f"nsa_w1_{kv}").rearrange("(l d) h -> d l h", d=HD)).then_inc(s_w1, 16)
                        sp.dma_start(pe_r[:, n, g], l0(f"nsa_pe_{kv}")).then_inc(s_w1, 16)
                for g in range(KVG):
                    sp.dma_start(w2k[:, g], l0("nsa_w2_k")).then_inc(s_w1, 16)
                sp.dma_start(w2v[:], l0("nsa_w2_v")).then_inc(s_w1, 16)
                sp.dma_start(wu[0][:], l0("w_up_ssm").rearrange("(k p) n -> p k n", p=P)).then_inc(s_wu, 16)
                sp.dma_start(wu[1], l0("w_up_nsa").rearrange("(k p) n -> p k n", p=P)).then_inc(s_wu, 16)

            @block.gpsimd
            def _(pool):
                n = [0]

                def step(ins):
                    n[0] += 1
                    ins.then_inc(s_tab, 1)
                    pool.wait_ge(s_tab, n[0])
                for h in range(HEADS):
                    last = pool.memset(slopes[:, h:h + 1], 2.0 ** (-8.0 * (h + 1) / HEADS))
                step(last)
                step(pool.iota(dist[:], [[1, S]], base=-(S - P), channel_multiplier=-1, allow_small_or_imprecise_dtypes=True))
                step(pool.affine_select(dist[:], dist[:], [[-1, S]], ALU.is_ge, NEG, base=S - P, channel_multiplier=1))
                step(pool.iota(distc[:], [[-P, TT], [CS, NC32]], base=CB - 1, channel_multiplier=-1, allow_small_or_imprecise_dtypes=True))
                step(pool.memset(maskc[:], 1.0))
                step(pool.affine_select(distc[:], distc[:], [[P, TT], [-CS, NC32]], ALU.is_ge, NEG, base=-(CB - 1), channel_multiplier=1))
                step(pool.affine_select(maskc[:], maskc[:], [[P, TT], [-CS, NC32]], ALU.is_ge, 0.0, base=-(CB - 1), channel_multiplier=1))
                step(pool.memset(vbd[:], 0.0))
                step(pool.memset(blk[:], 0.0))

            @block.scalar
            def _(act):
                act.activation(gate[:], vN[:, :, 2 * P:], ACT.Sigmoid).then_inc(s_gt, 1)
                for n in range(2):
                    act.wait_ge(s_hid, n + 1)
                    act.activation(hT[:, n], bank[n][:, 0:KVG * NC32].rearrange("p (g c) -> p g c", g=KVG),
                                   ACT.Gelu_apprx_tanh).then_inc(s_hT, 1)

                def turned(u):
                    i = HU[u][0]
                    act.wait_ge(s_tp, u + 1)
                    if u >= 2:
                        act.wait_ge(s_pv, u - 1)
                    act.activation(pT[:, u % 2, 0:P * (i + 1)], bank[2 + u % 2][:, 0:P * (i + 1)], ACT.Copy).then_inc(s_pt, 1)

                for u, (i, b, h) in enumerate(HU):
                    if u % PT_ == AT_CX + 1:
                        act.wait_ge(s_mxc, i + 1)
                        act.activation(p_c[:], sc_c[:], ACT.Exp).then_inc(s_exc, 1)
                    act.wait_ge(s_mx, u + 1)
                    if u >= 3:
                        act.wait_ge(s_tp, u - 2)
                    if i >= 2:
                        act.wait_ge(s_comb, i - 1)
                    L = P * (i + 1)
                    act.activation(pr[:, u % 3, 0:L], sc[:, u % 3, 0:L], ACT.Exp, bias=nmx[:, u % 3:u % 3 + 1],
                                   accum_out=den[:, i % 2, 1 + b, h:h + 1]).then_inc(s_ex, 1)
                    if u >= 1:
                        turned(u - 1)
                turned(len(HU) - 1)

            @block.tensor
            def _(pe):
                pe.wait_ge(s_w1, 16 * 11)
                for n in range(2):
                    last = pe.transpose(bank[4][:, n * CB:(n + 1) * CB], pe_r[:, n].rearrange("l g d -> l (g d)"), ident[0:CB, 0:CB])
                last.then_inc(s_pe3, 1)
                for n in range(2):
                    pe.wait_ge(s_blk, n + 1)
                    for l in range(CB):
                        last = pe.matmul(bank[n][:, 0:KVG * NC32], w1[:, n, l, :], blk[:, n, l].rearrange("p g c -> p (g c)"),
                                         start=l == 0, stop=l == CB - 1)
                    last.then_inc(s_hid, 1)
                pe.wait_ge(s_hT, 1)
                pe.matmul(bank[5][:, 0:2 * NC32], w2k[:].rearrange("p g d -> p (g d)"),
                          hT[:, 0].rearrange("p g c -> p (g c)"), start=True, stop=True).then_inc(s_cmp, 1)
                pe.wait_ge(s_cin, 1)
                for g in range(KVG):
                    last = pe.matmul(bank[6 + g][:, 0:HD], h4[:, g].rearrange("p h c -> p (h c)"), w2v[:], start=True, stop=True)
                last.then_inc(s_cmp, 1)
                pe.wait_ge(s_cin, 3)

                def scores(u):
                    i, b, h = HU[u]
                    g, c = h // HPG, h % HPG
                    r = slice(g * HD, (g + 1) * HD)
                    if u >= 2:
                        pe.wait_ge(s_mx, u - 1)
                    pe.matmul(bank[u % 2][:, 0:P * (i + 1)], qT[r, c, i * P:(i + 1) * P], kT[r, 2 + b, 0:P * (i + 1)],
                              start=True, stop=True).then_inc(s_sc, 1)

                def turn(u):
                    i = HU[u][0]
                    pe.wait_ge(s_ex, u + 1)
                    if u >= 2:
                        pe.wait_ge(s_pt, u - 1)
                    for k in range(i + 1):
                        last = pe.transpose(bank[2 + u % 2][:, k * P:(k + 1) * P], pr[:, u % 3, k * P:(k + 1) * P], ident[:])
                    last.then_inc(s_tp, 1)

                def weigh(u):
                    i, b, h = HU[u]
                    g = h // HPG
                    pe.wait_ge(s_pt, u + 1)
                    if h == 0 and i:
                        pe.wait_ge(s_comb, i)
                    for k in range(i + 1):
                        last = pe.matmul(bank[4 + b][:, h * HD:(h + 1) * HD], pT[:, u % 2, k * P:(k + 1) * P],
                                         vN[:, k, b * P + g * HD:b * P + (g + 1) * HD], start=k == 0, stop=k == i)
                    last.then_inc(s_pv, 1)

                def cmp_scores(i):
                    if i:
                        pe.wait_ge(s_nT, i)
                        pe.wait_ge(s_comb, i)
                    for g in range(KVG):
                        r = slice(g * HD, (g + 1) * HD)
                        for c in range(HPG):
                            last = pe.matmul(bank[6 + g][:, c * NC32:(c + 1) * NC32], qT[r, c, i * P:(i + 1) * P],
                                             kcmp[r, :], start=True, stop=True)
                        last.then_inc(s_scc, 1)

                def cmp_turn(i):
                    pe.wait_ge(s_pc, i + 1)
                    for g in range(KVG):
                        last = pe.transpose(bank[6][:, g * P:(g + 1) * P],
                                            p_c[:, g * HPG:(g + 1) * HPG].rearrange("p h c -> p (h c)"), ident[:])
                    last.then_inc(s_tpc, 1)

                def cmp_weigh(i):
                    pe.wait_ge(s_ptc, i + 1)
                    for g in range(KVG):
                        last = pe.matmul(bank[7][:, g * 256:(g + 1) * 256], pTc[:, g, :],
                                         vbd[:, g].rearrange("p h d -> p (h d)"), start=True, stop=True)
                    last.then_inc(s_oc, 1)

                def tile_turn(i):
                    pe.wait_ge(s_comb, i + 1)
                    for c in range(CH):
                        last = pe.transpose(bank[6][:, c * P:(c + 1) * P],
                                            acc[:, 2 * c:2 * c + 2].rearrange("p h d -> p (h d)"), ident[:])
                    last.then_inc(s_nt, 1)

                scores(0)
                scores(1)
                for u, (i, b, h) in enumerate(HU):
                    turn(u)
                    if u + 2 < len(HU):
                        scores(u + 2)
                    if u >= 1:
                        weigh(u - 1)
                    at = u % PT_
                    if at == AT_TURN and i:
                        tile_turn(i - 1)
                    if at == AT_CS:
                        cmp_scores(i)
                    if at == AT_CT:
                        cmp_turn(i)
                    if at == AT_CW:
                        cmp_weigh(i)
                weigh(len(HU) - 1)
                tile_turn(TT - 1)

            @block.vector
            def _(dve):
                link = chained(dve, s_v3)
                dve.wait_ge(s_pe3, 1)
                link(dve.tensor_copy(peT[:], bank[4][:, 0:2 * CB].rearrange("p (n l) -> p n l", n=2)))
                dve.wait_ge(s_tab, 9)
                for n in range(2):
                    v = kT[:, n, :].rearrange("p (c s) -> p s c", s=CS)
                    for m in range(2):
                        for g in range(KVG):
                            r = slice(g * HD, (g + 1) * HD)
                            pb = peT[r, n, m * CS:(m + 1) * CS].unsqueeze(2).broadcast_to([HD, CS, NCMP])
                            last = dve.tensor_tensor(blk[r, n, m * CS:(m + 1) * CS, g, 0:NCMP], v[r, :, m:m + NCMP], pb, ALU.add)
                        link(last)
                    dve.sem_inc(s_blk, 1)
                dve.wait_ge(s_hT, 2)
                for g in range(KVG):
                    last = dve.tensor_copy(h4[:, g], hT[:, 1, g].unsqueeze(1).broadcast_to([P, HPG, NC32]))
                last.then_inc(s_cin, 1)
                dve.wait_ge(s_cmp, 1)
                for g in range(KVG):
                    r = slice(g * HD, (g + 1) * HD)
                    last = dve.tensor_copy(kcmp[r, :], bank[5][r, g * NC32:(g + 1) * NC32])
                last.then_inc(s_cin, 1)
                dve.wait_ge(s_cmp, 2)
                for g in range(KVG):
                    for h in range(HPG):
                        r = slice(h * NC32, (h + 1) * NC32)
                        last = dve.tensor_copy(vbd[r, g, h, :], bank[6 + g][r, 0:HD])
                last.then_inc(s_cin, 1)
                dve.wait_ge(s_gt, 1)

                def combine(i):
                    dve.wait_ge(s_pv, PT_ * (i + 1))
                    dve.wait_ge(s_oc, i + 1)
                    if i:
                        dve.wait_ge(s_nt, i)
                    link(dve.reciprocal(coef[:], den[:, i % 2]))
                    link(dve.tensor_tensor(coef[:], coef[:], gate[:, i].rearrange("p (h b) -> p b h", b=3), ALU.mult))
                    by = lambda n: coef[:, n, :].unsqueeze(2).broadcast_to([P, HEADS, HD])
                    o = lambda n: bank[n][:].rearrange("p (h d) -> p h d", d=HD)
                    link(dve.tensor_tensor(acc[:], o(7), by(0), ALU.mult))
                    for n in (4, 5):
                        link(dve.tensor_tensor(tmp3[:], o(n), by(n - 3), ALU.mult))
                        link(dve.tensor_tensor(acc[:], acc[:], tmp3[:], ALU.add))
                    dve.sem_inc(s_comb, 1)

                def take(i):
                    dve.wait_ge(s_nt, i + 1)
                    dve.tensor_copy(nsaT[:, :, i * P:(i + 1) * P], bank[6][:].rearrange("p (c t) -> p c t", c=CH)).then_inc(s_nT, 1)

                for u, (i, b, h) in enumerate(HU):
                    o, L = u % 3, P * (i + 1)
                    dve.wait_ge(s_sc, u + 1)
                    if u >= 3:
                        dve.wait_ge(s_ex, u - 2)
                    link(dve.scalar_tensor_tensor(sc[:, o, 0:L], dist[:, S - L:S], slopes[:, h:h + 1], bank[u % 2][:, 0:L],
                                                  ALU.mult, ALU.add))
                    dve.tensor_reduce(nmx[:, o:o + 1], sc[:, o, 0:L], AX.X, ALU.max, negate=True).then_inc(s_mx, 1)
                    at = u % PT_
                    if at == AT_COMBINE and i:
                        combine(i - 1)
                    if at == AT_TURNED and i:
                        take(i - 1)
                    if at == AT_CX:
                        dve.wait_ge(s_scc, 2 * (i + 1))
                        if i:
                            dve.wait_ge(s_tpc, i)
                        link(dve.tensor_tensor(sc_c[:], distc[:, i].unsqueeze(1).broadcast_to([P, HEADS, NC32]),
                                               slopes[:].unsqueeze(2).broadcast_to([P, HEADS, NC32]), ALU.mult))
                        for g in range(KVG):
                            hs = slice(g * HPG, (g + 1) * HPG)
                            last = dve.tensor_tensor(sc_c[:, hs], sc_c[:, hs],
                                                     bank[6 + g][:, 0:P].rearrange("p (h c) -> p h c", c=NC32), ALU.add)
                            link(last)
                        link(dve.tensor_reduce(mx_c[:], sc_c[:], AX.X, ALU.max))
                        dve.tensor_tensor(sc_c[:], sc_c[:], mx_c[:].unsqueeze(2).broadcast_to([P, HEADS, NC32]),
                                          ALU.subtract).then_inc(s_mxc, 1)
                    if at == AT_CM:
                        dve.wait_ge(s_exc, i + 1)
                        link(dve.tensor_tensor(p_c[:], p_c[:], maskc[:, i].unsqueeze(1).broadcast_to([P, HEADS, NC32]), ALU.mult))
                        dve.sem_inc(s_pc, 1)
                        link(dve.tensor_reduce(den[:, i % 2, 0], p_c[:], AX.X, ALU.add))
                        link(dve.tensor_scalar(den[:, i % 2, 0], den[:, i % 2, 0], 1e-30, None, ALU.max))
                    if at == AT_CP:
                        dve.wait_ge(s_tpc, i + 1)
                        dve.tensor_copy(pTc[:], bank[6][:, 0:2 * P].rearrange("p (g t) -> p g t", g=2)).then_inc(s_ptc, 1)
                combine(TT - 1)
                take(TT - 1)

        def row(name, n0, n1):
            return spread(l0(name)[n0:n1], n1 - n0)

        p4 = ExitStack()
        xr2 = sb("xr2", [P, TT, D], on=p4)
        wo = sb("wo", [P, KD, D], on=p4)
        sk = sb("sk", [P, 2 * PH, HD], on=p4)
        ln1 = sb("ln1", [P, 2, D], on=p4)
        mt = x1T[:, 0:2]
        st = sb("st", [P, 2, 6], on=p4)
        mv = sb("mv", [P, TT, 2], on=p4)
        rs = sb("rs", [P, TT], on=p4)
        p4.close()

        s_wo = sem("w_out_loaded")
        s_wq = sem("w_q_loaded")
        s_sk = sem("subkeys_loaded")
        s_x2 = sem("x_loaded_again")
        s_up = sem("chunks_projected_up")
        s_mix = sem("chunks_merged")
        s_o = sem("halves_projected_out")
        s_res = sem("halves_added")
        s_var = sem("variances")
        s_std = sem("deviations")
        s_x1 = sem("x1_tiles")
        s_xt = sem("x1_turned")
        s_xT = sem("x1T_in_place")
        s_v4 = sem("dve_steps_4")
        s_xhl = sem("x1_parts_made")

        with nc.Block() as block:
            @block.sync
            def _(sp):
                sp.dma_start(wo[:], l0("w_out").rearrange("(k p) n -> p k n", p=P)).then_inc(s_wo, 16)
                sp.dma_start(xr2[:], a["x"][0].rearrange("(t p) d -> p t d", p=P)).then_inc(s_x2, 16)
                sp.dma_start(ln1[:, 0, :], row("ln1_g", 0, D)).then_inc(s_x2, 16)
                sp.dma_start(ln1[:, 1, :], row("ln1_b", 0, D)).then_inc(s_x2, 16)
                sp.dma_start(sk[:], l0("peer_subkeys").rearrange("h c k d -> k (h c) d")).then_inc(s_sk, 16)
                sp.wait_ge(s_mix, KD)
                sp.dma_start(wq[:], l0("peer_w_q").rearrange("(k p) n -> p k n", p=P)).then_inc(s_wq, 16)

            @block.tensor
            def _(pe):
                pe.wait_ge(s_wu, 32)
                for c in range(KD):
                    if c >= 2:
                        pe.wait_ge(s_mix, c - 1)
                    for n, y in enumerate((gluT, nsaT)):
                        for k in range(CH):
                            last = pe.matmul(bank[2 * (c % 2) + n][:], wu[n][:, k, c * P:(c + 1) * P], y[:, k, :],
                                             start=k == 0, stop=k == CH - 1)
                    last.then_inc(s_up, 1)
                pe.wait_ge(s_wo, 16)
                pe.wait_ge(s_mix, KD)
                for t in range(TT):
                    for n in range(2):
                        m = 2 * t + n
                        if m >= 4:
                            pe.wait_ge(s_res, m - 3)
                        for k in range(KD):
                            last = pe.matmul(bank[4 + m % 4][:], gmT[:, k, t * P:(t + 1) * P], wo[:, k, n * 512:(n + 1) * 512],
                                             start=k == 0, stop=k == KD - 1)
                        last.then_inc(s_o, 1)
                for t in range(TT):
                    pe.wait_ge(s_x1, t + 1)
                    for n in range(2):
                        m = 2 * t + n
                        if m >= 4:
                            pe.wait_ge(s_xT, m - 3)
                            pe.wait_ge(s_xhl, m - 3)
                        for k in range(4):
                            last = pe.transpose(bank[m % 4][:, k * P:(k + 1) * P], x1[:, t, (4 * n + k) * P:(4 * n + k + 1) * P], ident[:])
                        last.then_inc(s_xt, 1)

            @block.scalar
            def _(act):
                for t in range(TT):
                    act.wait_ge(s_var, t + 1)
                    act.activation(rs[:, t:t + 1], mv[:, t, 1:2], ACT.Sqrt).then_inc(s_std, 1)
                for m in range(2 * TT):
                    t, n = m // 2, m % 2
                    act.wait_ge(s_xt, m + 1)
                    b = bank[m % 4][:].rearrange("p (k t) -> p k t", k=4)
                    act.activation(xh[:, 4 * n:4 * n + 4, t * P:(t + 1) * P], b, ACT.Copy)
                    act.activation(x1T[:, 4 * n:4 * n + 4, t * P:(t + 1) * P], b, ACT.Copy).then_inc(s_xT, 1)

            @block.vector
            def _(dve):
                link = chained(dve, s_v4)
                for c in range(KD):
                    dve.wait_ge(s_up, c + 1)
                    b = 2 * (c % 2)
                    dve.tensor_tensor(mt[:, 0], bank[b][:], gmT[:, c, :], ALU.mult)
                    link(dve.tensor_tensor(mt[:, 1], bank[b + 1][:], gmT[:, KD + c, :], ALU.mult))
                    link(dve.tensor_tensor(gmT[:, c, :], mt[:, 0], mt[:, 1], ALU.add))
                    dve.sem_inc(s_mix, 1)
                dve.wait_ge(s_x2, 48)
                for t in range(TT):
                    for n in range(2):
                        h = slice(n * 512, (n + 1) * 512)
                        dve.wait_ge(s_o, 2 * t + n + 1)
                        link(dve.scalar_tensor_tensor(x1[:, t, h], xr2[:, t, h], DN_ALPHA, bank[4 + (2 * t + n) % 4][:], ALU.mult, ALU.add))
                        dve.sem_inc(s_res, 1)
                        link(dve.bn_stats(st[:, n, :], x1[:, t, h]))
                    link(dve.bn_aggr(mv[:, t, :], st[:].rearrange("p n s -> p (n s)")))
                    dve.tensor_scalar(mv[:, t, 1:2], mv[:, t, 1:2], LN_EPS, None, ALU.add).then_inc(s_var, 1)
                    dve.wait_ge(s_std, t + 1)
                    link(dve.reciprocal(rs[:, t:t + 1], rs[:, t:t + 1]))
                    link(dve.tensor_scalar(x1[:, t, :], x1[:, t, :], mv[:, t, 0:1], rs[:, t:t + 1], ALU.subtract, ALU.mult))
                    link(dve.tensor_tensor(x1[:, t, :], x1[:, t, :], ln1[:, 0, :], ALU.mult))
                    dve.tensor_tensor(x1[:, t, :], x1[:, t, :], ln1[:, 1, :], ALU.add).then_inc(s_x1, 1)
                for m in range(2 * TT):
                    t, n = m // 2, m % 2
                    dve.wait_ge(s_xT, m + 1)
                    at = (slice(None), slice(4 * n, 4 * n + 4), slice(t * P, (t + 1) * P))
                    dve.tensor_tensor(xl[at], bank[m % 4][:].rearrange("p (k t) -> p k t", k=4), xh[at].bitcast(F32),
                                      ALU.subtract).then_inc(s_xhl, 1)

        early.close()

        LISTS = 2 * PH
        TG = 8
        HT = P // 2
        STEPS = HT // TG
        IT = 4
        TURNS = PK // IT
        fence = ExitStack()
        sb("place_of_parts", [P, 2 * KD * S], on=fence)
        p6 = ExitStack()
        ub = sb("ub", [P, IT, D], on=p6)
        uTh = sb("uTh", [P, 2, KD, P], F32R, on=p6)
        uTl = sb("uTl", [P, 2, KD, P], F32R, on=p6)
        hb = sb("hb", [P, IT, S], on=p6)
        ss = sb("ss", [P, LISTS, PK], on=p6)
        sv = sb("sv", [P, LISTS, PE_TOP], on=p6)
        si = sb("si", [P, LISTS, PE_TOP], U32, on=p6)
        sif = sb("sif", [P, LISTS, PE_TOP], on=p6)
        cand = sb("cand", [P, PH * PE_TOP, PE_TOP], on=p6)
        best = sb("best", [P, PH, PE_TOP], on=p6)
        pos = sb("pos", [P, PH, PE_TOP], U32, on=p6)
        pab = sb("pab", [P, 2, PH, PE_TOP], U32, on=p6)
        pabf = sb("pabf", [P, 2, PH, PE_TOP], on=p6)
        picks = sb("picks", [P, 3, PH, PE_TOP], on=p6)
        gs = sb("gs", [P, 2, PH], on=p6)
        pkT = sb("pkT", [P, 2, 3, P], on=p6)
        gh = sb("gh", [P, 2, P], F32R, on=p6)
        gl = sb("gl", [P, 2, P], F32R, on=p6)
        iota = sb("iota", [P, P], on=p6)
        oh = sb("oh", [P, 2, TG, P], F32R, on=p6)
        ohj = sb("ohj", [P, 2, TG, P], on=p6)
        ogh = sb("ogh", [P, 2, TG, P], F32R, on=p6)
        ogl = sb("ogl", [P, 2, TG, P], F32R, on=p6)
        stg = sb("stg", [P, PK, HT], on=p6)
        p6.close()
        fence.close()
        p7 = ExitStack()
        wf = sb("wf", [P, 4, S], on=p7)
        wh = sb("wh", [P, 2, 4, S], F32R, on=p7)
        wl = sb("wl", [P, 2, 4, S], F32R, on=p7)
        vh, vl = [None, None], [None, None]
        for o_ in (1, 0):
            vh[o_] = sb(f"vh{o_}", [P, 4, D], F32R, on=p7)
            vl[o_] = sb(f"vl{o_}", [P, 4, D], F32R, on=p7)
        vb = sb("vb", [P, 2, 4, D], on=p7)
        gb = sb("gb", [P, 2, 2 * TT, 4 * HT], on=p7)
        hg = sb("hg", [P, 2, 4, S], on=p7)
        st8 = sb("st8", [P, TT, 2, 6], on=p7)
        mv8 = sb("mv8", [P, TT, 2], on=p7)
        rs8 = sb("rs8", [P, TT], on=p7)
        p7.close()

        s_u = [sem(f"u_loaded{n}") for n in range(IT)]
        ut = l0("peer_u").rearrange("(i j) d -> j i d", j=PK)
        s_skt = sem("subkeys_turned")
        s_skT = sem("subkeys_in_place")
        s_qp = sem("peer_queries")
        s_qpd = sem("peer_queries_in_place")

        with nc.Block() as block:
            @block.sync
            def _(sp):
                for r in range(IT):
                    sp.dma_start(ub[:, r, :], ut[r]).then_inc(s_u[r], 16)

            @block.tensor
            def _(pe):
                pe.wait_ge(s_sk, 16)
                for n in range(2):
                    for h in range(4):
                        last = pe.transpose(bank[n][:, h * P:(h + 1) * P],
                                            sk[:, 2 * (4 * n + h):2 * (4 * n + h) + 2].rearrange("p c d -> p (c d)"), ident[:])
                    last.then_inc(s_skt, 1)
                pe.wait_ge(s_wq, 16)
                for h in range(PH):
                    if h >= 4:
                        pe.wait_ge(s_qpd, h - 3)
                    for k in range(KD):
                        last = pe.matmul(bank[2 + h % 4][:], wq[:, k, h * P:(h + 1) * P], x1T[:, k, :],
                                         start=k == 0, stop=k == KD - 1)
                    last.then_inc(s_qp, 1)

            @block.scalar
            def _(act):
                for h in range(PH):
                    act.wait_ge(s_qp, h + 1)
                    act.activation(qp[:, h, :], bank[2 + h % 4][:], ACT.Copy).then_inc(s_qpd, 1)

            @block.vector
            def _(dve):
                for n in range(2):
                    dve.wait_ge(s_skt, n + 1)
                    dve.tensor_copy(skT[:, 4 * n:4 * n + 4, :], bank[n][:].rearrange("p (h k) -> p h k", h=4)).then_inc(s_skT, 1)

        gates = nc.dram_tensor("gates", [2 * TT, P, PK, HT], F32, kind="Internal").ap()
        hidden = nc.dram_tensor("hidden", [PK // 2, P, 2, S], F32, kind="Internal").ap()
        SEQ = [("pick", 0, 0), ("pick", 0, 1)]
        for t_ in range(TT):
            for part_ in range(2):
                SEQ.append(("gates", 2 * t_ + part_))
                SEQ.append(("pick", t_ + 1, part_) if t_ + 1 < TT else ("only", 1 if part_ == 0 else None))
        PICK_TURNS = (2, 3)

        def turns_of(s):
            return {"pick": PICK_TURNS[s[-1]] if s[0] == "pick" else 0, "gates": 1, "only": s[1]}[s[0]]

        SEQ[-1] = ("only", TURNS - sum(turns_of(s) for s in SEQ[:-1]))
        LAST = TURNS - 1

        JG = 4
        NG = PK // JG
        s_v = [sem(f"v_loaded{n}") for n in range(2)]
        vg = l0("peer_v").rearrange("(i g j) d -> g i (j d)", i=P, j=JG)
        gg = gates.rearrange("t i (g j) k -> g i t (j k)", j=JG)
        hh_ = hidden.rearrange("(g a) i b s -> g i a (b s)", a=JG // 2)
        s_g = [sem(f"gates_and_hidden_loaded{n}") for n in range(2)]
        s_vh = sem("v_high_parts")
        s_vl = sem("v_low_parts")
        s_sc7 = sem("residual_scaled")

        s_io = sem("counters_made")
        s_ss = sem("peer_scores")
        s_ssd = sem("peer_scores_in_place")
        s_v6 = sem("dve_steps_6")
        s_dif = sem("best_less_maximum")
        s_gex = sem("gate_exponentials")
        s_pk = sem("picks_made")
        s_pkt = sem("picks_turned")
        s_pkT = sem("picks_in_place")
        s_hot = sem("one_hots")
        s_ogh = sem("one_hots_by_high_gate")
        s_ogl = sem("one_hots_by_low_gate")
        s_gp = sem("gates_multiplied")
        s_ge = sem("gates_staged")
        s_gw = sem("gates_stored")
        s_t = sem("experts_turned")
        s_ua = sem("turned_high_parts")
        s_ud = sem("turned_low_parts")
        s_h = sem("experts_multiplied")
        s_hr = sem("experts_gelu")
        s_hs = [sem(f"hidden_stored{n}") for n in range(2)]

        with nc.Block() as block:
            @block.sync
            def _(sp):
                def store(m, q):
                    sp.wait_ge(s_hr, IT * m + 2 * q + 4)
                    sp.dma_start(hidden[2 * m + q], hb[:, 2 * q:2 * q + 2, :]).then_inc(s_hs[q], 16)

                def turns(first, count):
                    with sp.Fori(0, count) as i:
                        m = first + i
                        for r in range(IT):
                            sp.wait_ge(s_t, IT * m + r + 1)
                            sp.dma_start(ub[:, r, :], ut[IT * (m + 1) + r]).then_inc(s_u[r], 16)
                            if r == 2:
                                store(m, 0)
                        store(m, 1)

                turns(0, LAST - 1)
                sp.wait_ge(s_gw, 16 * 2 * TT)
                for q in range(2):
                    sp.wait_ge(s_hs[q], 16 * 3)
                for g in range(2):
                    sp.dma_start(gb[:, g], gg[g]).then_inc(s_g[g], 16)
                    sp.dma_start(hg[:, g].rearrange("p (a b) s -> p a (b s)", b=2), hh_[g]).then_inc(s_g[g], 16)
                    if g == 0:
                        turns(LAST - 1, 1)
                sp.dma_start(vb[:, 1].rearrange("p j d -> p (j d)"), vg[1]).then_inc(s_v[1], 16)
                store(TURNS - 1, 0)
                store(TURNS - 1, 1)
                for q in range(2):
                    sp.wait_ge(s_hs[q], 16 * (TURNS + 1))

            @block.gpsimd
            def _(pool):
                pool.iota(iota[:], [[1, P]], base=0, channel_multiplier=0, allow_small_or_imprecise_dtypes=True).then_inc(s_io, 1)
                pool.sem_inc(s_ogh, 2)
                for t in range(TT):
                    pool.wait_ge(s_pkT, t + 1)
                    with pool.Fori(0, STEPS) as i:
                        for o in range(2):
                            n = 2 * STEPS * t + 2 * i + o
                            pool.wait_ge(s_hot, 2 * n + 2)
                            pool.wait_ge(s_gp, n + 1)
                            g = gh[:, t % 2, bass.ds((2 * i + o) * TG, TG)].bitcast(F32)
                            if o == 1:
                                low = gl[:, t % 2, bass.ds((2 * i + o) * TG, TG)].bitcast(F32)
                                pool.tensor_tensor(ogl[:, o], ohj[:, o], low.unsqueeze(2).broadcast_to([P, TG, P]), ALU.mult)
                            pool.tensor_tensor(ogh[:, o], ohj[:, o], g.unsqueeze(2).broadcast_to([P, TG, P]),
                                               ALU.mult).then_inc(s_ogh, 1)
                for j in range(JG):
                    pool.wait_ge(s_vh, j + 1)
                    pool.tensor_tensor(vl[0][:, j, :], vb[:, 0, j, :], vh[0][:, j, :].bitcast(F32), ALU.subtract).then_inc(s_vl, 1)

            @block.scalar
            def _(act):
                act.sem_inc(s_ge, 2)
                act.sem_inc(s_hr, 2)

                def take(n, r):
                    act.wait_ge(s_t, n + 1)
                    act.wait_ge(s_h, n + 1)
                    for q in range(2):
                        last = act.activation(uTh[:, r % 2, 4 * q:4 * q + 4, :], bank[q][:].rearrange("p (k i) -> p k i", k=4), ACT.Copy)
                    last.then_inc(s_ua, 1)

                def tile(m, r, last=False, between=None):
                    n = IT * m + r
                    if not last:
                        take(n + 1, (r + 1) % IT)
                    if between:
                        between()
                    act.wait_ge(s_h, n + 3)
                    act.wait_ge(s_hs[r // 2], 16 * m + 16)
                    act.activation(hb[:, r, :], bank[2 + r % 2][:], ACT.Gelu_apprx_tanh).then_inc(s_hr, 1)

                def turns(m, count, final=False):
                    if count - final > 0:
                        with act.Fori(0, count - final) as i:
                            for r in range(IT):
                                tile(m + i, r)
                    if final:
                        act.wait_ge(s_v[0], 16)
                        for r in range(IT):
                            tile(TURNS - 1, r, last=r == IT - 1)
                            act.activation(vh[0][:, r, :], vb[:, 0, r, :], ACT.Copy).then_inc(s_vh, 1)

                def bring(t, c):
                    for n in range(2):
                        act.wait_ge(s_ss, 4 * t + 2 * c + n + 1)
                        act.activation(ss[:, 8 * c + 4 * n:8 * c + 4 * n + 4, :], bank[6 + n][:].rearrange("p (h k) -> p h k", h=4),
                                       ACT.Copy).then_inc(s_ssd, 1)

                take(0, 0)
                m = 0
                for s in SEQ:
                    if s[0] == "pick":
                        _, t, part = s
                        if part == 0:
                            if t:
                                act.wait_ge(s_pk, t)
                            bring(t, 0)
                            bring(t, 1)
                        turns(m, 2)
                        if part == 1:
                            act.wait_ge(s_dif, t + 1)
                            act.activation(picks[:, 2], picks[:, 2], ACT.Exp).then_inc(s_gex, 1)
                            turns(m + 2, 1)
                    elif s[0] == "gates":
                        k = s[1]
                        if k:
                            act.wait_ge(s_gw, 16 * k)

                        def stage(r):
                            for i in range(2):
                                n = STEPS * k + 2 * r + i
                                act.wait_ge(s_gp, 2 + n + 1)
                                for b in range(2):
                                    dst = stg[:, :, (2 * r + i) * TG + 4 * b:(2 * r + i) * TG + 4 * b + 4].rearrange("p j t -> p t j")
                                    act.activation(dst, bank[4 + b][:].rearrange("p (t j) -> p t j", t=4), ACT.Copy).then_inc(s_ge, 1)

                        for r in range(IT):
                            tile(m, r, between=lambda: stage(r))
                        act.wait_ge(s_ge, 2 + 2 * STEPS * (k + 1))
                        act.dma_start(gates[k].rearrange("i j t -> i (j t)"), stg[:].rearrange("p j t -> p (j t)")).then_inc(s_gw, 16)
                        if k == 2 * TT - 1:
                            act.dma_start(vb[:, 0].rearrange("p j d -> p (j d)"), vg[0]).then_inc(s_v[0], 16)
                    else:
                        turns(m, s[1], final=m + s[1] == TURNS)
                    m += turns_of(s)
                act.wait_ge(s_gw, 16 * 2 * TT)

            @block.tensor
            def _(pe):
                pe.sem_inc(s_gp, 2)
                pe.sem_inc(s_h, 2)
                for q in range(2):
                    pe.sem_inc(s_hs[q], 16)

                def turn(m, r):
                    n = IT * m + r
                    pe.wait_ge(s_u[r], 16 * m + 16)
                    pe.wait_ge(s_ud, n)
                    for k in range(KD):
                        last = pe.transpose(bank[k // 4][:, (k % 4) * P:(k % 4 + 1) * P], ub[:, r, k * P:(k + 1) * P], ident[:])
                    last.then_inc(s_t, 1)

                def tile(m, r, last_tile=False, between=None):
                    n = IT * m + r
                    if r + 1 < IT:
                        turn(m, r + 1)
                    elif not last_tile:
                        turn(m + 1, 0)
                    if between:
                        between()
                    pe.wait_ge(s_ud, n + 1)
                    pe.wait_ge(s_hr, n + 1)
                    for k in range(KD):
                        for q, (x, y) in enumerate(((uTh, xh), (uTh, xl), (uTl, xh))):
                            last = pe.matmul(bank[2 + r % 2][:], x[:, r % 2, k, :], y[:, k, :],
                                             start=k == 0 and q == 0, stop=k == KD - 1 and q == 2)
                    last.then_inc(s_h, 1)

                def turns(m, count, final=False):
                    if count - final > 0:
                        with pe.Fori(0, count - final) as i:
                            for r in range(IT):
                                tile(m + i, r)
                    if final:
                        for r in range(IT):
                            tile(TURNS - 1, r, last_tile=r == IT - 1)

                def scores(t, c):
                    for n in range(2):
                        if t or c:
                            pe.wait_ge(s_ssd, 4 * t + 2 * (c - 1) + n + 1)
                        if t and c == 0 and n == 0:
                            pe.wait_ge(s_pkT, t)
                        for h in range(4):
                            hh = 4 * n + h
                            last = pe.matmul(bank[6 + n][:, h * PK:(h + 1) * PK], qp[c * HD:(c + 1) * HD, hh, t * P:(t + 1) * P],
                                             skT[c * HD:(c + 1) * HD, hh, :], start=True, stop=True)
                        last.then_inc(s_ss, 1)

                turn(0, 0)
                m = 0
                for s in SEQ:
                    if s[0] == "pick":
                        _, t, part = s
                        if part == 0:
                            scores(t, 0)
                            scores(t, 1)
                        turns(m, 2)
                        if part == 1:
                            tile(m + 2, 0)
                            pe.wait_ge(s_pk, t + 1)
                            for n in range(3):
                                last = pe.transpose(bank[6][:, n * P:(n + 1) * P], picks[:, n].rearrange("p h k -> p (h k)"), ident[:])
                            last.then_inc(s_pkt, 1)
                            for r in range(1, IT):
                                tile(m + 2, r)
                    elif s[0] == "gates":
                        k = s[1]

                        def steps(r):
                            for i in range(2):
                                n, o = STEPS * k + 2 * r + i, i
                                pe.wait_ge(s_ogh, 2 + n + 1)
                                if i == 0:
                                    pe.wait_ge(s_ogl, n // 2 + 1)
                                for b in range(2):
                                    pe.wait_ge(s_ge, 2 * n + b + 1)
                                    for w in range(4):
                                        at = bank[4 + b][:, w * P:(w + 1) * P]
                                        pe.matmul(at, oh[:, o, 4 * b + w, :], ogh[:, o, 4 * b + w, :], start=True, stop=False)
                                        last = pe.matmul(at, oh[:, o, 4 * b + w, :], ogl[:, o, 4 * b + w, :], start=False, stop=True)
                                last.then_inc(s_gp, 1)

                        for r in range(IT):
                            tile(m, r, between=lambda: steps(r))
                    else:
                        turns(m, s[1], final=m + s[1] == TURNS)
                    m += turns_of(s)

            @block.vector
            def _(dve):
                link = chained(dve, s_v6)
                LOW = -3.0e38

                def take(n, r):
                    dve.wait_ge(s_ua, n + 1)
                    for q in range(2):
                        h = slice(4 * q, 4 * q + 4)
                        last = dve.tensor_tensor(uTl[:, r % 2, h, :], bank[q][:].rearrange("p (k i) -> p k i", k=4),
                                                 uTh[:, r % 2, h, :].bitcast(F32), ALU.subtract)
                    last.then_inc(s_ud, 1)

                def top16(vals, idx, lst):
                    link(dve.max(vals[:, 0:8], lst))
                    dve.max_index(idx[:, 0:8], vals[:, 0:8], lst)
                    link(dve.match_replace(lst, vals[:, 0:8], lst, LOW))
                    link(dve.max(vals[:, 8:16], lst))
                    link(dve.max_index(idx[:, 8:16], vals[:, 8:16], lst))

                def lists(t, c, h):
                    dve.wait_ge(s_ssd, 4 * t + 2 * c + h // 4 + 1)
                    l = PH * c + h
                    top16(sv[:, l, :], si[:, l, :], ss[:, l, :])

                def candidates():
                    link(dve.tensor_copy(sif[:], si[:]))
                    link(dve.tensor_tensor(cand[:].rearrange("p (h a) b -> p h a b", h=PH),
                                           sv[:, 0:PH].unsqueeze(3).broadcast_to([P, PH, PE_TOP, PE_TOP]),
                                           sv[:, PH:].unsqueeze(2).broadcast_to([P, PH, PE_TOP, PE_TOP]), ALU.add))

                def places():
                    link(dve.tensor_scalar(pab[:, 0], pos[:], 4, None, ALU.logical_shift_right))
                    link(dve.tensor_scalar(pab[:, 1], pos[:], 15, None, ALU.bitwise_and))
                    link(dve.tensor_copy(pabf[:], pab[:]))

                def keys(c):
                    e4 = cand[:].rearrange("p (h k) a -> p h k a", h=PH)
                    link(dve.tensor_tensor(cand[:], pabf[:, c].rearrange("p h k -> p (h k)").unsqueeze(2).broadcast_to([P, PH * PE_TOP, PE_TOP]),
                                           iota[:, 0:PE_TOP].unsqueeze(1).broadcast_to([P, PH * PE_TOP, PE_TOP]), ALU.is_equal))
                    link(dve.tensor_tensor(e4, e4, sif[:, c * PH:(c + 1) * PH].unsqueeze(2).broadcast_to([P, PH, PE_TOP, PE_TOP]), ALU.mult))
                    link(dve.tensor_reduce(picks[:, c].rearrange("p h k -> p (h k)"), cand[:], AX.X, ALU.add))

                def softmax_1():
                    link(dve.tensor_tensor(picks[:, 2], best[:], best[:, :, 0:1].broadcast_to([P, PH, PE_TOP]), ALU.subtract))
                    dve.sem_inc(s_dif, 1)

                def softmax_2(t):
                    dve.wait_ge(s_gex, t + 1)
                    link(dve.tensor_reduce(gs[:, 0], picks[:, 2], AX.X, ALU.add))
                    link(dve.reciprocal(gs[:, 1], gs[:, 0]))
                    link(dve.tensor_tensor(picks[:, 2], picks[:, 2], gs[:, 1].unsqueeze(2).broadcast_to([P, PH, PE_TOP]), ALU.mult))
                    dve.sem_inc(s_pk, 1)

                def place(t):
                    o = t % 2
                    dve.wait_ge(s_pkt, t + 1)
                    if t >= 2:
                        dve.wait_ge(s_ogh, 2 + 2 * STEPS * (t - 1))
                    link(dve.tensor_copy(pkT[:, o], bank[6][:, 0:3 * P].rearrange("p (n t) -> p n t", n=3)))
                    link(dve.tensor_copy(gh[:, o], pkT[:, o, 2]))
                    dve.tensor_tensor(gl[:, o], pkT[:, o, 2], gh[:, o].bitcast(F32), ALU.subtract).then_inc(s_pkT, 1)
                    dve.wait_ge(s_pkT, t + 1)

                def spread(k, e):
                    t, n, half_step, o = k // 2, STEPS * k + e, STEPS * (k % 2) + e, e % 2
                    at = slice(half_step * TG, (half_step + 1) * TG)
                    row3 = iota[:].unsqueeze(1).broadcast_to([P, TG, P])
                    dve.wait_ge(s_gp, n + 1)
                    dve.tensor_tensor(oh[:, o], row3, pkT[:, t % 2, 0, at].unsqueeze(2).broadcast_to([P, TG, P]),
                                      ALU.is_equal).then_inc(s_hot, 1)
                    dve.wait_ge(s_ogh, n + 1)
                    dve.tensor_tensor(ohj[:, o], row3, pkT[:, t % 2, 1, at].unsqueeze(2).broadcast_to([P, TG, P]),
                                      ALU.is_equal).then_inc(s_hot, 1)
                    if o == 1:
                        return
                    dve.wait_ge(s_hot, 2 * n + 2)
                    dve.tensor_tensor(ogl[:, o], ohj[:, o], gl[:, t % 2, at].bitcast(F32).unsqueeze(2).broadcast_to([P, TG, P]),
                                      ALU.mult).then_inc(s_ogl, 1)

                dve.wait_ge(s_io, 1)
                take(0, 0)
                m = 0
                for s in SEQ:
                    if s[0] == "pick":
                        _, t, part = s
                        if part == 0:
                            heads = [lambda l=l: lists(t, l // PH, l % PH) for l in range(LISTS)]
                            ends = [0, 3, 6, 8, 10, 12, 14, 15, 16] if t else [2 * e for e in range(9)]
                            todo = [heads[ends[e]:ends[e + 1]] for e in range(8)]
                            if t:
                                for e in range(2):
                                    todo[6 + e].append(lambda e=e: spread(2 * t - 1, e))
                        else:
                            cands = [lambda h=h: top16(best[:, h, :], pos[:, h, :],
                                                       cand[:, h * PE_TOP:(h + 1) * PE_TOP, :].rearrange("p a b -> p (a b)")) for h in range(PH)]
                            todo = [[candidates, cands[0]], cands[1:3], cands[3:4], cands[4:6], cands[6:7], [cands[7], softmax_1, places],
                                    [lambda: keys(0)], [lambda: keys(1)], [lambda: softmax_2(t)], [lambda: place(t)],
                                    [lambda: spread(2 * t, 0)], [lambda: spread(2 * t, 1)]]
                        for e, pieces in enumerate(todo):
                            for piece in pieces:
                                piece()
                            take(IT * m + e + 1, (e + 1) % IT)
                    elif s[0] == "gates":
                        k = s[1]
                        for r in range(IT):
                            take(IT * m + r + 1, (r + 1) % IT)
                            if r + 1 < IT:
                                spread(k, 2 * r + 2)
                                spread(k, 2 * r + 3)
                    elif s[1] == 1:
                        for r in range(IT):
                            if r >= 2:
                                spread(2 * TT - 1, r - 2)
                            take(IT * m + r + 1, (r + 1) % IT)
                    else:
                        last = m + s[1] == TURNS
                        if s[1] - last > 0:
                            with dve.Fori(0, s[1] - last) as i:
                                for r in range(IT):
                                    take(IT * (m + i) + r + 1, (r + 1) % IT)
                        if last:
                            for r in range(IT - 1):
                                take(IT * (TURNS - 1) + r + 1, (r + 1) % IT)
                                if r == 0:
                                    dve.tensor_scalar(x1[:], x1[:], DN_ALPHA, None, ALU.mult).then_inc(s_sc7, 1)
                    m += turns_of(s)

        s_w = sem("experts_weighed")
        s_wh = sem("weighed_high_parts")
        s_wl = sem("weighed_low_parts")
        s_y = sem("sums_made")
        s_ya = sem("sums_added")

        ln2 = qp[:, 0:4, :].rearrange("p (n a) s -> p n (a s)", n=2)
        s_ln = sem("ln2_loaded")
        s_v8 = sem("dve_steps_8")
        s_var8 = sem("variances_8")
        s_std8 = sem("deviations_8")
        s_fin = sem("tiles_finished")
        s_out = sem("output_stored")

        with nc.Block() as block:
            @block.sync
            def _(sp):
                def load_g(g, o):
                    sp.dma_start(gb[:, o], gg[g]).then_inc(s_g[o], 16)
                    sp.dma_start(hg[:, o].rearrange("p (a b) s -> p a (b s)", b=2), hh_[g]).then_inc(s_g[o], 16)

                def load_v(g, o):
                    sp.dma_start(vb[:, o].rearrange("p j d -> p (j d)"), vg[g]).then_inc(s_v[o], 16)

                sp.dma_start(ln2[:, 0, :], row("ln2_g", 0, D)).then_inc(s_ln, 16)
                sp.dma_start(ln2[:, 1, :], row("ln2_b", 0, D)).then_inc(s_ln, 16)
                with sp.Fori(0, NG // 2 - 1) as i:
                    for o in range(2):
                        g = 2 * i + o
                        sp.wait_ge(s_w, JG * g + JG)
                        load_g(g + 2, o)
                        sp.wait_ge(s_vl, JG * g + JG)
                        load_v(g + 2, o)
                for t in range(TT):
                    sp.wait_ge(s_fin, t + 1)
                    sp.dma_start(out[0, t * P:(t + 1) * P, :], x1[:, t, :]).then_inc(s_out, 16)
                sp.wait_ge(s_out, 16 * TT)

            @block.tensor
            def _(pe):
                pe.sem_inc(s_y, 16)

                def group(g, o):
                    pe.wait_ge(s_wl, JG * g + 2 * JG)
                    pe.wait_ge(s_vl, JG * g + JG)
                    for m in range(8):
                        t, c = m // 2, m % 2
                        pe.wait_ge(s_ya, 8 * g + m + 1)
                        for j in range(JG):
                            for q, (x, y) in enumerate(((wh, vh), (wh, vl), (wl, vh))):
                                last = pe.matmul(bank[m][:], x[:, o, j, t * P:(t + 1) * P], y[o][:, j, c * 512:(c + 1) * 512],
                                                 start=j == 0 and q == 0, stop=j == JG - 1 and q == 2)
                        last.then_inc(s_y, 1)

                with pe.Fori(0, NG // 2) as i:
                    for o in range(2):
                        group(2 * i + o, o)

            @block.scalar
            def _(act):
                def group(g, half, o):
                    act.wait_ge(s_y, 8 * g + 8)
                    for j in range(JG):
                        if half is not None:
                            if j == 0:
                                act.wait_ge(s_v[o], 16 * half + 16)
                            act.activation(vh[o][:, j, :], vb[:, o, j, :], ACT.Copy).then_inc(s_vh, 1)
                        act.wait_ge(s_w, JG * g + j + 1)
                        act.activation(wh[:, o, j, :], wf[:, j, :], ACT.Copy).then_inc(s_wh, 1)

                group(0, None, 0)
                group(1, 0, 1)
                with act.Fori(0, NG // 2 - 1) as i:
                    for o in range(2):
                        group(2 * i + 2 + o, i + 1, o)
                for t in range(TT):
                    act.wait_ge(s_var8, t + 1)
                    act.activation(rs8[:, t:t + 1], mv8[:, t, 1:2], ACT.Sqrt).then_inc(s_std8, 1)

            @block.gpsimd
            def _(pool):
                pool.sem_inc(s_wl, JG)

                def group(g, o, with_v=True):
                    for j in range(JG):
                        if with_v:
                            pool.wait_ge(s_vh, JG * g + j + 1)
                            pool.tensor_tensor(vl[o][:, j, :], vb[:, o, j, :], vh[o][:, j, :].bitcast(F32), ALU.subtract).then_inc(s_vl, 1)
                        pool.wait_ge(s_wh, JG * g + j + 1)
                        pool.tensor_tensor(wl[:, o, j, :], wf[:, j, :], wh[:, o, j, :].bitcast(F32), ALU.subtract).then_inc(s_wl, 1)

                group(0, 0, with_v=False)
                group(1, 1)
                with pool.Fori(0, NG // 2 - 1) as i:
                    for o in range(2):
                        group(2 * i + 2 + o, o)

            @block.vector
            def _(dve):
                link = chained(dve, s_v8)
                dve.wait_ge(s_sc7, 1)
                dve.sem_inc(s_ya, 8)

                def prepare(g, half, o, j):
                    if j == 0:
                        dve.wait_ge(s_g[o], 32 * half + 32)
                    dve.wait_ge(s_wl, JG * g + j + 1)
                    dve.tensor_tensor(wf[:, j, :].rearrange("p (t k) -> p t k", k=HT),
                                      hg[:, o, j, :].rearrange("p (t k) -> p t k", k=HT), gb[:, o, :, j * HT:(j + 1) * HT],
                                      ALU.mult).then_inc(s_w, 1)

                def add(g, m):
                    t, h = m // 2, slice((m % 2) * 512, (m % 2 + 1) * 512)
                    dve.wait_ge(s_y, 8 * g + m + 17)
                    dve.tensor_tensor(x1[:, t, h], x1[:, t, h], bank[m][:], ALU.add).then_inc(s_ya, 1)

                def group(g, ahead):
                    dve.wait_ge(s_ya, 8 * g + 8)
                    for j in range(JG):
                        prepare(g + 1, *ahead, j)
                        add(g, 2 * j)
                        add(g, 2 * j + 1)

                for j in range(JG):
                    prepare(0, 0, 0, j)
                with dve.Fori(0, NG // 2 - 1) as i:
                    group(2 * i, (i, 1))
                    group(2 * i + 1, (i + 1, 0))
                group(NG - 2, (NG // 2 - 1, 1))
                dve.wait_ge(s_ya, 8 * NG)
                dve.wait_ge(s_ln, 32)
                for t in range(TT):
                    add(NG - 1, 2 * t)
                    add(NG - 1, 2 * t + 1)
                    dve.wait_ge(s_ya, 8 * NG + 2 * t + 2)
                    for n in range(2):
                        last = dve.bn_stats(st8[:, t, n, :], x1[:, t, n * 512:(n + 1) * 512])
                    link(last)
                    link(dve.bn_aggr(mv8[:, t, :], st8[:, t].rearrange("p n s -> p (n s)")))
                    dve.tensor_scalar(mv8[:, t, 1:2], mv8[:, t, 1:2], LN_EPS, None, ALU.add).then_inc(s_var8, 1)
                    dve.wait_ge(s_std8, t + 1)
                    link(dve.reciprocal(rs8[:, t:t + 1], rs8[:, t:t + 1]))
                    link(dve.tensor_scalar(x1[:, t, :], x1[:, t, :], mv8[:, t, 0:1], rs8[:, t:t + 1], ALU.subtract, ALU.mult))
                    link(dve.tensor_tensor(x1[:, t, :], x1[:, t, :], ln2[:, 0, :], ALU.mult))
                    dve.tensor_tensor(x1[:, t, :], x1[:, t, :], ln2[:, 1, :], ALU.add).then_inc(s_fin, 1)



_INS = ['x', 'w_in', 'b_in', 'ssm_a_re', 'ssm_a_im', 'ssm_log_dt', 'ssm_b_re', 'ssm_b_im', 'ssm_c_re', 'ssm_c_im',
        'ssm_d', 'w_glu', 'w_up_ssm', 'nsa_pe_k', 'nsa_w1_k', 'nsa_w2_k', 'nsa_pe_v', 'nsa_w1_v', 'nsa_w2_v',
        'w_up_nsa', 'w_out', 'ln1_g', 'ln1_b', 'peer_w_q', 'peer_subkeys', 'peer_u', 'peer_v', 'ln2_g', 'ln2_b']


def kernel(**inputs):
    import numpy as _np
    import concourse.bacc as _bacc
    from concourse import mybir as _mybir
    from concourse.bass_utils import run_bass_kernel_spmd as _run

    nc = _bacc.Bacc("TRN2", target_bir_lowering=False, num_devices=1)
    arrays, args = {}, {}
    for name in _INS:
        v = _np.ascontiguousarray(inputs[name])
        arrays[f"in_{name}_dram"] = v
        args[name] = nc.dram_tensor(f"in_{name}_dram", v.shape, _mybir.dt.from_np(v.dtype), kind="ExternalInput").ap()
    out = nc.dram_tensor("out_0_dram", (1, S, D), F32, kind="ExternalOutput").ap()
    build(nc, args, out)
    r = _run(nc, [arrays], core_ids=[0])
    return r.results[0]["out_0_dram"]
```
